# Optimizing a Trainium2 kernel written in Bass

```python
import jax, jax.numpy as jnp
from jax import lax
import numpy as np

D_MODEL = 1024
BATCH = 1
SEQ = 512
DEPTH = 2

GRID_W = 64
CTX_LEN = 256
HEAD_DIM = 64
N_Q_HEADS = 8
N_KV_HEADS = 2
Q_GROUP = N_Q_HEADS // N_KV_HEADS
ATTN_WIDTH = N_Q_HEADS * HEAD_DIM
KV_WIDTH = N_KV_HEADS * HEAD_DIM
AXIS_DIM = HEAD_DIM // 2
ROPE_THETA = 10000.0
Q_BLOCK = 128
ATTN_SCALE = HEAD_DIM ** -0.5
CONF_WIDTH = D_MODEL // 2
CONF_KERNEL = 31
SC_WIDTH = D_MODEL // 2
SC_KERNEL = 3
N_BRANCHES = 3
N_MOD = 6
FFN_HIDDEN = -(-8 * D_MODEL // (3 * 256)) * 256
EPS = 1e-6

OFF_K = ATTN_WIDTH
OFF_V = OFF_K + KV_WIDTH
OFF_CONF = OFF_V + KV_WIDTH
OFF_SC = OFF_CONF + 2 * CONF_WIDTH
OFF_GATE = OFF_SC + 3 * SC_WIDTH
IN_WIDTH = OFF_GATE + N_BRANCHES * D_MODEL

kernel_name = 'hybrid_gqa_conformer_shortconv_dit_block'

def rms_norm(x):
    xf = x.astype(jnp.float32)
    return (xf * lax.rsqrt(jnp.mean(xf * xf, axis=-1, keepdims=True) + EPS)).astype(x.dtype)

def head_rms_norm(x, g):
    return rms_norm(x) * g

def layer_norm(x, g, b):
    xf = x.astype(jnp.float32)
    mu = jnp.mean(xf, axis=-1, keepdims=True)
    var = jnp.mean(jnp.square(xf - mu), axis=-1, keepdims=True)
    return ((xf - mu) * lax.rsqrt(var + EPS)).astype(x.dtype) * g + b

def rope_tables(seq_len):
    rows = seq_len // GRID_W
    r_ids, c_ids = jnp.meshgrid(jnp.arange(rows), jnp.arange(GRID_W), indexing='ij')
    r_ids = r_ids.reshape(-1).astype(jnp.float32)
    c_ids = c_ids.reshape(-1).astype(jnp.float32)
    freqs = ROPE_THETA ** (-jnp.arange(0, AXIS_DIM, 2, dtype=jnp.float32) / AXIS_DIM)
    ang_r = r_ids[:, None] * freqs
    ang_c = c_ids[:, None] * freqs
    return (jnp.cos(ang_r)[:, None, :], jnp.sin(ang_r)[:, None, :],
            jnp.cos(ang_c)[:, None, :], jnp.sin(ang_c)[:, None, :])

def _rotate_half(xp, cos, sin):
    x1, x2 = jnp.split(xp, 2, axis=-1)
    return jnp.concatenate([x1 * cos - x2 * sin, x1 * sin + x2 * cos], axis=-1)

def apply_rope_2d(x, tabs):
    cos_r, sin_r, cos_c, sin_c = tabs
    xf = x.astype(jnp.float32)
    out = jnp.concatenate([_rotate_half(xf[..., :AXIS_DIM], cos_r, sin_r),
                           _rotate_half(xf[..., AXIS_DIM:], cos_c, sin_c)], axis=-1)
    return out.astype(x.dtype)

def depthwise_conv(x, w):
    k = w.shape[0]
    return lax.conv_general_dilated(x, w[:, None, :].astype(x.dtype), window_strides=(1,),
                                    padding=[(k // 2, k // 2)],
                                    dimension_numbers=('NWC', 'WIO', 'NWC'),
                                    feature_group_count=x.shape[-1])

def latent_attention(q, k_all, v_all):
    b, s = q.shape[0], q.shape[1]
    n_blk = s // Q_BLOCK
    qb = q.reshape(b, n_blk, Q_BLOCK, N_KV_HEADS, Q_GROUP, HEAD_DIM).transpose(1, 0, 2, 3, 4, 5)

    def one_block(qi):
        sc = jnp.einsum('bqhgd,bkhd->bhgqk', qi, k_all).astype(jnp.float32) * ATTN_SCALE
        p = jax.nn.softmax(sc, axis=-1).astype(v_all.dtype)
        return jnp.einsum('bhgqk,bkhd->bqhgd', p, v_all)

    o = lax.map(one_block, qb)
    return o.transpose(1, 0, 2, 3, 4, 5).reshape(b, s, ATTN_WIDTH)

def context_attention(qc, kc, vc):
    b, l = qc.shape[0], qc.shape[1]
    qg = qc.reshape(b, l, N_KV_HEADS, Q_GROUP, HEAD_DIM)
    sc = jnp.einsum('bqhgd,bkhd->bhgqk', qg, kc).astype(jnp.float32) * ATTN_SCALE
    p = jax.nn.softmax(sc, axis=-1).astype(vc.dtype)
    return jnp.einsum('bhgqk,bkhd->bqhgd', p, vc).reshape(b, l, ATTN_WIDTH)

def conformer_branch(u, dw_w, dw_b, ln_g, ln_b, w_out):
    a, g = jnp.split(u, 2, axis=-1)
    h = a * jax.nn.sigmoid(g)
    h = depthwise_conv(h, dw_w) + dw_b
    h = jax.nn.silu(layer_norm(h, ln_g, ln_b))
    return h @ w_out

def shortconv_branch(u, dw_w, w_out):
    bg, cg, xs = jnp.split(u, 3, axis=-1)
    return (bg * depthwise_conv(cg * xs, dw_w)) @ w_out

def merge_branches(attn_heads, conf_u, sc_u, gate_logits, w_attn_o, conf_dw_w, conf_dw_b,
                   conf_ln_g, conf_ln_b, w_conf_out, sc_dw_w, w_sc_out, w_mix_out):
    y_attn = attn_heads @ w_attn_o
    y_conf = conformer_branch(conf_u, conf_dw_w, conf_dw_b, conf_ln_g, conf_ln_b, w_conf_out)
    y_sc = shortconv_branch(sc_u, sc_dw_w, w_sc_out)
    g = jax.nn.sigmoid(gate_logits.reshape(gate_logits.shape[:-1] + (N_BRANCHES, D_MODEL)))
    merged = g[..., 0, :] * y_attn + g[..., 1, :] * y_conf + g[..., 2, :] * y_sc
    return merged @ w_mix_out

def swiglu(h, w_in, w_out):
    a, b = jnp.split(h @ w_in, 2, axis=-1)
    return (jax.nn.silu(a) * b) @ w_out

def setup_inputs(seed: int = 0) -> dict:
    key = jax.random.key(seed)
    ks = jax.random.split(key, 24)
    f32 = jnp.float32
    L, D = DEPTH, D_MODEL

    def nrm(k, shape, scale):
        return jax.random.normal(k, shape, f32) * scale

    return {
        'x': nrm(ks[0], (BATCH, SEQ, D), 1.0),
        'c': nrm(ks[1], (BATCH, D), 1.0),
        'ctx': nrm(ks[2], (BATCH, CTX_LEN, D), 1.0),
        'c_ctx': nrm(ks[3], (D,), 1.0),
        'w_ada': nrm(ks[4], (L, D, N_MOD * D), 0.5 * D ** -0.5),
        'b_ada': nrm(ks[5], (L, N_MOD * D), 0.02),
        'w_in': nrm(ks[6], (L, D, IN_WIDTH), D ** -0.5),
        'q_norm': 1.0 + nrm(ks[7], (L, HEAD_DIM), 0.02),
        'k_norm': 1.0 + nrm(ks[8], (L, HEAD_DIM), 0.02),
        'w_attn_o': nrm(ks[9], (L, ATTN_WIDTH, D), ATTN_WIDTH ** -0.5),
        'conf_dw_w': nrm(ks[10], (L, CONF_KERNEL, CONF_WIDTH), CONF_KERNEL ** -0.5),
        'conf_dw_b': nrm(ks[11], (L, CONF_WIDTH), 0.02),
        'conf_ln_g': 1.0 + nrm(ks[12], (L, CONF_WIDTH), 0.02),
        'conf_ln_b': nrm(ks[13], (L, CONF_WIDTH), 0.02),
        'w_conf_out': nrm(ks[14], (L, CONF_WIDTH, D), CONF_WIDTH ** -0.5),
        'sc_dw_w': nrm(ks[15], (L, SC_KERNEL, SC_WIDTH), SC_KERNEL ** -0.5),
        'w_sc_out': nrm(ks[16], (L, SC_WIDTH, D), SC_WIDTH ** -0.5),
        'w_mix_out': nrm(ks[17], (L, D, D), D ** -0.5),
        'w_ffn_in': nrm(ks[18], (L, D, 2 * FFN_HIDDEN), D ** -0.5),
        'w_ffn_out': nrm(ks[19], (L, FFN_HIDDEN, D), FFN_HIDDEN ** -0.5),
    }

def reference(x, c, ctx, c_ctx, w_ada, b_ada, w_in, q_norm, k_norm, w_attn_o, conf_dw_w, conf_dw_b,
              conf_ln_g, conf_ln_b, w_conf_out, sc_dw_w, w_sc_out, w_mix_out, w_ffn_in, w_ffn_out):
    b, s = x.shape[0], x.shape[1]
    lc = ctx.shape[1]
    rope = rope_tables(s)
    for i in range(DEPTH):
        last = i == DEPTH - 1
        wi = w_in[i]
        branch_w = (w_attn_o[i], conf_dw_w[i], conf_dw_b[i], conf_ln_g[i], conf_ln_b[i],
                    w_conf_out[i], sc_dw_w[i], w_sc_out[i], w_mix_out[i])
        mod = (jax.nn.silu(c) @ w_ada[i] + b_ada[i]).reshape(b, N_MOD, 1, D_MODEL)
        modc = (jax.nn.silu(c_ctx) @ w_ada[i] + b_ada[i]).reshape(N_MOD, D_MODEL)

        hc = rms_norm(ctx) * (1 + modc[1]) + modc[0]
        kvc = hc @ wi[:, OFF_K:OFF_CONF]
        kc = head_rms_norm(kvc[..., :KV_WIDTH].reshape(b, lc, N_KV_HEADS, HEAD_DIM), k_norm[i])
        vc = kvc[..., KV_WIDTH:].reshape(b, lc, N_KV_HEADS, HEAD_DIM)

        h = rms_norm(x) * (1 + mod[:, 1]) + mod[:, 0]
        p = h @ wi
        q = apply_rope_2d(head_rms_norm(p[..., :OFF_K].reshape(b, s, N_Q_HEADS, HEAD_DIM), q_norm[i]), rope)
        k = apply_rope_2d(head_rms_norm(p[..., OFF_K:OFF_V].reshape(b, s, N_KV_HEADS, HEAD_DIM), k_norm[i]), rope)
        v = p[..., OFF_V:OFF_CONF].reshape(b, s, N_KV_HEADS, HEAD_DIM)
        attn = latent_attention(q, jnp.concatenate([kc, k], axis=1), jnp.concatenate([vc, v], axis=1))
        mixed = merge_branches(attn, p[..., OFF_CONF:OFF_SC], p[..., OFF_SC:OFF_GATE], p[..., OFF_GATE:], *branch_w)
        x_new = x + mod[:, 2] * mixed
        h2 = rms_norm(x_new) * (1 + mod[:, 4]) + mod[:, 3]
        x_new = x_new + mod[:, 5] * swiglu(h2, w_ffn_in[i], w_ffn_out[i])

        if not last:
            qc = head_rms_norm((hc @ wi[:, :OFF_K]).reshape(b, lc, N_Q_HEADS, HEAD_DIM), q_norm[i])
            pc = hc @ wi[:, OFF_CONF:]
            attn_c = context_attention(qc, kc, vc)
            mixed_c = merge_branches(attn_c, pc[..., :OFF_SC - OFF_CONF], pc[..., OFF_SC - OFF_CONF:OFF_GATE - OFF_CONF],
                                     pc[..., OFF_GATE - OFF_CONF:], *branch_w)
            ctx = ctx + modc[2] * mixed_c
            h2c = rms_norm(ctx) * (1 + modc[4]) + modc[3]
            ctx = ctx + modc[5] * swiglu(h2c, w_ffn_in[i], w_ffn_out[i])
        x = x_new
    return x


_drawn_inputs = setup_inputs


def setup_inputs(seed=0):
    import zlib

    import numpy as np

    out = dict(_drawn_inputs(seed))
    spreads = {}
    factors = {'ctx': 6.946,
     'q_norm': 8.0,
     'k_norm': 8.0,
     'conf_dw_b': 8.0,
     'conf_ln_g': 8.0,
     'conf_ln_b': 8.0}
    for name, (base, spread) in spreads.items():
        noise = np.random.default_rng([zlib.crc32(name.encode()), seed]).standard_normal(out[name].shape)
        drawn = base * np.exp(spread * noise) if base else spread * noise
        out[name] = __import__('jax').numpy.asarray(drawn.astype(out[name].dtype))
    for name, factor in factors.items():
        out[name] = (out[name] * factor).astype(out[name].dtype)
    return out
```

```python
import numpy as np
import concourse.bass as bass
from concourse import mybir

F32, F32R = mybir.dt.float32, mybir.dt.float32r
ALU, ACT, AX = mybir.AluOpType, mybir.ActivationFunctionType, mybir.AxisListType

DEPTH, D, S, LC = 2, 1024, 512, 256
T = S + LC
KD = D // 128
HD, NH, NKV = 64, 8, 2
ATT, KVW = NH * HD, NKV * HD
CW = D // 2
KC = CW // 128
TAPS, SC_TAPS = 31, 3
PAD = TAPS // 2
FFN = 2816
OFF_K, OFF_V, OFF_CONF = ATT, ATT + KVW, ATT + 2 * KVW
OFF_SC = OFF_CONF + 2 * CW
OFF_GATE = OFF_SC + 3 * CW
IN_WIDTH = OFF_GATE + 3 * D
N_MOD = 6
EPS = 1e-6
ROPE_THETA, GRID_W = 10000.0, 64
MT = N_MOD * KD
PARTS = [6, 6, 6, 4]
SEGS = [[(0, S, 0), (S, LC, 1)], [(0, S, 0)]]
WIDTH = [T, S]
GAP = 2 * PAD
CONV_W = [T + GAP, S]
PAR_ROWS = MT + 3 * KC + SC_TAPS * KC + 2 + 2 * KD
R_CB, R_LG, R_LB = MT, MT + KC, MT + 2 * KC
R_SC = MT + 3 * KC
R_QN = R_SC + SC_TAPS * KC
R_KN, R_C = R_QN + 1, R_QN + 2
CONV_ROWS = TAPS * KC
LOOPS = True


def ctok(c):
    return c if c < S else c + GAP


class Plan:

    def __init__(self):
        self.unit, self.tile, self.last = {}, {}, []
        u = t = 0
        self.tile["load"] = 0
        t += KD
        for l in range(DEPTH):
            phases = [("qkv", [1] * 6), ("conf", [1] * 8), ("att", None)]
            phases += [(("branch", 0), [1, 1, 2] * 4), ("sc", [1] * 12)]
            phases += [(("branch", 2), [1, 1, 2] * 4), (("branch", 1), [1, 1, 2] * 4)]
            phases += [("mix", [1] * KD)]
            for p, n in enumerate(PARTS):
                phases += [(("up", p), [1] * 2 * n), (("down", p), [1] * KD)]
            for name, tiles in phases:
                self.unit[l, name], self.tile[l, name] = u, t
                if name == "att":
                    t += len(steps(l))
                    continue
                for n in tiles:
                    t += n
                    u += 1
                    self.last.append(t)
            assert u % 2 == 0 and t % 2 == 0
        self.tile["store"] = t
        self.units = u


def steps(l):
    out = []
    for h in range(NH):
        out += [(h, 128 * j, 0, T) for j in range(S // 128)]
    if l == 0:
        for h in range(NH):
            out += [(h, S + 128 * j, S, LC) for j in range(LC // 128)]
    return out


def loop(eng, n, body):
    if LOOPS and n > 2:
        with eng.Fori(0, n) as i:
            body(i)
    else:
        for i in range(n):
            body(i)


def build(nc, A, out):
    plan = Plan()

    base = 17 * 1024
    at = {}

    def region(name, size):
        at[name] = base + sum(sizes.values())
        sizes[name] = size
    sizes = {}
    region("X", KD * T * 4)
    region("H", KD * T * 8)
    region("AS", KC * T * 8)
    region("CF", KC * T * 8)
    region("DD", KD * T * 4)
    region("EE", 19200)
    region("RAW", 2 * 4096)
    region("WHL", 2 * 8192)
    region("GS", 2 * T * 4)
    region("CONST", 9000)

    def sb(name, shape, dt, where, off=0):
        return nc.alloc_sbuf_tensor_at(name, shape, dt, offset=at[where] + off)

    X = sb("x_T", [128, KD, T], F32, "X")
    H = sb("h_parts", [128, 2, KD, T], F32R, "H")
    ada = sb("ada_weights", [128, 6, KD, 256], F32, "H")
    Q = sb("q_parts", [128, 2, KC, T], F32R, "AS")
    SCO = sb("shortconv_parts", [128, 2, KC, T], F32R, "AS")
    hpad = sb("conf_padded", [128, KC, T + 2 * GAP], F32, "CF")
    CF = sb("conf_parts", [128, 2, KC, T], F32R, "CF")
    ln_sum = sb("ln_sum", [128, T + GAP], F32, "CF")
    ln_sq = sb("ln_square", [128, 2, T + GAP], F32, "CF", 3200)
    sig = sb("ln_sigmoid", [128, 2, T + GAP], F32, "CF", 9600)
    merged = sb("merged", [128, KD, T], F32, "DD")
    xin = sb("x_rows", [128, T // 128, D], F32, "DD")
    qraw = sb("q_raw", [128, 4, T], F32, "DD")
    qsq = sb("q_square", [128, T], F32, "DD", 16 * T)
    qspread = sb("q_inverse_spread", [128, T // 128, 2, HD], F32, "DD", 20 * T)
    qrot = sb("q_rotated", [128, S], F32, "DD", 24 * T)
    rope = sb("rope_tables", [128, 2, S], F32, "DD", 24 * T + 4 * S)
    PT = sb("probs_T_parts", [128, 2, 2, T // 128, 256], F32R, "DD")
    U = sb("hidden_parts", [128, 2 * PARTS[0], 2, T], F32R, "AS")
    K = sb("k_parts", [128, 2, T], F32R, "EE")
    V = sb("v_parts", [128, 2, T // 128, 128], F32R, "EE", 8 * T)
    P = sb("probs", [128, 2, T], F32, "EE", 16 * T)
    acc = sb("conv_sum", [128, KC, T + GAP], F32, "EE")
    E2 = 16 * (T + GAP)
    bx = sb("sc_padded", [128, T + 4], F32, "EE", E2)
    sc_sum = sb("sc_sum", [128, T + 2], F32, "EE", E2 + 3104)
    ybuf = sb("gated", [128, 2, T], F32, "EE", E2)
    SQ = sb("x_square", [128, 2, T], F32, "EE")
    SSQ = sb("sum_square", [128, T], F32, "EE", 8 * T)
    HT = sb("h_scaled", [128, 2, T], F32, "EE", 12 * T)
    stage = sb("parameter_rows", [128, 4, 128], F32, "EE")
    xout = sb("out_rows", [128, S // 128, D], F32, "EE")
    raw = sb("w_raw", [128, 2, 1024], F32, "RAW")
    WHL = sb("w_parts", [128, 2, 2, 1024], F32R, "WHL")
    GS = sb("gates", [128, 2, T], F32, "GS")
    used = [0]

    def const(name, shape):
        t_ = sb(name, shape, F32, "CONST", used[0])
        used[0] += -(-4 * int(np.prod(shape[1:])) // 32) * 32
        return t_

    ident = const("identity", [128, 128])
    swap = const("rope_swap", [128, 128])
    ones = const("ones", [128, 1])
    heads = const("head_columns", [128, 2])
    eps = const("eps", [128, 1])
    par = const("parameters", [128, DEPTH, PAR_ROWS])
    cw = const("conv_taps", [128, DEPTH, CONV_ROWS])
    qg = const("head_gains", [128, DEPTH, 2])
    csil = const("silu_c", [128, KD, 2])
    sgc = const("sigmoid_c", [128, 2, KD])
    mod = const("modulation", [128, MT, 2])
    sd = const("deviation", [128, 2, 12])
    rs = const("inverse_deviation", [128, 2, 12])
    nmax = const("minus_max", [128, 4])
    psum_ = const("prob_sum", [128, 4])
    pinv = const("prob_scale", [128, 4])
    assert used[0] <= sizes["CONST"] and at["CONST"] + used[0] <= nc.sbuf_usable_end

    G = nc.alloc_psum_tensor("tiles", [128, 2, 1024], F32)
    M = nc.alloc_psum_tensor("small_wide", [128, 1024], F32)
    O = nc.alloc_psum_tensor("small_pair", [128, 2, 512], F32)

    sem = nc.alloc_semaphore
    s_const, s_in, s_par, s_rope = sem("constants_in"), sem("rows_in"), sem("parameter_rows_in"), sem("rope_in")
    s_ada = [sem(f"ada_in_{i}") for i in range(6)]
    s_w = [sem(f"raw_in_{i}") for i in range(2)]
    s_out = sem("out_stored")
    s_set = sem("constants_set")
    s_part, s_parc, s_qg = sem("parameters_transposed"), sem("parameters_copied"), sem("gains_scaled")
    s_sgc, s_csil = sem("sigmoid_c_done"), sem("silu_c_done")
    s_adt, s_mod = sem("ada_tile_done"), sem("modulation_steps")
    s_hi, s_lo = sem("w_high_done"), sem("w_rest_done")
    s_tile = sem("tile_done")
    s_free = [sem(f"tile_read_out_{i}") for i in range(2)]
    s_sq, s_ssq = sem("square_done"), sem("square_summed")
    s_stat, s_sd, s_rc, s_inv, s_spread = (sem("statistic_done"), sem("deviation_done"), sem("reciprocal_done"),
                                           sem("inverse_done"), sem("spread_done"))
    s_ht, s_hh, s_h = sem("h_scaled_done"), sem("h_high_done"), sem("h_parts_done")
    s_qsq, s_qn, s_rot, s_qr = sem("q_square_done"), sem("q_scaled"), sem("q_rotation_done"), sem("q_rope_steps")
    s_qh, s_q, s_vh = sem("q_high_done"), sem("q_parts_done"), sem("v_high_done")
    s_nm, s_pi, s_pn = sem("minus_max_done"), sem("prob_scale_done"), sem("probs_scaled")
    s_pt, s_ph, s_pl = sem("probs_transposed"), sem("probs_T_high_done"), sem("probs_T_parts_done")
    s_o, s_oh, s_ol = sem("heads_done"), sem("heads_high_done"), sem("heads_parts_done")
    s_pad, s_sg = sem("padding_set"), sem("gate_done")
    s_tap, s_ls, s_lsq, s_lsm = sem("conv_step"), sem("ln_sum_step"), sem("ln_square_done"), sem("ln_scale_step")
    s_lsg, s_lv, s_lh, s_ll = sem("ln_sigmoid_done"), sem("ln_silu_done"), sem("conf_high_done"), sem("conf_parts_done")
    s_cg, s_bx, s_sct, s_sch, s_scl = (sem("cg_copied"), sem("sc_padded_done"), sem("sc_conv_step"), sem("sc_high_done"),
                                       sem("sc_parts_done"))
    s_mg, s_mh = sem("merged_added"), sem("merged_high_done")
    s_uh, s_u = sem("hidden_high_done"), sem("hidden_parts_done")

    def f(ap):
        return ap.bitcast(F32)

    def read_out(eng, t, slot):
        eng.wait_ge(s_free[slot], t - slot + 2)

    def phase_read_out(eng, t):
        for r in range(2):
            eng.wait_ge(s_free[r], t)

    def lagging(p, lag):
        n = 0 if p - lag == 0 else p - lag - 1
        return n if p - lag == 0 or 1 <= n <= 4 else None

    step_base = [sum(len(steps(x)) for x in range(l)) for l in range(DEPTH)]
    up_base = {}
    n = 0
    for l in range(DEPTH):
        for p, w in enumerate(PARTS):
            up_base[l, p] = n
            n += w

    with nc.Block() as block:
        @block.sync
        def _(sp):
            dma = sp.dma_start
            dma(ident[:, :], A["ident"]).then_inc(s_const, 16)
            dma(swap[:, :], A["swap"]).then_inc(s_const, 16)
            dma(heads[:, :], A["heads"]).then_inc(s_const, 16)
            for l in range(DEPTH):
                pr = stage[:, 2 * l, :]

                def rows(r, ap):
                    dma(pr[r:r + ap.shape[0], 0:ap.shape[1]], ap).then_inc(s_par, 16)
                rows(0, A["b_ada"][l].rearrange("(r p) -> r p", p=128))
                rows(R_CB, A["conf_dw_b"][l].rearrange("(r p) -> r p", p=128))
                rows(R_LG, A["conf_ln_g"][l].rearrange("(r p) -> r p", p=128))
                rows(R_LB, A["conf_ln_b"][l].rearrange("(r p) -> r p", p=128))
                rows(R_SC, A["sc_dw_w"][l].rearrange("j (r p) -> (j r) p", p=128))
                for half in range(2):
                    for r, name in ((R_QN, "q_norm"), (R_KN, "k_norm")):
                        dma(pr[r:r + 1, 64 * half:64 * half + 64], A[name][l:l + 1, :]).then_inc(s_par, 16)
                rows(R_C, A["c"][0].rearrange("(r p) -> r p", p=128))
                rows(R_C + KD, A["c_ctx"].rearrange("(r p) -> r p", p=128))
                dma(stage[0:CONV_ROWS, 2 * l + 1, :],
                    A["conf_dw_w"][l].rearrange("j (r p) -> (j r) p", p=128)).then_inc(s_par, 16)
            dma(xin[:, 0:4, :], A["x"][0].rearrange("(t p) n -> p t n", p=128)).then_inc(s_in, 16)
            dma(xin[:, 4:6, :], A["ctx"][0].rearrange("(t p) n -> p t n", p=128)).then_inc(s_in, 16)

            def unit(u, slot, halves, turn=None):
                ahead = u - 1 if not (isinstance(u, int) and u < 2) else None
                if ahead is not None:
                    sp.wait_ge(s_lo, ahead)
                for dst, src in halves:
                    dma(dst, src).then_inc(s_w[slot], 16)

            def cols(slot, view, c0):
                nk = view.shape[1]
                r = raw[:, slot, 0:nk * 128].rearrange("p (k n) -> p k n", n=128)
                return [(r[q:q + 64], view[q:q + 64, :, bass.ds(c0, 128)]) for q in (0, 64)]

            for l in range(DEPTH):
                aw = A["w_ada"][l].rearrange("(k p) n -> p k n", p=128)
                if l:
                    sp.wait_ge(s_tile, plan.tile[l, "qkv"])
                for j in range(MT // 2):
                    if j >= 6:
                        sp.wait_ge(s_adt, MT * l + 2 * (j - 5))
                    dma(ada[:, j % 6], aw[:, :, 256 * j:256 * j + 256]).then_inc(s_ada[j % 6], 16)
                wi = A["w_in"][l].rearrange("(k p) n -> p k n", p=128)
                u = plan.unit[l, "qkv"]
                unit(u, 0, cols(0, wi, OFF_K))
                unit(u + 1, 1, cols(1, wi, OFF_V))
                if l == 0:
                    sp.wait_ge(s_tile, KD)
                for half in range(2):
                    dma(rope[:, half, :], A["rope"][half]).then_inc(s_rope, 16)
                for i in range(4):
                    r = raw[:, i % 2, :].rearrange("p (k n) -> p k n", n=128)
                    unit(u + 2 + i, i % 2, [(r[:, :, 64 * g:64 * g + 64], wi[:, :, 64 * (4 * g + i):64 * (4 * g + i) + 64])
                                            for g in range(2)])

                u = plan.unit[l, "conf"]

                def conf(i):
                    unit(u + 2 * i, 0, cols(0, wi, 128 * i + OFF_CONF + CW))
                    unit(u + 2 * i + 1, 1, cols(1, wi, 128 * i + OFF_CONF))
                loop(sp, KC, conf)

                for b in (0, "sc", 2, 1):
                    if b == "sc":
                        u_sc = plan.unit[l, "sc"]

                        def sc(i):
                            for r in range(2):
                                for n, c in enumerate((1, 2, 0)):
                                    q = 3 * r + n
                                    unit(u_sc + 6 * i + q, q % 2, cols(q % 2, wi, 256 * i + 128 * r + OFF_SC + c * CW))
                        loop(sp, KC // 2, sc)
                        continue
                    u_b = plan.unit[l, ("branch", b)]
                    wo = A[("w_attn_o", "w_conf_out", "w_sc_out")[b]][l]

                    def branch(i, b=b, u_b=u_b, wo=wo):
                        for r in range(2):
                            q = 3 * r
                            for n in range(2):
                                unit(u_b + 6 * i + q + n, (q + n) % 2,
                                     cols((q + n) % 2, wi, 512 * i + 256 * r + 128 * n + OFF_GATE + b * D))
                            slot = (q + 2) % 2
                            rw = raw[:, slot, :].rearrange("p (k n) -> p k n", n=256)
                            v = (wo.rearrange("(g k p) n -> g p k n", g=2, p=64) if b == 0
                                 else wo.rearrange("(k g p) n -> g p k n", g=2, p=64))
                            unit(u_b + 6 * i + q + 2, slot,
                                 [(rw[64 * g:64 * g + 64], v[g, :, :, bass.ds(512 * i + 256 * r, 256)]) for g in range(2)])
                    loop(sp, 2, branch)

                wm = A["w_mix_out"][l].rearrange("(k p) n -> p k n", p=128)
                u_m = plan.unit[l, "mix"]

                def mix(i):
                    for r in range(2):
                        unit(u_m + 2 * i + r, r, cols(r, wm, 256 * i + 128 * r))
                loop(sp, KD // 2, mix)
                wf = A["w_ffn_in"][l].rearrange("(k p) n -> p k n", p=128)
                f0 = 0
                for p, n in enumerate(PARTS):
                    u_u, u_d = plan.unit[l, ("up", p)], plan.unit[l, ("down", p)]

                    def up(i, u_u=u_u, f0=f0):
                        for r in range(2):
                            unit(u_u + 2 * i + r, r, cols(r, wf, 128 * i + 128 * f0 + r * FFN))
                    loop(sp, n, up)
                    wd = A["w_ffn_out"][l][128 * f0:128 * (f0 + n), :].rearrange("(k p) n -> p k n", p=128)

                    def down(i, u_d=u_d, wd=wd):
                        for r in range(2):
                            unit(u_d + 2 * i + r, r, cols(r, wd, 256 * i + 128 * r))
                    loop(sp, KD // 2, down)
                    f0 += n
            for r in range(2):
                sp.wait_ge(s_free[r], plan.tile["store"] + KD)
            dma(out[0].rearrange("(t p) n -> p t n", p=128), xout[:, :, :]).then_inc(s_out, 16)
            sp.wait_ge(s_out, 16)

        @block.tensor
        def _(pe):
            def mm(o_, a, b, start=True, stop=True):
                return nc.tensor.matmul(o_, a, b, start=start, stop=stop)

            def done(ins):
                ins.then_inc(s_tile, 1)

            def take_slot(t, slot):
                if not (isinstance(t, int) and t < 2):
                    pe.wait_ge(s_free[slot], t - slot)

            def three(dst, a, b, first, last):
                mm(dst, a(0), b(0), first, False)
                mm(dst, a(0), b(1), False, False)
                return mm(dst, a(1), b(0), False, last)

            def product(slot, wslot, ks, rhs, width, before_k=None, cut=0, wn=128):
                segs = [(0, 512)] + ([(512, width)] if width > 512 else [])
                for k in range(ks):
                    if before_k:
                        before_k(k)
                    for pw, px in ((0, 0), (0, 1), (1, 0)):
                        w = WHL[:, wslot, pw, k * wn + cut:k * wn + cut + 128]
                        for a, b in segs:
                            ins = mm(G[:, slot, a:b], w, rhs(px, k, a, b),
                                     k == 0 and (pw, px) == (0, 0), k == ks - 1 and pw == 1)
                return ins

            def from_h(part, k, a, b):
                return H[:, part, k, a:b]

            pe.wait_ge(s_const, 48)
            pe.wait_ge(s_par, 16 * 12 * DEPTH)
            for l in range(DEPTH):
                nc.tensor.transpose(O[:, l, 0:PAR_ROWS], stage[0:PAR_ROWS, 2 * l, :],
                                    ident[0:PAR_ROWS, 0:PAR_ROWS])
                nc.tensor.transpose(O[:, l, 128:128 + CONV_ROWS],
                                    stage[0:CONV_ROWS, 2 * l + 1, :], ident[0:CONV_ROWS, 0:CONV_ROWS])\
                    .then_inc(s_part, 1)
            pe.wait_ge(s_in, 32)
            for i in range(KD):
                take_slot(i, i % 2)
                for t in range(T // 128):
                    ins = nc.tensor.transpose(G[:, i % 2, 128 * t:128 * t + 128],
                                              xin[:, t, 128 * i:128 * i + 128], ident[:, :])
                done(ins)

            stats, spreads, squared, normed = [0], [0], [0], [0]

            def statistic(src, width, rhs, n=1, off=lambda c: c):
                k = stats[0]
                if k:
                    pe.wait_ge(s_sd, k)
                for t in range(width // 128):
                    c = off(128 * t)
                    b = 16 * (k % 2) + n * t
                    ins = mm(O[:, 0, b:b + n], src[:, c:c + 128], rhs)
                ins.then_inc(s_stat, 1)
                stats[0] += 1

            def spread(width, n=1):
                k = spreads[0]
                pe.wait_ge(s_inv, k + 1)
                for t in range(width // 128):
                    if n == 1:
                        ins = mm(M[:, 128 * t:128 * t + 128], rs[:, k % 2, t:t + 1].to_broadcast([128, 128]), ident[:, :])
                    else:
                        ins = nc.tensor.transpose(M[:, 128 * t:128 * t + 128],
                                                  qspread[:, t].rearrange("p h d -> p (h d)"), ident[:, :])
                ins.then_inc(s_spread, 1)
                spreads[0] += 1

            def norm(width):
                squared[0] += KD - 1
                pe.wait_ge(s_ssq, squared[0])
                statistic(SSQ, width, ones[:, :])
                spread(width)

            def h_ready(k):
                pe.wait_ge(s_h, normed[0] + k + 1)

            pe.wait_ge(s_set, 2)
            for l in range(DEPTH):
                W = WIDTH[l]
                if l == 0:
                    pe.wait_ge(s_csil, 1)
                for m in range(MT):
                    j = m // 2
                    if m % 2 == 0:
                        pe.wait_ge(s_ada[j % 6], 16 * (4 * l + j // 6 + 1))
                    for k in range(KD):
                        ins = mm(O[:, 1, 2 * m:2 * m + 2], ada[:, j % 6, k, 128 * (m % 2):128 * (m % 2) + 128],
                                 csil[:, k, :], k == 0, k == KD - 1)
                    ins.then_inc(s_adt, 1)
                norm(T)

                def qk_steps(p):
                    n = lagging(p, 1)
                    if n is not None:
                        pe.wait_ge(s_qsq, 5 * l + n + 1)
                        statistic(qsq, T if n == 0 else W, heads[:, :], n=2)
                    n = lagging(p, 2)
                    if n is not None:
                        if n == 0:
                            pe.wait_ge(s_h, normed[0])
                        else:
                            pe.wait_ge(s_qn, 5 * l + n)
                        spread(T if n == 0 else W, n=2)
                    n = lagging(p, 3)
                    if n is not None:
                        pe.wait_ge(s_qn, 5 * l + n + 1)
                        if n:
                            pe.wait_ge(s_qr, 3 * (5 * l + n))
                        mm(O[:, 1, 0:S], swap[:, :], qraw[:, n % 4, 0:S]).then_inc(s_rot, 1)

                u, t = plan.unit[l, "qkv"], plan.tile[l, "qkv"]
                for i in range(6):
                    pe.wait_ge(s_lo, u + i + 1)
                    take_slot(t + i, i % 2)
                    if i == 1:
                        for tt in range(T // 128):
                            c = slice(128 * tt, 128 * tt + 128)
                            for k in range(KD):
                                ins = three(G[:, 1, c], lambda part: H[:, part, k, c],
                                            lambda part: WHL[:, 1, part, 128 * k:128 * k + 128], k == 0, k == KD - 1)
                    else:
                        ins = product(i % 2, i % 2, KD, from_h, T if i == 0 else W, h_ready if i == 0 else None)
                    done(ins)
                    if i == 0:
                        normed[0] += KD
                    qk_steps(i)

                u, t = plan.unit[l, "conf"], plan.tile[l, "conf"]
                for i in range(2 * KC):
                    pe.wait_ge(s_lo, u + i + 1)
                    take_slot(t + i, i % 2)
                    done(product(i % 2, i % 2, KD, from_h, W))
                    qk_steps(6 + i)

                t, st_ = plan.tile[l, "att"], steps(l)
                s0 = step_base[l]

                def scores(i):
                    h, q0, k0, nk = st_[i]
                    r = slice(64 * (h // 4), 64 * (h // 4) + 64)
                    take_slot(t + i, i % 2)
                    for a, b in ([(0, 512), (512, 768)] if nk == T else [(512, 768)]):
                        ins = three(G[:, i % 2, a:b], lambda part: Q[r, part, h % 4, q0:q0 + 128],
                                    lambda part: K[r, part, a:b], True, True)
                    done(ins)

                def turn(i):
                    h, q0, k0, nk = st_[i]
                    pe.wait_ge(s_pn, s0 + i + 1)
                    pe.wait_ge(s_pl, s0 + i)
                    for kt in range(k0 // 128, (k0 + nk) // 128):
                        c = slice(128 * kt, 128 * kt + 128)
                        ins = nc.tensor.transpose(M[:, c], P[:, i % 2, c], ident[:, :])
                    ins.then_inc(s_pt, 1)

                def values(j):
                    h, q0, k0, nk = st_[2 * j]
                    pe.wait_ge(s_pl, s0 + 2 * j + 2)
                    if s0 // 2 + j >= 2:
                        pe.wait_ge(s_ol, s0 // 2 + j - 1)
                    kts = range(k0 // 128, (k0 + nk) // 128)
                    for kt in kts:
                        ins = three(O[:, j % 2, 0:256], lambda part: V[:, part, kt, :],
                                    lambda part: PT[:, j % 2, part, kt, :], kt == kts[0], kt == kts[-1])
                    ins.then_inc(s_o, 1)
                pe.wait_ge(s_q, 5 * (l + 1))
                read_out(pe, plan.tile[l, "qkv"] + 1, 1)
                scores(0)
                for i in range(len(st_)):
                    if i + 1 < len(st_):
                        scores(i + 1)
                    if i % 2 == 0 and i >= 2:
                        values(i // 2 - 1)
                    turn(i)
                values(len(st_) // 2 - 1)

                def branch(b, i):
                    u, t = plan.unit[l, ("branch", b)] + 3 * i, plan.tile[l, ("branch", b)] + 4 * i
                    Y = (Q, CF, SCO)[b]
                    for n in range(2):
                        pe.wait_ge(s_lo, u + n + 1)
                        take_slot(t + n, n)
                        done(product(n, (i + n) % 2, KD, from_h, W))
                    pe.wait_ge(s_lo, u + 3)
                    if i == 0:
                        pe.wait_ge(*((s_ol, (s0 + len(st_)) // 2), (s_ll, KC * (l + 1)), (s_scl, KC * (l + 1)))[b])
                    for n in range(2):
                        take_slot(t + 2 + n, n)
                        done(product(n, i % 2, KC, lambda part, k, a, b_: Y[:, part, k, a:b_], W, cut=128 * n, wn=256))
                for i in range(4):
                    branch(0, i)

                u, t = plan.unit[l, "sc"], plan.tile[l, "sc"]

                def sc(i, u=u, t=t):
                    for q in range(2):
                        pe.wait_ge(s_lo, u + 2 * i + q + 1)
                        take_slot(t + 2 * i + q, q)
                        done(product(q, q, KD, from_h, W))
                loop(pe, 6, sc)

                for i in range(4):
                    if i == 2:
                        pe.wait_ge(s_ls, 6 * l + 3)
                        statistic(ln_sum, W, ones[:, :], off=ctok)
                        spread(W)
                    branch(2, i)
                pe.wait_ge(s_ls, 6 * l + 6)
                statistic(ln_sum, W, ones[:, :], off=ctok)
                pe.wait_ge(s_lsm, KC * (2 * l + 1))
                spread(W)
                for i in range(4):
                    branch(1, i)

                def pairs(phase, n, ks, rhs, ready):
                    u, t = plan.unit[l, phase], plan.tile[l, phase]

                    def turn_(i, first=False):
                        for r in range(2):
                            pe.wait_ge(s_lo, u + 2 * i + r + 1)
                            take_slot(t + 2 * i + r, r)
                            done(product(r, r, ks, rhs, W, ready if first and r == 0 else None))
                    if ready:
                        turn_(0, True)
                        loop(pe, n - 1, lambda i: turn_(i + 1))
                    else:
                        loop(pe, n, turn_)
                pairs("mix", KD // 2, KD, from_h, h_ready)
                normed[0] += KD
                norm(W)
                for p, n in enumerate(PARTS):
                    pairs(("up", p), n, KD, from_h, None if p else h_ready)
                    u0 = PARTS[0] * (p % 2)
                    pairs(("down", p), KD // 2, n, lambda part, k, a, b: U[:, u0 + k, part, a:b],
                          lambda k: pe.wait_ge(s_u, up_base[l, p] + k + 1))
                normed[0] += KD

            t = plan.tile["store"]
            phase_read_out(pe, t)
            for i in range(KD):
                take_slot(t + i, i % 2)
                for tt in range(S // 128):
                    ins = nc.tensor.transpose(G[:, i % 2, 128 * tt:128 * tt + 128], X[:, i, 128 * tt:128 * tt + 128],
                                              ident[:, :])
                done(ins)

        @block.gpsimd
        def _(pool):
            nc.gpsimd.memset(ones[:, :], 1.0).then_inc(s_set, 1)
            nc.gpsimd.memset(eps[:, :], EPS).then_inc(s_set, 1)

            def rest(u, slot):
                pool.wait_ge(s_hi, u + 1)
                nc.gpsimd.tensor_tensor(WHL[:, slot, 1, :], raw[:, slot, :], f(WHL[:, slot, 0, :]),
                                        ALU.subtract).then_inc(s_lo, 1)

            def rests(phase, n):
                u = plan.unit[l, phase] + 2

                def turn(i):
                    for r in range(2):
                        rest(u + 2 * i + r, r)
                loop(pool, n, turn)

            for r in range(2):
                rest(r, r)
            for l in range(DEPTH):
                W = WIDTH[l]
                if l:
                    pool.wait_ge(s_tile, plan.tile[l, "qkv"])
                for a, b in ((0, PAD), (PAD + S, PAD + S + GAP), (PAD + S + GAP + LC, T + 2 * GAP)):
                    nc.gpsimd.memset(hpad[:, :, a:b], 0.0).then_inc(s_pad, 1)
                rests("qkv", 3)
                rests("conf", KC)
                for i, (h, q0, k0, nk) in enumerate(steps(l)):
                    pool.wait_ge(s_pi, step_base[l] + i + 1)
                    p = P[:, i % 2, k0:k0 + nk]
                    nc.gpsimd.tensor_scalar(p, p, pinv[:, i % 4:i % 4 + 1], None, ALU.mult).then_inc(s_pn, 1)
                for b in (0, "sc", 2, 1):
                    if b == "sc":
                        pool.wait_ge(s_tile, plan.tile[l, "sc"])
                        for a in (0, S + 1, S + 2, T + 3):
                            nc.gpsimd.memset(bx[:, a:a + 1], 0.0).then_inc(s_pad, 1)
                        rests("sc", 6)
                        continue
                    u, t = plan.unit[l, ("branch", b)] + 2, plan.tile[l, ("branch", b)]
                    for i in range(4):
                        for n in range(3):
                            rest(u + 3 * i + n, (i + n) % 2)
                        if b:
                            for n in range(2):
                                read_out(pool, t + 4 * i + 2 + n, n)
                                if b == 1:
                                    pool.wait_ge(s_mg, 16 * l + 2 * i + n + 1)
                                m = merged[:, 2 * i + n, 0:W]
                                nc.gpsimd.tensor_tensor(m, m, ybuf[:, n, 0:W], ALU.add).then_inc(s_mg, 1)
                rests("mix", KD // 2)
                for p, n in enumerate(PARTS):
                    rests(("up", p), n)
                    rests(("down", p), KD // 2 - (l == DEPTH - 1 and p == len(PARTS) - 1))

        @block.scalar
        def _(act):
            def high(u, slot):
                act.wait_ge(s_w[slot], 16 * (u - slot) + 32)
                nc.scalar.activation(WHL[:, slot, 0, :], raw[:, slot, :], ACT.Copy).then_inc(s_hi, 1)

            def tile_and_high(t, u, slot):
                act.wait_ge(s_tile, t + 1)
                high(u + 2, slot)

            def free(ins, slot):
                ins.then_inc(s_free[slot], 2)

            stats, squares, hh = [0], [0], [0]

            def deviation(n, func, scale):
                k = stats[0]
                act.wait_ge(s_stat, k + 1)
                if k >= 2:
                    act.wait_ge(s_inv, k - 1)
                src = O[:, 0, 16 * (k % 2):16 * (k % 2) + n]
                if func == ACT.Sqrt:
                    ins = nc.scalar.activation(sd[:, k % 2, 0:n], src, func, bias=eps[:, :], scale=scale)
                else:
                    ins = nc.scalar.activation(sd[:, k % 2, 0:n], src, func, scale=scale)
                ins.then_inc(s_sd, 1)
                stats[0] += 1

            def square(i, r, t, width):
                read_out(act, t, r)
                if isinstance(i, int) and i < 3:
                    if i == 0:
                        nc.scalar.activation(SSQ[:, 0:width], X[:, 0, 0:width], ACT.Square).then_inc(s_sq, 1)
                        return
                else:
                    act.wait_ge(s_ssq, squares[0] + i - 2)
                src = X[:, bass.ds(i, 1), 0:width].rearrange("p a n -> p (a n)")
                nc.scalar.activation(SQ[:, r, 0:width], src, ACT.Square).then_inc(s_sq, 1)

            def h_high(shift, segs):
                for i in range(KD):
                    act.wait_ge(s_ht, hh[0] + i + 1)
                    for a, n, v in segs:
                        ins = nc.scalar.activation(H[:, 0, i, a:a + n], HT[:, i % 2, a:a + n], ACT.Identity,
                                                   bias=mod[:, shift * KD + i, v:v + 1])
                    ins.then_inc(s_hh, 1)
                hh[0] += KD

            act.wait_ge(s_parc, DEPTH)
            nc.scalar.activation(sgc[:, :, :], par[:, 0, R_C:R_C + 2 * KD].rearrange("p (v k) -> p v k", v=2),
                                 ACT.Sigmoid).then_inc(s_sgc, 1)
            for r in range(2):
                high(r, r)
            act.wait_ge(s_set, 2)
            for i in range(KD):
                square(i, i % 2, i, T)
            squares[0] += KD - 1
            for l in range(DEPTH):
                W, segs = WIDTH[l], SEGS[l]
                deviation(T // 128, ACT.Sqrt, 1.0 / D)
                act.wait_ge(s_mod, 4 * (l + 1))
                h_high(0, SEGS[0])

                def qk_steps(p):
                    n = lagging(p, 1)
                    if n is not None:
                        deviation(2 * (T if n == 0 else W) // 128, ACT.Sqrt, 1.0 / HD)
                    n = lagging(p, 4)
                    if n is not None:
                        w = T if n == 0 else W
                        act.wait_ge(s_qr, 3 * (5 * l + n + 1))
                        dst = K[:, 0, 0:w] if n == 0 else Q[:, 0, n - 1, 0:w]
                        nc.scalar.activation(dst, qraw[:, n % 4, 0:w], ACT.Copy).then_inc(s_qh, 1)

                u, t = plan.unit[l, "qkv"], plan.tile[l, "qkv"]
                for i in range(6):
                    tile_and_high(t + i, u + i, i % 2)
                    g = G[:, i % 2]
                    if i == 1:
                        nc.scalar.activation(V[:, 0].rearrange("p t n -> p (t n)"), g[:, 0:T], ACT.Copy).then_inc(s_vh, 1)
                    else:
                        n = max(i - 1, 0)
                        w = T if n == 0 else W
                        if n == 4:
                            act.wait_ge(s_q, 5 * l + 1)
                        if n:
                            act.wait_ge(s_stat, stats[0] + (n > 1))
                        nc.scalar.activation(qsq[:, 0:w], g[:, 0:w], ACT.Square).then_inc(s_qsq, 1)
                        free(nc.scalar.activation(qraw[:, n % 4, 0:w], g[:, 0:w], ACT.Copy), i % 2)
                    qk_steps(i)

                u, t = plan.unit[l, "conf"], plan.tile[l, "conf"]
                for i in range(2 * KC):
                    tile_and_high(t + i, u + i, i % 2)
                    if i % 2 == 0:
                        if i:
                            read_out(act, t + i - 1, 1)
                        free(nc.scalar.activation(GS[:, 0, 0:W], G[:, 0, 0:W], ACT.Sigmoid), 0)
                    qk_steps(6 + i)

                st_, s0, t = steps(l), step_base[l], plan.tile[l, "att"]

                def probs(i):
                    h, q0, k0, nk = st_[i]
                    act.wait_ge(s_nm, s0 + i + 1)
                    if i >= 2:
                        act.wait_ge(s_pt, s0 + i - 1)
                    free(nc.scalar.activation(P[:, i % 2, k0:k0 + nk], G[:, i % 2, k0:k0 + nk], ACT.Exp,
                                              bias=nmax[:, i % 4:i % 4 + 1], accum_out=psum_[:, i % 4:i % 4 + 1]), i % 2)

                def turned(i):
                    h, q0, k0, nk = st_[i]
                    act.wait_ge(s_pt, s0 + i + 1)
                    j = i // 2
                    if j >= 2:
                        act.wait_ge(s_o, s0 // 2 + j - 1)
                    nc.scalar.activation(PT[:, j % 2, 0, k0 // 128:(k0 + nk) // 128, 128 * (i % 2):128 * (i % 2) + 128],
                                         M[:, k0:k0 + nk].rearrange("p (k n) -> p k n", n=128), ACT.Copy)\
                        .then_inc(s_ph, 1)

                def outs(j):
                    h, q0, k0, nk = st_[2 * j]
                    r = slice(64 * (h // 4), 64 * (h // 4) + 64)
                    act.wait_ge(s_o, s0 // 2 + j + 1)
                    nc.scalar.activation(Q[r, 0, h % 4, q0:q0 + 256], O[r, j % 2, 0:256], ACT.Copy).then_inc(s_oh, 1)
                probs(0)
                for i in range(len(st_)):
                    if i + 1 < len(st_):
                        probs(i + 1)
                    if i % 2 == 0 and i >= 2:
                        outs(i // 2 - 1)
                    turned(i)
                outs(len(st_) // 2 - 1)

                def branch(b, i, middle=None):
                    u, t = plan.unit[l, ("branch", b)] + 3 * i, plan.tile[l, ("branch", b)] + 4 * i
                    for n in range(2):
                        tile_and_high(t + n, u + n, (i + n) % 2)
                        if i:
                            read_out(act, t - 2 + n, n)
                        free(nc.scalar.activation(GS[:, n, 0:W], G[:, n, 0:W], ACT.Sigmoid), n)
                    tile_and_high(t + 3, u + 2, i % 2)
                for i in range(4):
                    branch(0, i)

                u, t = plan.unit[l, "sc"], plan.tile[l, "sc"]
                phase_read_out(act, t)
                for i in range(KC):
                    a = 3 * i
                    tile_and_high(t + a, u + a, a % 2)
                    if i:
                        read_out(act, t + a - 2, a % 2)
                    free(nc.scalar.activation(GS[:, 0, 0:W], G[:, a % 2, 0:W], ACT.Copy), a % 2)
                    for n in (1, 2):
                        tile_and_high(t + a + n, u + a + n, (a + n) % 2)
                    read_out(act, t + a + 2, a % 2)
                    nc.scalar.activation(SCO[:, 0, i, 0:W], GS[:, 1, 0:W], ACT.Copy).then_inc(s_sch, 1)
                act.wait_ge(s_scl, KC * (l + 1))

                Wc = CONV_W[l]
                for i in range(4):
                    branch(2, i)
                    if i == 1:
                        deviation(W // 128, ACT.Copy, 1.0 / CW)
                    if i == 2:
                        for n in range(KC):
                            act.wait_ge(s_lsm, KC * 2 * l + n + 1)
                            if n == 3:
                                act.wait_ge(s_ls, 6 * l + 4)
                            nc.scalar.activation(ln_sum[:, 0:Wc] if n == 0 else ln_sq[:, n % 2, 0:Wc], acc[:, n, 0:Wc],
                                                 ACT.Square).then_inc(s_lsq, 1)
                deviation(W // 128, ACT.Sqrt, 1.0 / CW)
                for n in range(KC):
                    act.wait_ge(s_lsm, KC * (2 * l + 1) + n + 1)
                    if n >= 2:
                        act.wait_ge(s_lv, KC * l + n - 1)
                    nc.scalar.activation(sig[:, n % 2, 0:Wc], acc[:, n, 0:Wc], ACT.Sigmoid,
                                         bias=par[:, l, R_LB + n:R_LB + n + 1]).then_inc(s_lsg, 1)
                act.wait_ge(s_lv, KC * (l + 1))
                for n in range(KC):
                    for a, w, v in segs:
                        ins = nc.scalar.activation(CF[:, 0, n, a:a + w], acc[:, n, ctok(a):ctok(a) + w], ACT.Copy)
                    ins.then_inc(s_lh, 1)
                for i in range(4):
                    branch(1, i)

                act.wait_ge(s_tile, plan.tile[l, ("branch", 1)] + 14)
                for i in range(KD):
                    act.wait_ge(s_mg, 16 * l + KD + i + 1)
                    nc.scalar.activation(H[:, 0, i, 0:W], merged[:, i, 0:W], ACT.Copy).then_inc(s_mh, 1)

                def x_tiles(phase, width, with_squares):
                    u, t = plan.unit[l, phase], plan.tile[l, phase]

                    def turn(i, more=True):
                        for r in range(2):
                            if more:
                                tile_and_high(t + 2 * i + r, u + 2 * i + r, r)
                            if with_squares:
                                square(2 * i + r, r, t + 2 * i + r, width)
                    turn(0)
                    loop(act, KD // 2 - 2, lambda i: turn(i + 1))
                    turn(KD // 2 - 1, u + KD < plan.units)
                    if with_squares:
                        squares[0] += KD - 1
                x_tiles("mix", W, True)
                deviation(W // 128, ACT.Sqrt, 1.0 / D)
                h_high(3, segs)

                for p, n in enumerate(PARTS):
                    u, t = plan.unit[l, ("up", p)], plan.tile[l, ("up", p)]

                    def up(i, u=u, t=t, p=p, first=False):
                        tile_and_high(t + 2 * i, u + 2 * i, 0)
                        if not first:
                            act.wait_ge(s_u, up_base[l, p] + i)
                        free(nc.scalar.activation(GS[:, 0, 0:W], G[:, 0, 0:W], ACT.Silu), 0)
                        tile_and_high(t + 2 * i + 1, u + 2 * i + 1, 1)
                        read_out(act, t + 2 * i + 1, 1)
                        dst = U[:, bass.ds(i + PARTS[0] * (p % 2), 1), 0, 0:W].rearrange("p a n -> p (a n)")
                        nc.scalar.activation(dst, GS[:, 0, 0:W], ACT.Copy).then_inc(s_uh, 1)
                    up(0, first=up_base[l, p] == 0)
                    loop(act, n - 1, lambda i: up(i + 1))
                    x_tiles(("down", p), W, p == len(PARTS) - 1 and l < DEPTH - 1)

            t = plan.tile["store"]
            for i in range(KD):
                act.wait_ge(s_tile, t + i + 1)
                free(nc.scalar.activation(xout[:, :, 128 * i:128 * i + 128],
                                          G[:, i % 2, 0:S].rearrange("p (t n) -> p t n", n=128), ACT.Copy), i % 2)

        @block.vector
        def _(dve):
            V_ = nc.vector

            def stt(o_, a, s, b, op0, op1):
                return V_.scalar_tensor_tensor(o_, a, s, b, op0, op1)

            def free(ins, slot):
                ins.then_inc(s_free[slot], 2)

            for l in range(DEPTH):
                dve.wait_ge(s_part, l + 1)
                V_.tensor_copy(par[:, l, :], O[:, l, 0:PAR_ROWS])
                V_.tensor_copy(cw[:, l, :], O[:, l, 128:128 + CONV_ROWS]).then_inc(s_parc, 1)
            dve.wait_ge(s_parc, DEPTH)
            for l in range(DEPTH):
                V_.tensor_scalar(qg[:, l, 1:2], par[:, l, R_QN:R_QN + 1], HD ** -0.5, None, ALU.mult)
                V_.tensor_copy(qg[:, l, 0:1], par[:, l, R_KN:R_KN + 1]).then_inc(s_qg, 1)
            dve.wait_ge(s_sgc, 1)
            V_.tensor_tensor(csil[:, :, :].rearrange("p k v -> p v k"),
                             par[:, 0, R_C:R_C + 2 * KD].rearrange("p (v k) -> p v k", v=2), sgc[:, :, :], ALU.mult)\
                .then_inc(s_csil, 1)

            for i in range(KD):
                dve.wait_ge(s_tile, i + 1)
                free(V_.tensor_copy(X[:, i, :], G[:, i % 2, 0:T]), i % 2)

            invs, squares, norms, split = [0], [0], [0], [0]

            def inverse(n, func="reciprocal"):
                k = invs[0]
                dve.wait_ge(s_sd, k + 1)
                if k >= 2:
                    dve.wait_ge(s_spread, k - 1)
                if func == "mean":
                    V_.tensor_copy(rs[:, k % 2, 0:n], sd[:, k % 2, 0:n]).then_inc(s_inv, 1)
                elif func == "heads":
                    V_.reciprocal(rs[:, k % 2, 0:n], sd[:, k % 2, 0:n]).then_inc(s_rc, 1)
                    dve.wait_ge(s_rc, heads_done[0] + 1)
                    dve.wait_ge(s_spread, k)
                    V_.tensor_copy(qspread[:, 0:n // 2].rearrange("p t h d -> p (t h) d"),
                                   rs[:, k % 2, 0:n].unsqueeze(2).to_broadcast([128, n, HD])).then_inc(s_inv, 1)
                    heads_done[0] += 1
                else:
                    V_.reciprocal(rs[:, k % 2, 0:n], sd[:, k % 2, 0:n]).then_inc(s_inv, 1)
                invs[0] += 1
            heads_done = [0]

            def add_square(i, r, width):
                if isinstance(i, int) and i == 0:
                    return
                dve.wait_ge(s_sq, squares[0] + i + 1)
                if not (isinstance(i, int) and i == 1):
                    dve.wait_ge(s_ssq, squares[0] // KD * (KD - 1) + i - 1)
                V_.tensor_tensor(SSQ[:, 0:width], SSQ[:, 0:width], SQ[:, r, 0:width], ALU.add).then_inc(s_ssq, 1)

            def norm(scale, shift, segs, width):
                dve.wait_ge(s_spread, invs[0])

                def scaled(i):
                    if i >= 2:
                        dve.wait_ge(s_h, split[0] + i - 1)
                    for a, n, v in segs:
                        ins = stt(HT[:, i % 2, a:a + n], X[:, i, a:a + n], mod[:, scale * KD + i, v:v + 1],
                                  M[:, a:a + n], ALU.mult, ALU.mult)
                    ins.then_inc(s_ht, 1)

                def rests(i):
                    dve.wait_ge(s_hh, norms[0] + i + 1)
                    for a, n, v in segs:
                        ins = stt(H[:, 1, i, a:a + n], HT[:, i % 2, a:a + n], mod[:, shift * KD + i, v:v + 1],
                                  f(H[:, 0, i, a:a + n]), ALU.add, ALU.subtract)
                    ins.then_inc(s_h, 1)
                scaled(0)
                for i in range(KD):
                    if i + 1 < KD:
                        scaled(i + 1)
                    rests(i)
                norms[0] += KD
                split[0] += KD

            def x_tiles(phase, gate, segs, with_squares):
                t = plan.tile[l, phase]
                phase_read_out(dve, t)

                def turn(i):
                    for r in range(2):
                        dve.wait_ge(s_tile, t + 2 * i + r + 1)
                        for a, n, v in segs:
                            x = X[:, bass.ds(2 * i + r, 1), a:a + n].rearrange("p a n -> p (a n)")
                            m = mod[:, bass.ds(2 * i + r + gate * KD, 1), v:v + 1].rearrange("p a n -> p (a n)")
                            ins = stt(x, G[:, r, a:a + n], m, x, ALU.mult, ALU.add)
                        free(ins, r)
                        if with_squares:
                            add_square(2 * i + r, r, WIDTH[l])
                turn(0)
                loop(dve, KD // 2 - 1, lambda i: turn(i + 1))
                if with_squares:
                    squares[0] += KD

            for i in range(KD):
                add_square(i, i % 2, T)
            squares[0] += KD

            for l in range(DEPTH):
                W, segs, Wc = WIDTH[l], SEGS[l], CONV_W[l]
                inverse(T // 128)
                dve.wait_ge(s_adt, MT * (l + 1))
                for v in range(2):
                    V_.tensor_tensor(mod[:, :, v], O[:, 1, 0:2 * MT].rearrange("p (m v) -> p m v", v=2)[:, :, v],
                                     par[:, l, 0:MT], ALU.add).then_inc(s_mod, 1)
                dve.wait_ge(s_mod, 4 * l + 2)
                for c in (1, 4):
                    V_.tensor_scalar(mod[:, c * KD:(c + 1) * KD, :], mod[:, c * KD:(c + 1) * KD, :], 1.0, None,
                                     ALU.add).then_inc(s_mod, 1)
                dve.wait_ge(s_mod, 4 * l + 4)
                norm(1, 0, SEGS[0], T)

                dve.wait_ge(s_rope, 32 * (l + 1))
                dve.wait_ge(s_qg, DEPTH)

                def qk_steps(p):
                    n = lagging(p, 4)
                    if n is not None:
                        w = T if n == 0 else W
                        dve.wait_ge(s_qh, 5 * l + n + 1)
                        hi, lo = [K[:, part, 0:w] if n == 0 else Q[:, part, n - 1, 0:w] for part in range(2)]
                        V_.tensor_tensor(lo, qraw[:, n % 4, 0:w], f(hi), ALU.subtract).then_inc(s_q, 1)
                    n = lagging(p, 1)
                    if n is not None:
                        inverse(2 * (T if n == 0 else W) // 128, "heads")
                    n = lagging(p, 2)
                    if n is not None:
                        w = T if n == 0 else W
                        dve.wait_ge(s_spread, invs[0] - (lagging(p, 1) is not None))
                        tq = plan.tile[l, "qkv"] + (n + 1 if n else 0)
                        read_out(dve, tq, tq % 2)
                        stt(qraw[:, n % 4, 0:w], qraw[:, n % 4, 0:w], qg[:, l, (0 if n == 0 else 1):(1 if n == 0 else 2)],
                            M[:, 0:w], ALU.mult, ALU.mult).then_inc(s_qn, 1)
                    n = lagging(p, 3)
                    if n is not None:
                        q, c = qraw[:, n % 4, 0:S], 3 * (5 * l + n)
                        dve.wait_ge(s_rot, 5 * l + n + 1)
                        if c:
                            dve.wait_ge(s_qr, c)
                        V_.tensor_tensor(qrot[:, :], O[:, 1, 0:S], rope[:, 1, :], ALU.mult).then_inc(s_qr, 1)
                        V_.tensor_tensor(q, q, rope[:, 0, :], ALU.mult).then_inc(s_qr, 1)
                        dve.wait_ge(s_qr, c + 2)
                        V_.tensor_tensor(q, q, qrot[:, :], ALU.add).then_inc(s_qr, 1)

                t = plan.tile[l, "qkv"]
                for i in range(6):
                    if i == 1:
                        dve.wait_ge(s_vh, l + 1)
                        free(V_.tensor_tensor(V[:, 1].rearrange("p t n -> p (t n)"), G[:, 1, 0:T],
                                              f(V[:, 0].rearrange("p t n -> p (t n)")), ALU.subtract), 1)
                    qk_steps(i)

                t = plan.tile[l, "conf"]
                dve.wait_ge(s_pad, 7 * l + 3)
                for i in range(2 * KC):
                    if i % 2:
                        dve.wait_ge(s_tile, t + i + 1)
                        read_out(dve, t + i - 1, 0)
                        for a, n, v in segs:
                            ins = V_.tensor_tensor(hpad[:, i // 2, PAD + ctok(a):PAD + ctok(a) + n], G[:, 1, a:a + n],
                                                   GS[:, 0, a:a + n], ALU.mult)
                        free(ins, 1)
                    qk_steps(6 + i)

                st_, s0, t = steps(l), step_base[l], plan.tile[l, "att"]

                def maxima(i):
                    h, q0, k0, nk = st_[i]
                    dve.wait_ge(s_tile, t + i + 1)
                    V_.tensor_reduce(nmax[:, i % 4:i % 4 + 1], G[:, i % 2, k0:k0 + nk], AX.X, ALU.max, negate=True)\
                        .then_inc(s_nm, 1)

                def scales(i):
                    read_out(dve, t + i, i % 2)
                    V_.reciprocal(pinv[:, i % 4:i % 4 + 1], psum_[:, i % 4:i % 4 + 1]).then_inc(s_pi, 1)

                def turned(i):
                    h, q0, k0, nk = st_[i]
                    j, a, b, c = i // 2, k0 // 128, (k0 + nk) // 128, 128 * (i % 2)
                    dve.wait_ge(s_ph, s0 + i + 1)
                    V_.tensor_tensor(PT[:, j % 2, 1, a:b, c:c + 128], M[:, k0:k0 + nk].rearrange("p (k n) -> p k n", n=128),
                                     f(PT[:, j % 2, 0, a:b, c:c + 128]), ALU.subtract).then_inc(s_pl, 1)

                def outs(j):
                    h, q0, k0, nk = st_[2 * j]
                    r = slice(64 * (h // 4), 64 * (h // 4) + 64)
                    dve.wait_ge(s_oh, s0 // 2 + j + 1)
                    V_.tensor_tensor(Q[r, 1, h % 4, q0:q0 + 256], O[r, j % 2, 0:256], f(Q[r, 0, h % 4, q0:q0 + 256]),
                                     ALU.subtract).then_inc(s_ol, 1)
                maxima(0)
                for i in range(len(st_)):
                    if i + 1 < len(st_):
                        maxima(i + 1)
                    scales(i)
                    if i % 2 == 0 and i >= 2:
                        outs(i // 2 - 1)
                    turned(i)
                outs(len(st_) // 2 - 1)

                def taps(j0, n):
                    def tap(i):
                        for k in range(KC):
                            step = KC * TAPS * l + KC * j0 + k + KC * i
                            dve.wait_ge(s_tap, step - KC + 1)
                            w = cw[:, l, bass.ds(i * KC + KC * j0 + k, 1)]
                            stt(acc[:, k, 0:Wc], hpad[:, k, bass.ds(i + j0, Wc)], w, acc[:, k, 0:Wc],
                                ALU.mult, ALU.add).then_inc(s_tap, 1)
                    loop(dve, n, tap)

                for k in range(KC):
                    V_.tensor_scalar(acc[:, k, 0:Wc], hpad[:, k, 0:Wc], cw[:, l, k:k + 1],
                                     par[:, l, R_CB + k:R_CB + k + 1], ALU.mult, ALU.add).then_inc(s_tap, 1)

                def branch(b, i):
                    t = plan.tile[l, ("branch", b)] + 4 * i
                    for n in range(2):
                        dve.wait_ge(s_tile, t + 2 + n + 1)
                        read_out(dve, t + n, n)
                        if b == 0:
                            dst = merged[:, 2 * i + n, 0:W]
                        else:
                            dst = ybuf[:, n, 0:W]
                            done = 16 * l + KD * (b == 1) + 2 * (i - 1) + n + 1
                            if i or b == 1:
                                dve.wait_ge(s_mg, done)
                        free(V_.tensor_tensor(dst, G[:, n, 0:W], GS[:, n, 0:W], ALU.mult), n)
                for i in range(4):
                    taps(1 + 4 * i, 4)
                    branch(0, i)

                t = plan.tile[l, "sc"]
                phase_read_out(dve, t)
                dve.wait_ge(s_pad, 7 * (l + 1))
                Ws = W + 2 if l == 0 else W
                j0 = 17
                for i in range(KC):
                    a, n_taps = 3 * i, 4 - i % 2
                    taps(j0, n_taps)
                    j0 += n_taps
                    dve.wait_ge(s_tile, t + a + 2)
                    read_out(dve, t + a, a % 2)
                    for c, n, v in segs:
                        o_ = 1 + c + 2 * v
                        ins = V_.tensor_tensor(bx[:, o_:o_ + n], G[:, (a + 1) % 2, c:c + n], GS[:, 0, c:c + n], ALU.mult)
                    free(ins, (a + 1) % 2)
                    read_out(dve, t + a + 1, (a + 1) % 2)
                    c0 = 3 * (KC * l + i)
                    for j in range(SC_TAPS):
                        w = par[:, l, R_SC + j * KC + i:R_SC + j * KC + i + 1]
                        if j == 0:
                            ins = V_.tensor_scalar(sc_sum[:, 0:Ws], bx[:, 0:Ws], w, None, ALU.mult)
                        else:
                            dve.wait_ge(s_sct, c0 + j)
                            ins = stt(sc_sum[:, 0:Ws], bx[:, j:j + Ws], w, sc_sum[:, 0:Ws], ALU.mult, ALU.add)
                        ins.then_inc(s_sct, 1)
                    dve.wait_ge(s_sct, c0 + 3)
                    dve.wait_ge(s_tile, t + a + 3)
                    if i:
                        dve.wait_ge(s_scl, KC * l + i)
                    for c, n, v in segs:
                        ins = V_.tensor_tensor(GS[:, 1, c:c + n], G[:, a % 2, c:c + n], sc_sum[:, c + 2 * v:c + 2 * v + n],
                                               ALU.mult)
                    free(ins, a % 2)
                    dve.wait_ge(s_sch, KC * l + i + 1)
                    V_.tensor_tensor(SCO[:, 1, i, 0:W], GS[:, 1, 0:W], f(SCO[:, 0, i, 0:W]), ALU.subtract).then_inc(s_scl, 1)
                assert j0 == TAPS

                def ln_add(k, out_, in_, src):
                    V_.tensor_tensor(out_, in_, src, ALU.add).then_inc(s_ls, 1)
                dve.wait_ge(s_tap, KC * TAPS * (l + 1))
                for k in range(1, KC):
                    if k > 1:
                        dve.wait_ge(s_ls, 6 * l + k - 1)
                    V_.tensor_tensor(ln_sum[:, 0:Wc], acc[:, 0, 0:Wc] if k == 1 else ln_sum[:, 0:Wc], acc[:, k, 0:Wc],
                                     ALU.add).then_inc(s_ls, 1)
                for i in range(4):
                    branch(2, i)
                    if i == 1:
                        inverse(W // 128, "mean")
                        dve.wait_ge(s_spread, invs[0])
                        for k in range(KC):
                            for a, n, v in segs:
                                c = ctok(a)
                                ins = V_.tensor_tensor(acc[:, k, c:c + n], acc[:, k, c:c + n], M[:, a:a + n], ALU.subtract)
                            ins.then_inc(s_lsm, 1)
                    if i == 2:
                        for k in range(1, KC):
                            dve.wait_ge(s_lsq, KC * l + k + 1)
                            if k > 1:
                                dve.wait_ge(s_ls, 6 * l + 3 + k - 1)
                            V_.tensor_tensor(ln_sum[:, 0:Wc], ln_sum[:, 0:Wc], ln_sq[:, k % 2, 0:Wc], ALU.add)\
                                .then_inc(s_ls, 1)
                inverse(W // 128)
                dve.wait_ge(s_spread, invs[0])
                dve.wait_ge(s_lsm, KC * (2 * l + 1))
                for k in range(KC):
                    for a, n, v in segs:
                        c = ctok(a)
                        ins = stt(acc[:, k, c:c + n], acc[:, k, c:c + n], par[:, l, R_LG + k:R_LG + k + 1], M[:, a:a + n],
                                  ALU.mult, ALU.mult)
                    ins.then_inc(s_lsm, 1)
                for k in range(KC):
                    dve.wait_ge(s_lsg, KC * l + k + 1)
                    stt(acc[:, k, 0:Wc], acc[:, k, 0:Wc], par[:, l, R_LB + k:R_LB + k + 1], sig[:, k % 2, 0:Wc],
                        ALU.add, ALU.mult).then_inc(s_lv, 1)
                for k in range(KC):
                    dve.wait_ge(s_lh, KC * l + k + 1)
                    for a, n, v in segs:
                        c = ctok(a)
                        ins = V_.tensor_tensor(CF[:, 1, k, a:a + n], acc[:, k, c:c + n], f(CF[:, 0, k, a:a + n]), ALU.subtract)
                    ins.then_inc(s_ll, 1)
                for i in range(4):
                    branch(1, i)

                for i in range(KD):
                    dve.wait_ge(s_mh, KD * l + i + 1)
                    V_.tensor_tensor(H[:, 1, i, 0:W], merged[:, i, 0:W], f(H[:, 0, i, 0:W]), ALU.subtract).then_inc(s_h, 1)
                split[0] += KD
                x_tiles("mix", 2, segs, True)
                inverse(W // 128)
                norm(4, 3, segs, W)

                for p, n in enumerate(PARTS):
                    t = plan.tile[l, ("up", p)]

                    def up(i, t=t, p=p):
                        dve.wait_ge(s_tile, t + 2 * i + 2)
                        read_out(dve, t + 2 * i, 0)
                        free(V_.tensor_tensor(GS[:, 0, 0:W], G[:, 1, 0:W], GS[:, 0, 0:W], ALU.mult), 1)
                        dve.wait_ge(s_uh, up_base[l, p] + i + 1)
                        c = bass.ds(i + PARTS[0] * (p % 2), 1)
                        hi, lo = [U[:, c, part, 0:W].rearrange("p a n -> p (a n)") for part in range(2)]
                        V_.tensor_tensor(lo, GS[:, 0, 0:W], f(hi), ALU.subtract).then_inc(s_u, 1)
                    loop(dve, n, up)
                    x_tiles(("down", p), 5, segs, p == len(PARTS) - 1 and l < DEPTH - 1)


_INS = ['x', 'c', 'ctx', 'c_ctx', 'w_ada', 'b_ada', 'w_in', 'q_norm', 'k_norm', 'w_attn_o', 'conf_dw_w', 'conf_dw_b',
        'conf_ln_g', 'conf_ln_b', 'w_conf_out', 'sc_dw_w', 'w_sc_out', 'w_mix_out', 'w_ffn_in', 'w_ffn_out']


def _constants():
    f32 = np.float32
    freqs = (ROPE_THETA ** (-np.arange(0, HD // 2, 2, dtype=f32) / f32(HD // 2))).astype(f32)
    tok = np.arange(S)
    angles = np.concatenate([np.tile((tok // GRID_W).astype(f32)[:, None] * freqs, 2),
                             np.tile((tok % GRID_W).astype(f32)[:, None] * freqs, 2)], axis=1)
    ang = np.tile(angles, 2).T
    swap = np.zeros((128, 128), f32)
    for m in range(128):
        if m % 32 < 16:
            swap[m + 16, m] = -1
        else:
            swap[m - 16, m] = 1
    heads = np.zeros((128, 2), f32)
    heads[:64, 0] = heads[64:, 1] = 1
    return {"ident": np.eye(128, dtype=f32), "swap": swap, "heads": heads,
            "rope": np.ascontiguousarray(np.stack([np.cos(ang), np.sin(ang)]).astype(f32))}


def kernel(**inputs):
    import concourse.bacc as _bacc
    from concourse.bass_utils import run_bass_kernel_spmd as _run

    nc = _bacc.Bacc("TRN2", target_bir_lowering=False, num_devices=1)
    arrays, aps = {}, {}
    for name, a in [(n, np.ascontiguousarray(inputs[n])) for n in _INS] + list(_constants().items()):
        arrays[f"in_{name}"] = a
        aps[name] = nc.dram_tensor(f"in_{name}", a.shape, mybir.dt.from_np(a.dtype), kind="ExternalInput").ap()
    out = nc.dram_tensor("out", (1, S, D), F32, kind="ExternalOutput").ap()
    build(nc, aps, out)
    return _run(nc, [arrays], core_ids=[0]).results[0]["out"]
```

```python
import numpy as np
import concourse.bass as bass
from concourse import mybir

F32, F32R = mybir.dt.float32, mybir.dt.float32r
ALU, ACT, AX = mybir.AluOpType, mybir.ActivationFunctionType, mybir.AxisListType

DEPTH, D, S, LC = 2, 1024, 512, 256
T = S + LC
KD = D // 128
HD, NH, NKV = 64, 8, 2
ATT, KVW = NH * HD, NKV * HD
CW = D // 2
KC = CW // 128
TAPS, SC_TAPS = 31, 3
PAD = TAPS // 2
FFN = 2816
OFF_K, OFF_V, OFF_CONF = ATT, ATT + KVW, ATT + 2 * KVW
OFF_SC = OFF_CONF + 2 * CW
OFF_GATE = OFF_SC + 3 * CW
IN_WIDTH = OFF_GATE + 3 * D
N_MOD = 6
EPS = 1e-6
ROPE_THETA, GRID_W = 10000.0, 64
MT = N_MOD * KD
PARTS = [6, 6, 6, 4]
SEGS = [[(0, S, 0), (S, LC, 1)], [(0, S, 0)]]
WIDTH = [T, S]
GAP = 2 * PAD
CONV_W = [T + GAP, S]
R_CB = 0
R_LG = R_CB + DEPTH * KC
R_LB = R_LG + DEPTH * KC
R_SC = R_LB + DEPTH * KC
R_QN = R_SC + DEPTH * SC_TAPS * KC
R_KN = R_QN + DEPTH
R_C = R_KN + DEPTH
PAR_ROWS = R_C + 2 * KD
CONV_ROWS = TAPS * KC
LOOPS = True


def ctok(c):
    return c if c < S else c + GAP


class Plan:

    def __init__(self):
        self.unit, self.tile, self.last = {}, {}, []
        u = t = 0
        self.tile["load"] = 0
        t += KD
        for l in range(DEPTH):
            phases = [("qkv", [1] * 6), ("conf", [1] * 8), ("att", None)]
            phases += [(("branch", 0), [1, 1, 2] * 4), ("sc", [1] * 12)]
            phases += [(("branch", 2), [1, 1, 2] * 4), (("branch", 1), [1, 1, 2] * 4)]
            phases += [("mix", [1] * KD)]
            for p, n in enumerate(PARTS):
                phases += [(("up", p), [1] * 2 * n), (("down", p), [1] * KD)]
            for name, tiles in phases:
                self.unit[l, name], self.tile[l, name] = u, t
                if name == "att":
                    t += len(steps(l))
                    continue
                for n in tiles:
                    t += n
                    u += 1
                    self.last.append(t)
            assert u % 2 == 0 and t % 2 == 0
        self.tile["store"] = t
        self.units = u


def batches(l):
    out = [(i, 0, S, 0, T, 8 * i) for i in range(KC)]
    if l == 0:
        out += [(i, S, LC, S, LC, 32 + 4 * i) for i in range(KC)]
    return out


def steps(l):
    return [(g, i, q0 + 128 * j, k0, nk, c0 + 2 * j + g)
            for i, q0, nq, k0, nk, c0 in batches(l) for g in range(NKV) for j in range(nq // 128)]


ADA_FIRST = 2 * KD
ADA_PHASES = [("branch", 0), "sc", ("branch", 2), ("branch", 1), "mix", ("up", 0), ("up", 1)]
ADA_UNITS = [12, 12, 12, 12, KD, 2 * PARTS[0], 2 * PARTS[1]]
ADA_BASE = {ph: sum(ADA_UNITS[:i]) for i, ph in enumerate(ADA_PHASES)}
assert sum(ADA_UNITS) == DEPTH * MT - ADA_FIRST

def loop(eng, n, body):
    if LOOPS and n > 2:
        with eng.Fori(0, n) as i:
            body(i)
    else:
        for i in range(n):
            body(i)


def build(nc, A, out):
    plan = Plan()

    base = 17 * 1024
    at = {}

    def region(name, size):
        at[name] = base + sum(sizes.values())
        sizes[name] = size
    sizes = {}
    region("X", KD * T * 4)
    region("H", KD * T * 8)
    region("AS", KC * T * 8)
    region("CF", KC * T * 8)
    region("DD", KD * T * 4)
    region("EE", 19200)
    region("RAW", 2 * 4096)
    region("WHL", 2 * 8192)
    region("GS", 2 * T * 4)
    region("CONST", 14400)

    def sb(name, shape, dt, where, off=0):
        return nc.alloc_sbuf_tensor_at(name, shape, dt, offset=at[where] + off)

    X = sb("x_T", [128, KD, T], F32, "X")
    H = sb("h_parts", [128, 2, KD, T], F32R, "H")
    ada = sb("ada_weights", [128, 6, KD, 256], F32, "H")
    Q = sb("q_parts", [128, 2, KC, T], F32R, "AS")
    SCO = sb("shortconv_parts", [128, 2, KC, T], F32R, "AS")
    hpad = sb("conf_padded", [128, KC, T + 2 * GAP], F32, "CF")
    CF = sb("conf_parts", [128, 2, KC, T], F32R, "CF")
    ln_sum = sb("ln_sum", [128, T + GAP], F32, "CF")
    ln_sq = sb("ln_square", [128, 2, T + GAP], F32, "CF", 3200)
    sig = sb("ln_sigmoid", [128, 2, T + GAP], F32, "CF", 9600)
    merged = sb("merged", [128, KD, T], F32, "DD")
    xin = sb("x_rows", [128, T // 128, D], F32, "DD")
    qraw = sb("q_raw", [128, 4, T], F32, "DD")
    qsq = sb("q_square", [128, T], F32, "DD", 16 * T)
    qspread = sb("q_inverse_spread", [128, T // 128, 2, HD], F32, "DD", 20 * T)
    qrot = sb("q_rotated", [128, S], F32, "DD", 24 * T)
    rope = sb("rope_tables", [128, 2, S], F32, "DD", 24 * T + 4 * S)
    heads_raw = sb("heads_unscaled", [128, KC, T], F32, "AS", 4 * KC * T)
    PT = sb("probs_T_parts", [128, 2, 2, T // 128, 256], F32R, "DD")
    U = sb("hidden_parts", [128, 2 * PARTS[0], 2, T], F32R, "AS")
    K = sb("k_parts", [128, 2, T], F32R, "EE")
    V = sb("v_parts", [128, 2, T // 128, 128], F32R, "EE", 8 * T)
    P = sb("probs", [128, 2, T], F32, "EE", 16 * T)
    acc = sb("conv_sum", [128, KC, T + GAP], F32, "EE")
    E2 = 16 * (T + GAP)
    bx = sb("sc_padded", [128, T + 4], F32, "EE", E2)
    sc_sum = sb("sc_sum", [128, T + 2], F32, "EE", E2 + 3104)
    ybuf = sb("gated", [128, 2, T], F32, "EE", E2)
    SQ = sb("x_square", [128, 2, T], F32, "EE")
    SSQ = sb("sum_square", [128, T], F32, "EE", 8 * T)
    HT = sb("h_scaled", [128, 2, T], F32, "EE", 12 * T)
    stage = sb("parameter_rows", [128, 4, 128], F32, "EE")
    xout = sb("out_rows", [128, S // 128, D], F32, "EE")
    raw = sb("w_raw", [128, 2, 1024], F32, "RAW")
    WHL = sb("w_parts", [128, 2, 2, 1024], F32R, "WHL")
    GS = sb("gates", [128, 2, T], F32, "GS")
    pspread = sb("prob_scale_spread", [128, 8, HD], F32, "GS")
    used = [0]

    def const(name, shape):
        t_ = sb(name, shape, F32, "CONST", used[0])
        used[0] += -(-4 * int(np.prod(shape[1:])) // 32) * 32
        return t_

    ident = const("identity", [128, 128])
    swap = const("rope_swap", [128, 128])
    ones = const("ones", [128, 1])
    heads = const("head_columns", [128, 2])
    eps = const("eps", [128, 1])
    bada = const("modulation_bias", [128, DEPTH, MT])
    par = const("parameters", [128, PAR_ROWS])
    cw = const("conv_taps", [128, DEPTH, CONV_ROWS])
    qg = const("head_gains", [128, DEPTH, 2])
    csil = const("silu_c", [128, KD, 2])
    sgc = const("sigmoid_c", [128, 2, KD])
    mods = const("modulation", [128, DEPTH, MT, 2])
    adaw = const("ada_tile_weights", [128, KD, 128])
    sd = const("deviation", [128, 2, 12])
    rs = const("inverse_deviation", [128, 2, 12])
    nmax = const("minus_max", [128, 4])
    psums = const("prob_sums", [128, 48])
    pinv = const("prob_scales", [128, 48])
    assert used[0] <= sizes["CONST"] and at["CONST"] + used[0] <= nc.sbuf_usable_end

    G = nc.alloc_psum_tensor("tiles", [128, 2, 1024], F32)
    M = nc.alloc_psum_tensor("small_wide", [128, 1024], F32)
    O = nc.alloc_psum_tensor("small_pair", [128, 2, 512], F32)

    sem = nc.alloc_semaphore
    s_const, s_in, s_par, s_rope = sem("constants_in"), sem("rows_in"), sem("parameter_rows_in"), sem("rope_in")
    s_ada = [sem(f"ada_in_{i}") for i in range(6)]
    s_w = [sem(f"raw_in_{i}") for i in range(2)]
    s_out = sem("out_stored")
    s_set = sem("constants_set")
    s_part, s_parc, s_qg = sem("parameters_transposed"), sem("parameters_copied"), sem("gains_scaled")
    s_sgc, s_csil = sem("sigmoid_c_done"), sem("silu_c_done")
    s_adw, s_mt = sem("ada_tile_in"), sem("modulation_tile_done")
    s_adt, s_mod = sem("ada_tile_done"), sem("modulation_steps")
    s_hi, s_lo = sem("w_high_done"), sem("w_rest_done")
    s_tile = sem("tile_done")
    s_free = [sem(f"tile_read_out_{i}") for i in range(2)]
    s_sq, s_ssq = sem("square_done"), sem("square_summed")
    s_stat, s_sd, s_rc, s_inv, s_spread = (sem("statistic_done"), sem("deviation_done"), sem("reciprocal_done"),
                                           sem("inverse_done"), sem("spread_done"))
    s_ht, s_hh, s_h = sem("h_scaled_done"), sem("h_high_done"), sem("h_parts_done")
    s_qsq, s_qn, s_rot, s_qr = sem("q_square_done"), sem("q_scaled"), sem("q_rotation_done"), sem("q_rope_steps")
    s_qh, s_q, s_vh = sem("q_high_done"), sem("q_parts_done"), sem("v_high_done")
    s_nm = sem("minus_max_done")
    s_pt = [sem(f"probs_transposed_{i}") for i in range(2)]
    s_ph = [sem(f"probs_T_high_done_{i}") for i in range(2)]
    s_pl = [sem(f"probs_T_parts_done_{i}") for i in range(2)]
    s_o, s_oc = sem("heads_done"), sem("heads_copied")
    s_pr, s_pi, s_ps = sem("prob_reciprocal_done"), sem("prob_scale_done"), sem("prob_scale_spread_done")
    s_os, s_oh, s_ol = sem("heads_scaled"), sem("heads_high_done"), sem("heads_parts_done")
    s_pad, s_sg = sem("padding_set"), sem("gate_done")
    s_tap, s_ls, s_lsq, s_lsm = sem("conv_step"), sem("ln_sum_step"), sem("ln_square_done"), sem("ln_scale_step")
    s_lsg, s_lv, s_lh, s_ll = sem("ln_sigmoid_done"), sem("ln_silu_done"), sem("conf_high_done"), sem("conf_parts_done")
    s_cg, s_bx, s_sct, s_sch, s_scl = (sem("cg_copied"), sem("sc_padded_done"), sem("sc_conv_step"), sem("sc_high_done"),
                                       sem("sc_parts_done"))
    s_mg, s_mh = sem("merged_added"), sem("merged_high_done")
    s_uh, s_u = sem("hidden_high_done"), sem("hidden_parts_done")

    def f(ap):
        return ap.bitcast(F32)

    def read_out(eng, t, slot):
        eng.wait_ge(s_free[slot], t - slot + 2)

    def ada_tile(n):
        m = n + ADA_FIRST
        return (0, m) if isinstance(n, int) and m < MT else (1, m - MT)

    def ada_number(l, phase, q):
        return ADA_BASE[phase] + q if l == 0 and phase in ADA_BASE else None

    def phase_read_out(eng, t):
        for r in range(2):
            eng.wait_ge(s_free[r], t)

    def lagging(p, lag):
        n = 0 if p - lag == 0 else p - lag - 1
        return n if p - lag == 0 or 1 <= n <= 4 else None

    batch_base = [sum(len(batches(x)) for x in range(l)) for l in range(DEPTH)]
    step_base = [sum(len(steps(x)) for x in range(l)) for l in range(DEPTH)]
    up_base = {}
    n = 0
    for l in range(DEPTH):
        for p, w in enumerate(PARTS):
            up_base[l, p] = n
            n += w

    with nc.Block() as block:
        @block.sync
        def _(sp):
            dma = sp.dma_start
            dma(ident[:, :], A["ident"]).then_inc(s_const, 16)
            dma(swap[:, :], A["swap"]).then_inc(s_const, 16)
            dma(heads[:, :], A["heads"]).then_inc(s_const, 16)

            def rows(block, r, ap):
                dma(stage[r:r + ap.shape[0], block, 0:ap.shape[1]], ap).then_inc(s_par, 16)
            rows(1, R_C, A["c"][0].rearrange("(r p) -> r p", p=128))
            rows(1, R_C + KD, A["c_ctx"].rearrange("(r p) -> r p", p=128))
            for r, name in ((R_CB, "conf_dw_b"), (R_LG, "conf_ln_g"), (R_LB, "conf_ln_b")):
                rows(1, r, A[name].rearrange("l (r p) -> (l r) p", p=128))
            rows(1, R_SC, A["sc_dw_w"].rearrange("l j (r p) -> (l j r) p", p=128))
            for half in range(2):
                for r, name in ((R_QN, "q_norm"), (R_KN, "k_norm")):
                    dma(stage[r:r + DEPTH, 1, 64 * half:64 * half + 64], A[name]).then_inc(s_par, 16)
            rows(0, 0, A["b_ada"].rearrange("l (r p) -> (l r) p", p=128))
            for l in range(DEPTH):
                rows(2 + l, 0, A["conf_dw_w"][l].rearrange("j (r p) -> (j r) p", p=128))

            def unit(u, slot, halves, turn=None):
                ahead = u - 1 if not (isinstance(u, int) and u < 2) else None
                if ahead is not None:
                    sp.wait_ge(s_lo, ahead)
                for dst, src in halves:
                    dma(dst, src).then_inc(s_w[slot], 16)

            def cols(slot, view, c0):
                nk = view.shape[1]
                r = raw[:, slot, 0:nk * 128].rearrange("p (k n) -> p k n", n=128)
                return [(r[q:q + 64], view[q:q + 64, :, bass.ds(c0, 128)]) for q in (0, 64)]

            for l in range(DEPTH):
                wi = A["w_in"][l].rearrange("(k p) n -> p k n", p=128)
                u = plan.unit[l, "qkv"]
                unit(u, 0, cols(0, wi, OFF_K))
                unit(u + 1, 1, cols(1, wi, OFF_V))
                sp.wait_ge(s_tile, plan.tile[l, "qkv"])
                for half in range(2):
                    dma(rope[:, half, :], A["rope"][half]).then_inc(s_rope, 16)
                for i in range(4):
                    r = raw[:, i % 2, :].rearrange("p (k n) -> p k n", n=128)
                    unit(u + 2 + i, i % 2, [(r[:, :, 64 * g:64 * g + 64], wi[:, :, 64 * (4 * g + i):64 * (4 * g + i) + 64])
                                            for g in range(2)])

                u = plan.unit[l, "conf"]

                def conf(i):
                    unit(u + 2 * i, 0, cols(0, wi, 128 * i + OFF_CONF + CW))
                    unit(u + 2 * i + 1, 1, cols(1, wi, 128 * i + OFF_CONF))
                loop(sp, KC, conf)

                for b in (0, "sc", 2, 1):
                    if b == "sc":
                        u_sc = plan.unit[l, "sc"]

                        def sc(i):
                            for r in range(2):
                                for n, c in enumerate((1, 2, 0)):
                                    q = 3 * r + n
                                    unit(u_sc + 6 * i + q, q % 2, cols(q % 2, wi, 256 * i + 128 * r + OFF_SC + c * CW))
                        loop(sp, KC // 2, sc)
                        continue
                    u_b = plan.unit[l, ("branch", b)]
                    wo = A[("w_attn_o", "w_conf_out", "w_sc_out")[b]][l]

                    def branch(i, b=b, u_b=u_b, wo=wo):
                        for r in range(2):
                            q = 3 * r
                            for n in range(2):
                                unit(u_b + 6 * i + q + n, (q + n) % 2,
                                     cols((q + n) % 2, wi, 512 * i + 256 * r + 128 * n + OFF_GATE + b * D))
                            slot = (q + 2) % 2
                            rw = raw[:, slot, :].rearrange("p (k n) -> p k n", n=256)
                            v = (wo.rearrange("(g k p) n -> g p k n", g=2, p=64) if b == 0
                                 else wo.rearrange("(k g p) n -> g p k n", g=2, p=64))
                            unit(u_b + 6 * i + q + 2, slot,
                                 [(rw[64 * g:64 * g + 64], v[g, :, :, bass.ds(512 * i + 256 * r, 256)]) for g in range(2)])
                    loop(sp, 2, branch)

                wm = A["w_mix_out"][l].rearrange("(k p) n -> p k n", p=128)
                u_m = plan.unit[l, "mix"]

                def mix(i):
                    for r in range(2):
                        unit(u_m + 2 * i + r, r, cols(r, wm, 256 * i + 128 * r))
                loop(sp, KD // 2, mix)
                wf = A["w_ffn_in"][l].rearrange("(k p) n -> p k n", p=128)
                f0 = 0
                for p, n in enumerate(PARTS):
                    u_u, u_d = plan.unit[l, ("up", p)], plan.unit[l, ("down", p)]

                    def up(i, u_u=u_u, f0=f0):
                        for r in range(2):
                            unit(u_u + 2 * i + r, r, cols(r, wf, 128 * i + 128 * f0 + r * FFN))
                    loop(sp, n, up)
                    wd = A["w_ffn_out"][l][128 * f0:128 * (f0 + n), :].rearrange("(k p) n -> p k n", p=128)

                    def down(i, u_d=u_d, wd=wd):
                        for r in range(2):
                            unit(u_d + 2 * i + r, r, cols(r, wd, 256 * i + 128 * r))
                    loop(sp, KD // 2, down)
                    f0 += n
            for r in range(2):
                sp.wait_ge(s_free[r], plan.tile["store"] + KD)
            dma(out[0].rearrange("(t p) n -> p t n", p=128), xout[:, :, :]).then_inc(s_out, 16)
            sp.wait_ge(s_out, 16)

        @block.tensor
        def _(pe):
            def mm(o_, a, b, start=True, stop=True):
                return nc.tensor.matmul(o_, a, b, start=start, stop=stop)

            def done(ins):
                ins.then_inc(s_tile, 1)

            def take_slot(t, slot):
                if not (isinstance(t, int) and t < 2):
                    pe.wait_ge(s_free[slot], t - slot)

            def three(dst, a, b, first, last):
                mm(dst, a(0), b(0), first, False)
                mm(dst, a(0), b(1), False, False)
                return mm(dst, a(1), b(0), False, last)

            def product(slot, wslot, ks, rhs, width, before_k=None, cut=0, wn=128):
                segs = [(0, 512)] + ([(512, width)] if width > 512 else [])
                for k in range(ks):
                    if before_k:
                        before_k(k)
                    for pw, px in ((0, 0), (0, 1), (1, 0)):
                        w = WHL[:, wslot, pw, k * wn + cut:k * wn + cut + 128]
                        for a, b in segs:
                            ins = mm(G[:, slot, a:b], w, rhs(px, k, a, b),
                                     k == 0 and (pw, px) == (0, 0), k == ks - 1 and pw == 1)
                return ins

            def from_h(part, k, a, b):
                return H[:, part, k, a:b]

            pe.wait_ge(s_const, 48)
            pe.wait_ge(s_par, 16 * (11 + DEPTH))
            nc.tensor.transpose(O[:, 0, 0:DEPTH * MT], stage[0:DEPTH * MT, 0, :], ident[0:DEPTH * MT, 0:DEPTH * MT])
            nc.tensor.transpose(O[:, 0, 128:128 + PAR_ROWS], stage[0:PAR_ROWS, 1, :], ident[0:PAR_ROWS, 0:PAR_ROWS])\
                .then_inc(s_part, 1)
            for l in range(DEPTH):
                ins = nc.tensor.transpose(O[:, 1, 128 * l:128 * l + CONV_ROWS],
                                          stage[0:CONV_ROWS, 2 + l, :], ident[0:CONV_ROWS, 0:CONV_ROWS])
            ins.then_inc(s_part, 1)
            pe.wait_ge(s_csil, 1)
            for m in range(ADA_FIRST):
                j = m // 2
                if m % 2 == 0:
                    pe.wait_ge(s_ada[j % 6], 16 * (j // 6 + 1))
                for k in range(KD):
                    ins = mm(O[:, 1, 2 * m:2 * m + 2], ada[:, j % 6, k, 128 * (m % 2):128 * (m % 2) + 128],
                             csil[:, k, :], k == 0, k == KD - 1)
                ins.then_inc(s_adt, 1)
            pe.wait_ge(s_in, 32)
            for i in range(KD):
                take_slot(i, i % 2)
                for t in range(T // 128):
                    ins = nc.tensor.transpose(G[:, i % 2, 128 * t:128 * t + 128],
                                              xin[:, t, 128 * i:128 * i + 128], ident[:, :])
                done(ins)

            stats, spreads, squared, normed = [0], [0], [0], [0]

            def statistic(src, width, rhs, n=1, off=lambda c: c):
                k = stats[0]
                if k:
                    pe.wait_ge(s_sd, k)
                for t in range(width // 128):
                    c = off(128 * t)
                    b = 16 * (k % 2) + n * t
                    ins = mm(O[:, 0, b:b + n], src[:, c:c + 128], rhs)
                ins.then_inc(s_stat, 1)
                stats[0] += 1

            def spread(width, n=1):
                k = spreads[0]
                pe.wait_ge(s_inv, k + 1)
                for t in range(width // 128):
                    if n == 1:
                        ins = mm(M[:, 128 * t:128 * t + 128], rs[:, k % 2, t:t + 1].to_broadcast([128, 128]), ident[:, :])
                    else:
                        ins = nc.tensor.transpose(M[:, 128 * t:128 * t + 128],
                                                  qspread[:, t].rearrange("p h d -> p (h d)"), ident[:, :])
                ins.then_inc(s_spread, 1)
                spreads[0] += 1

            def modulation(n):
                if n is None:
                    return
                pe.wait_ge(s_adw, 16 * n + 16)
                pe.wait_ge(*((s_mod, 2) if isinstance(n, int) and n == 0 else (s_mt, n)))
                for k in range(KD):
                    ins = mm(O[:, 1, 0:2], adaw[:, k, :], csil[:, k, :], k == 0, k == KD - 1)
                ins.then_inc(s_adt, 1)

            def norm(width):
                squared[0] += KD - 1
                pe.wait_ge(s_ssq, squared[0])
                statistic(SSQ, width, ones[:, :])
                spread(width)

            def h_ready(k):
                pe.wait_ge(s_h, normed[0] + k + 1)

            pe.wait_ge(s_set, 2)
            for l in range(DEPTH):
                W = WIDTH[l]
                norm(T)

                def qk_steps(p):
                    n = lagging(p, 1)
                    if n is not None:
                        pe.wait_ge(s_qsq, 5 * l + n + 1)
                        statistic(qsq, T if n == 0 else W, heads[:, :], n=2)
                    n = lagging(p, 2)
                    if n is not None:
                        if n == 0:
                            pe.wait_ge(s_h, normed[0])
                        else:
                            pe.wait_ge(s_qn, 5 * l + n)
                        spread(T if n == 0 else W, n=2)
                    n = lagging(p, 3)
                    if n is not None:
                        pe.wait_ge(s_qn, 5 * l + n + 1)
                        if n:
                            pe.wait_ge(s_qr, 3 * (5 * l + n))
                        mm(O[:, 1, 0:S], swap[:, :], qraw[:, n % 4, 0:S]).then_inc(s_rot, 1)

                u, t = plan.unit[l, "qkv"], plan.tile[l, "qkv"]
                for i in range(6):
                    pe.wait_ge(s_lo, u + i + 1)
                    take_slot(t + i, i % 2)
                    if i == 1:
                        for tt in range(T // 128):
                            c = slice(128 * tt, 128 * tt + 128)
                            for k in range(KD):
                                ins = three(G[:, 1, c], lambda part: H[:, part, k, c],
                                            lambda part: WHL[:, 1, part, 128 * k:128 * k + 128], k == 0, k == KD - 1)
                    else:
                        ins = product(i % 2, i % 2, KD, from_h, T if i == 0 else W, h_ready if i == 0 else None)
                    done(ins)
                    if i == 0:
                        normed[0] += KD
                    qk_steps(i)

                u, t = plan.unit[l, "conf"], plan.tile[l, "conf"]
                for i in range(2 * KC):
                    pe.wait_ge(s_lo, u + i + 1)
                    take_slot(t + i, i % 2)
                    done(product(i % 2, i % 2, KD, from_h, W))
                    qk_steps(6 + i)

                t, st_ = plan.tile[l, "att"], steps(l)
                s0 = step_base[l]

                bt = batches(l)
                b0 = batch_base[l]
                ends = [sum(NKV * b[2] // 128 for b in bt[:n + 1]) for n in range(len(bt))]

                def scores(i):
                    g, tile, q0, k0, nk, c = st_[i]
                    r = slice(64 * g, 64 * g + 64)
                    take_slot(t + i, i % 2)
                    for a, b in ([(0, 512), (512, 768)] if nk == T else [(512, 768)]):
                        ins = three(G[:, i % 2, a:b], lambda part: Q[r, part, tile, q0:q0 + 128],
                                    lambda part: K[r, part, a:b], True, True)
                    done(ins)

                def turn(i):
                    g, tile, q0, k0, nk, c = st_[i]
                    read_out(pe, t + i, i % 2)
                    for half, kts in ((0, range(4)), (1, range(4, T // 128))):
                        if k0 > 128 * kts[0]:
                            continue
                        if half == 0:
                            pe.wait_ge(s_pl[0], S // 128 * NH * l + i)
                            if spread_[0]:
                                pe.wait_ge(s_os, spread_[0])
                        else:
                            pe.wait_ge(s_pl[1], s0 + i)
                        for kt in kts:
                            cols_ = slice(128 * kt, 128 * kt + 128)
                            ins = nc.tensor.transpose(M[:, cols_], P[:, i % 2, cols_], ident[:, :])
                        ins.then_inc(s_pt[half], 1)

                def values(j):
                    g, tile, q0, k0, nk, c = st_[2 * j]
                    pe.wait_ge(s_pl[1], s0 + 2 * j + 2)
                    if s0 // 2 + j >= 2:
                        pe.wait_ge(s_oc, s0 // 2 + j - 1)
                    kts = range(k0 // 128, (k0 + nk) // 128)
                    for kt in kts:
                        ins = three(O[:, j % 2, 0:256], lambda part: V[:, part, kt, :],
                                    lambda part: PT[:, j % 2, part, kt, :], kt == kts[0], kt == kts[-1])
                    ins.then_inc(s_o, 1)

                def spread_scales(n):
                    pe.wait_ge(s_pi, b0 + n + 1)
                    pe.wait_ge(s_pl[0], S // 128 * NH * l + min(ends[n] + 2, S // 128 * NH))
                    if b0 + n:
                        pe.wait_ge(s_os, b0 + n)
                    for j in range(bt[n][2] // 128):
                        ins = nc.tensor.transpose(M[:, 128 * j:128 * j + 128],
                                                  pspread[:, 2 * j:2 * j + 2].rearrange("p h d -> p (h d)"), ident[:, :])
                    ins.then_inc(s_ps, 1)
                    spread_[0] = b0 + n + 1
                spread_ = [0]
                pe.wait_ge(s_q, 5 * (l + 1))
                read_out(pe, plan.tile[l, "qkv"] + 1, 1)
                scores(0)
                for i in range(len(st_) + 3):
                    if i + 1 < len(st_):
                        scores(i + 1)
                    if i % 2 == 0 and 2 <= i <= len(st_):
                        values(i // 2 - 1)
                    if i - 2 in ends:
                        spread_scales(ends.index(i - 2))
                    if i < len(st_):
                        turn(i)
                pe.wait_ge(s_oc, (s0 + len(st_)) // 2)

                def branch(b, i):
                    u, t = plan.unit[l, ("branch", b)] + 3 * i, plan.tile[l, ("branch", b)] + 4 * i
                    Y = (Q, CF, SCO)[b]
                    for n in range(2):
                        pe.wait_ge(s_lo, u + n + 1)
                        take_slot(t + n, n)
                        done(product(n, (i + n) % 2, KD, from_h, W))
                        modulation(ada_number(l, ("branch", b), 3 * i + n))
                    pe.wait_ge(s_lo, u + 3)
                    if i == 0:
                        pe.wait_ge(*((s_ol, b0 + len(bt)), (s_ll, KC * (l + 1)), (s_scl, KC * (l + 1)))[b])
                    for n in range(2):
                        take_slot(t + 2 + n, n)
                        done(product(n, i % 2, KC, lambda part, k, a, b_: Y[:, part, k, a:b_], W, cut=128 * n, wn=256))
                    modulation(ada_number(l, ("branch", b), 3 * i + 2))
                for i in range(4):
                    branch(0, i)

                u, t = plan.unit[l, "sc"], plan.tile[l, "sc"]

                def sc(i, u=u, t=t):
                    for q in range(2):
                        pe.wait_ge(s_lo, u + 2 * i + q + 1)
                        take_slot(t + 2 * i + q, q)
                        done(product(q, q, KD, from_h, W))
                        modulation(ada_number(l, "sc", 2 * i + q))
                loop(pe, 6, sc)

                for i in range(4):
                    if i == 2:
                        pe.wait_ge(s_ls, 6 * l + 3)
                        statistic(ln_sum, W, ones[:, :], off=ctok)
                        spread(W)
                    branch(2, i)
                pe.wait_ge(s_ls, 6 * l + 6)
                statistic(ln_sum, W, ones[:, :], off=ctok)
                pe.wait_ge(s_lsm, KC * (2 * l + 1))
                spread(W)
                for i in range(4):
                    branch(1, i)

                def pairs(phase, n, ks, rhs, ready):
                    u, t = plan.unit[l, phase], plan.tile[l, phase]

                    def turn_(i, first=False):
                        for r in range(2):
                            pe.wait_ge(s_lo, u + 2 * i + r + 1)
                            take_slot(t + 2 * i + r, r)
                            done(product(r, r, ks, rhs, W, ready if first and r == 0 else None))
                            modulation(ada_number(l, phase, 2 * i + r))
                    if ready:
                        turn_(0, True)
                        loop(pe, n - 1, lambda i: turn_(i + 1))
                    else:
                        loop(pe, n, turn_)
                pairs("mix", KD // 2, KD, from_h, h_ready)
                normed[0] += KD
                norm(W)
                for p, n in enumerate(PARTS):
                    pairs(("up", p), n, KD, from_h, None if p else h_ready)
                    u0 = PARTS[0] * (p % 2)
                    pairs(("down", p), KD // 2, n, lambda part, k, a, b: U[:, u0 + k, part, a:b],
                          lambda k: pe.wait_ge(s_u, up_base[l, p] + k + 1))
                normed[0] += KD

            t = plan.tile["store"]
            phase_read_out(pe, t)
            for i in range(KD):
                take_slot(t + i, i % 2)
                for tt in range(S // 128):
                    ins = nc.tensor.transpose(G[:, i % 2, 128 * tt:128 * tt + 128], X[:, i, 128 * tt:128 * tt + 128],
                                              ident[:, :])
                done(ins)

        @block.gpsimd
        def _(pool):
            nc.gpsimd.memset(ones[:, :], 1.0).then_inc(s_set, 1)
            nc.gpsimd.memset(eps[:, :], EPS).then_inc(s_set, 1)

            def rest(u, slot):
                pool.wait_ge(s_hi, u + 1)
                nc.gpsimd.tensor_tensor(WHL[:, slot, 1, :], raw[:, slot, :], f(WHL[:, slot, 0, :]),
                                        ALU.subtract).then_inc(s_lo, 1)

            def rests(phase, n):
                u = plan.unit[l, phase] + 2

                def turn(i):
                    for r in range(2):
                        rest(u + 2 * i + r, r)
                loop(pool, n, turn)

            for r in range(2):
                rest(r, r)
            for l in range(DEPTH):
                W = WIDTH[l]
                if l:
                    pool.wait_ge(s_tile, plan.tile[l, "qkv"])
                for a, b in ((0, PAD), (PAD + S, PAD + S + GAP), (PAD + S + GAP + LC, T + 2 * GAP)):
                    nc.gpsimd.memset(hpad[:, :, a:b], 0.0).then_inc(s_pad, 1)
                rests("qkv", 3)
                rests("conf", KC)
                for b in (0, "sc", 2, 1):
                    if b == "sc":
                        pool.wait_ge(s_tile, plan.tile[l, "sc"])
                        for a in (0, S + 1, S + 2, T + 3):
                            nc.gpsimd.memset(bx[:, a:a + 1], 0.0).then_inc(s_pad, 1)
                        rests("sc", 6)
                        continue
                    u, t = plan.unit[l, ("branch", b)] + 2, plan.tile[l, ("branch", b)]
                    for i in range(4):
                        for n in range(3):
                            rest(u + 3 * i + n, (i + n) % 2)
                        if b:
                            for n in range(2):
                                read_out(pool, t + 4 * i + 2 + n, n)
                                if b == 1:
                                    pool.wait_ge(s_mg, 16 * l + 2 * i + n + 1)
                                m = merged[:, 2 * i + n, 0:W]
                                nc.gpsimd.tensor_tensor(m, m, ybuf[:, n, 0:W], ALU.add).then_inc(s_mg, 1)
                rests("mix", KD // 2)
                for p, n in enumerate(PARTS):
                    rests(("up", p), n)
                    rests(("down", p), KD // 2 - (l == DEPTH - 1 and p == len(PARTS) - 1))

        @block.scalar
        def _(act):
            def high(u, slot):
                act.wait_ge(s_w[slot], 16 * (u - slot) + 32)
                nc.scalar.activation(WHL[:, slot, 0, :], raw[:, slot, :], ACT.Copy).then_inc(s_hi, 1)

            def tile_and_high(t, u, slot):
                act.wait_ge(s_tile, t + 1)
                high(u + 2, slot)

            def free(ins, slot):
                ins.then_inc(s_free[slot], 2)

            stats, squares, hh = [0], [0], [0]

            def deviation(n, func, scale):
                k = stats[0]
                act.wait_ge(s_stat, k + 1)
                if k >= 2:
                    act.wait_ge(s_inv, k - 1)
                src = O[:, 0, 16 * (k % 2):16 * (k % 2) + n]
                if func == ACT.Sqrt:
                    ins = nc.scalar.activation(sd[:, k % 2, 0:n], src, func, bias=eps[:, :], scale=scale)
                else:
                    ins = nc.scalar.activation(sd[:, k % 2, 0:n], src, func, scale=scale)
                ins.then_inc(s_sd, 1)
                stats[0] += 1

            def square(i, r, t, width):
                read_out(act, t, r)
                if isinstance(i, int) and i < 3:
                    if i == 0:
                        nc.scalar.activation(SSQ[:, 0:width], X[:, 0, 0:width], ACT.Square).then_inc(s_sq, 1)
                        return
                else:
                    act.wait_ge(s_ssq, squares[0] + i - 2)
                src = X[:, bass.ds(i, 1), 0:width].rearrange("p a n -> p (a n)")
                nc.scalar.activation(SQ[:, r, 0:width], src, ACT.Square).then_inc(s_sq, 1)

            def h_high(shift, segs):
                for i in range(KD):
                    act.wait_ge(s_ht, hh[0] + i + 1)
                    for a, n, v in segs:
                        ins = nc.scalar.activation(H[:, 0, i, a:a + n], HT[:, i % 2, a:a + n], ACT.Identity,
                                                   bias=mods[:, l, shift * KD + i, v:v + 1])
                    ins.then_inc(s_hh, 1)
                hh[0] += KD

            def ada_load(n):
                la, m = ada_tile(n)
                src = A["w_ada"][la].rearrange("(k p) n -> p k n", p=128)[:, :, bass.ds(m * 128, 128)]
                act.dma_start(adaw[:, :, :], src).then_inc(s_adw, 16)

            def modulation(n, more=True):
                if n is None:
                    return
                act.wait_ge(s_adt, ADA_FIRST + 1 + n)
                la, m = ada_tile(n)
                dst = mods[:, la, bass.ds(m, 1), :].rearrange("p a v -> p (a v)")
                nc.scalar.activation(dst, O[:, 1, 0:2], ACT.Identity, bias=bada[:, la, bass.ds(m, 1)]).then_inc(s_mt, 1)
                if more:
                    ada_load(n + 1)

            act.dma_start(xin[:, 0:4, :], A["x"][0].rearrange("(t p) n -> p t n", p=128)).then_inc(s_in, 16)
            act.dma_start(xin[:, 4:6, :], A["ctx"][0].rearrange("(t p) n -> p t n", p=128)).then_inc(s_in, 16)
            w0 = A["w_ada"][0].rearrange("(k p) n -> p k n", p=128)
            for j in range(ADA_FIRST // 2):
                if j == 6:
                    act.wait_ge(s_parc, 1)
                    nc.scalar.activation(sgc[:, :, :], par[:, R_C:R_C + 2 * KD].rearrange("p (v k) -> p v k", v=2),
                                         ACT.Sigmoid).then_inc(s_sgc, 1)
                if j >= 6:
                    act.wait_ge(s_adt, 2 * (j - 5))
                act.dma_start(ada[:, j % 6], w0[:, :, 256 * j:256 * j + 256]).then_inc(s_ada[j % 6], 16)
            ada_load(0)
            for r in range(2):
                high(r, r)
            act.wait_ge(s_set, 2)
            for i in range(KD):
                square(i, i % 2, i, T)
            squares[0] += KD - 1
            for l in range(DEPTH):
                W, segs = WIDTH[l], SEGS[l]
                deviation(T // 128, ACT.Sqrt, 1.0 / D)
                act.wait_ge(*((s_mt, DEPTH * MT - ADA_FIRST) if l else (s_mod, 2)))
                h_high(0, SEGS[0])

                def qk_steps(p):
                    n = lagging(p, 1)
                    if n is not None:
                        deviation(2 * (T if n == 0 else W) // 128, ACT.Sqrt, 1.0 / HD)
                    n = lagging(p, 4)
                    if n is not None:
                        w = T if n == 0 else W
                        act.wait_ge(s_qr, 3 * (5 * l + n + 1))
                        dst = K[:, 0, 0:w] if n == 0 else Q[:, 0, n - 1, 0:w]
                        nc.scalar.activation(dst, qraw[:, n % 4, 0:w], ACT.Copy).then_inc(s_qh, 1)

                u, t = plan.unit[l, "qkv"], plan.tile[l, "qkv"]
                for i in range(6):
                    tile_and_high(t + i, u + i, i % 2)
                    g = G[:, i % 2]
                    if i == 1:
                        nc.scalar.activation(V[:, 0].rearrange("p t n -> p (t n)"), g[:, 0:T], ACT.Copy).then_inc(s_vh, 1)
                    else:
                        n = max(i - 1, 0)
                        w = T if n == 0 else W
                        if n == 4:
                            act.wait_ge(s_q, 5 * l + 1)
                        if n:
                            act.wait_ge(s_stat, stats[0] + (n > 1))
                        nc.scalar.activation(qsq[:, 0:w], g[:, 0:w], ACT.Square).then_inc(s_qsq, 1)
                        free(nc.scalar.activation(qraw[:, n % 4, 0:w], g[:, 0:w], ACT.Copy), i % 2)
                    qk_steps(i)

                u, t = plan.unit[l, "conf"], plan.tile[l, "conf"]
                for i in range(2 * KC):
                    tile_and_high(t + i, u + i, i % 2)
                    if i % 2 == 0:
                        if i:
                            read_out(act, t + i - 1, 1)
                        free(nc.scalar.activation(GS[:, 0, 0:W], G[:, 0, 0:W], ACT.Sigmoid), 0)
                    qk_steps(6 + i)

                st_, s0, t = steps(l), step_base[l], plan.tile[l, "att"]

                bt, b0 = batches(l), batch_base[l]
                ends = [sum(NKV * b[2] // 128 for b in bt[:n + 1]) for n in range(len(bt))]

                def probs(i):
                    g, tile, q0, k0, nk, c = st_[i]
                    act.wait_ge(s_nm, s0 + i + 1)
                    if i >= 2:
                        act.wait_ge(s_pt[1], s0 + i - 1)
                    free(nc.scalar.activation(P[:, i % 2, k0:k0 + nk], G[:, i % 2, k0:k0 + nk], ACT.Exp,
                                              bias=nmax[:, i % 4:i % 4 + 1], accum_out=psums[:, c:c + 1]), i % 2)

                def turned(i):
                    g, tile, q0, k0, nk, c = st_[i]
                    j = i // 2
                    if j >= 2:
                        act.wait_ge(s_o, s0 // 2 + j - 1)
                    for half, (a, b) in enumerate(((0, 4), (4, T // 128))):
                        if k0 > 128 * a:
                            continue
                        act.wait_ge(s_pt[half], (s0 if half else S // 128 * NH * l) + i + 1)
                        nc.scalar.activation(PT[:, j % 2, 0, a:b, 128 * (i % 2):128 * (i % 2) + 128],
                                             M[:, 128 * a:128 * b].rearrange("p (k n) -> p k n", n=128), ACT.Copy)\
                            .then_inc(s_ph[half], 1)

                def outs(j):
                    g, tile, q0, k0, nk, c = st_[2 * j]
                    r = slice(64 * g, 64 * g + 64)
                    act.wait_ge(s_o, s0 // 2 + j + 1)
                    nc.scalar.activation(heads_raw[r, tile, q0:q0 + 256], O[r, j % 2, 0:256], ACT.Copy).then_inc(s_oc, 1)

                def batch_high(n):
                    i, q0, nq = bt[n][:3]
                    act.wait_ge(s_os, b0 + n + 1)
                    nc.scalar.activation(Q[:, 0, i, q0:q0 + nq], heads_raw[:, i, q0:q0 + nq], ACT.Copy).then_inc(s_oh, 1)
                probs(0)
                for i in range(len(st_) + 5):
                    if i + 1 < len(st_):
                        probs(i + 1)
                    if i % 2 == 0 and 2 <= i <= len(st_):
                        outs(i // 2 - 1)
                    if i - 4 in ends:
                        batch_high(ends.index(i - 4))
                    if i < len(st_):
                        turned(i)

                def branch(b, i, middle=None):
                    u, t = plan.unit[l, ("branch", b)] + 3 * i, plan.tile[l, ("branch", b)] + 4 * i
                    for n in range(2):
                        tile_and_high(t + n, u + n, (i + n) % 2)
                        if i:
                            read_out(act, t - 2 + n, n)
                        free(nc.scalar.activation(GS[:, n, 0:W], G[:, n, 0:W], ACT.Sigmoid), n)
                        modulation(ada_number(l, ("branch", b), 3 * i + n))
                    tile_and_high(t + 3, u + 2, i % 2)
                    modulation(ada_number(l, ("branch", b), 3 * i + 2))
                for i in range(4):
                    branch(0, i)

                u, t = plan.unit[l, "sc"], plan.tile[l, "sc"]
                phase_read_out(act, t)
                for i in range(KC):
                    a = 3 * i
                    tile_and_high(t + a, u + a, a % 2)
                    if i:
                        read_out(act, t + a - 2, a % 2)
                    free(nc.scalar.activation(GS[:, 0, 0:W], G[:, a % 2, 0:W], ACT.Copy), a % 2)
                    modulation(ada_number(l, "sc", a))
                    tile_and_high(t + a + 1, u + a + 1, (a + 1) % 2)
                    modulation(ada_number(l, "sc", a + 1))
                    tile_and_high(t + a + 2, u + a + 2, a % 2)
                    read_out(act, t + a + 2, a % 2)
                    nc.scalar.activation(SCO[:, 0, i, 0:W], GS[:, 1, 0:W], ACT.Copy).then_inc(s_sch, 1)
                    modulation(ada_number(l, "sc", a + 2))
                act.wait_ge(s_scl, KC * (l + 1))

                Wc = CONV_W[l]
                for i in range(4):
                    branch(2, i)
                    if i == 1:
                        deviation(W // 128, ACT.Copy, 1.0 / CW)
                    if i == 2:
                        for n in range(KC):
                            act.wait_ge(s_lsm, KC * 2 * l + n + 1)
                            if n == 3:
                                act.wait_ge(s_ls, 6 * l + 4)
                            nc.scalar.activation(ln_sum[:, 0:Wc] if n == 0 else ln_sq[:, n % 2, 0:Wc], acc[:, n, 0:Wc],
                                                 ACT.Square).then_inc(s_lsq, 1)
                deviation(W // 128, ACT.Sqrt, 1.0 / CW)
                for n in range(KC):
                    act.wait_ge(s_lsm, KC * (2 * l + 1) + n + 1)
                    if n >= 2:
                        act.wait_ge(s_lv, KC * l + n - 1)
                    nc.scalar.activation(sig[:, n % 2, 0:Wc], acc[:, n, 0:Wc], ACT.Sigmoid,
                                         bias=par[:, R_LB + KC * l + n:R_LB + KC * l + n + 1]).then_inc(s_lsg, 1)
                act.wait_ge(s_lv, KC * (l + 1))
                for n in range(KC):
                    for a, w, v in segs:
                        ins = nc.scalar.activation(CF[:, 0, n, a:a + w], acc[:, n, ctok(a):ctok(a) + w], ACT.Copy)
                    ins.then_inc(s_lh, 1)
                for i in range(4):
                    branch(1, i)

                act.wait_ge(s_tile, plan.tile[l, ("branch", 1)] + 14)
                for i in range(KD):
                    act.wait_ge(s_mg, 16 * l + KD + i + 1)
                    nc.scalar.activation(H[:, 0, i, 0:W], merged[:, i, 0:W], ACT.Copy).then_inc(s_mh, 1)

                def x_tiles(phase, width, with_squares):
                    u, t = plan.unit[l, phase], plan.tile[l, phase]

                    def turn(i, more=True):
                        for r in range(2):
                            if more:
                                tile_and_high(t + 2 * i + r, u + 2 * i + r, r)
                            if with_squares:
                                square(2 * i + r, r, t + 2 * i + r, width)
                            modulation(ada_number(l, phase, 2 * i + r))
                    turn(0)
                    loop(act, KD // 2 - 2, lambda i: turn(i + 1))
                    turn(KD // 2 - 1, u + KD < plan.units)
                    if with_squares:
                        squares[0] += KD - 1
                x_tiles("mix", W, True)
                deviation(W // 128, ACT.Sqrt, 1.0 / D)
                h_high(3, segs)

                for p, n in enumerate(PARTS):
                    u, t = plan.unit[l, ("up", p)], plan.tile[l, ("up", p)]

                    def up(i, u=u, t=t, p=p, first=False, last=False):
                        tile_and_high(t + 2 * i, u + 2 * i, 0)
                        if not first:
                            act.wait_ge(s_u, up_base[l, p] + i)
                        free(nc.scalar.activation(GS[:, 0, 0:W], G[:, 0, 0:W], ACT.Silu), 0)
                        modulation(ada_number(l, ("up", p), 2 * i))
                        tile_and_high(t + 2 * i + 1, u + 2 * i + 1, 1)
                        read_out(act, t + 2 * i + 1, 1)
                        dst = U[:, bass.ds(i + PARTS[0] * (p % 2), 1), 0, 0:W].rearrange("p a n -> p (a n)")
                        nc.scalar.activation(dst, GS[:, 0, 0:W], ACT.Copy).then_inc(s_uh, 1)
                        modulation(ada_number(l, ("up", p), 2 * i + 1), not last)
                    up(0, first=up_base[l, p] == 0)
                    loop(act, n - 2, lambda i: up(i + 1))
                    up(n - 1, last=("up", p) == ADA_PHASES[-1])
                    x_tiles(("down", p), W, p == len(PARTS) - 1 and l < DEPTH - 1)

            t = plan.tile["store"]
            for i in range(KD):
                act.wait_ge(s_tile, t + i + 1)
                free(nc.scalar.activation(xout[:, :, 128 * i:128 * i + 128],
                                          G[:, i % 2, 0:S].rearrange("p (t n) -> p t n", n=128), ACT.Copy), i % 2)

        @block.vector
        def _(dve):
            V_ = nc.vector

            def stt(o_, a, s, b, op0, op1):
                return V_.scalar_tensor_tensor(o_, a, s, b, op0, op1)

            def free(ins, slot):
                ins.then_inc(s_free[slot], 2)

            dve.wait_ge(s_part, 1)
            V_.tensor_copy(bada[:, :, :].rearrange("p l m -> p (l m)"), O[:, 0, 0:DEPTH * MT])
            V_.tensor_copy(par[:, :], O[:, 0, 128:128 + PAR_ROWS]).then_inc(s_parc, 1)
            dve.wait_ge(s_part, 2)
            V_.tensor_copy(cw[:, :, :], O[:, 1, 0:128 * DEPTH].rearrange("p (l c) -> p l c", c=128)[:, :, 0:CONV_ROWS])\
                .then_inc(s_parc, 1)
            dve.wait_ge(s_parc, 2)
            for c in (1, 4):
                V_.tensor_scalar(bada[:, :, c * KD:(c + 1) * KD], bada[:, :, c * KD:(c + 1) * KD], 1.0, None, ALU.add)\
                    .then_inc(s_parc, 1)
            for l in range(DEPTH):
                V_.tensor_scalar(qg[:, l, 1:2], par[:, R_QN + l:R_QN + l + 1], HD ** -0.5, None, ALU.mult)
                V_.tensor_copy(qg[:, l, 0:1], par[:, R_KN + l:R_KN + l + 1]).then_inc(s_qg, 1)
            dve.wait_ge(s_sgc, 1)
            V_.tensor_tensor(csil[:, :, :].rearrange("p k v -> p v k"),
                             par[:, R_C:R_C + 2 * KD].rearrange("p (v k) -> p v k", v=2), sgc[:, :, :], ALU.mult)\
                .then_inc(s_csil, 1)

            for i in range(KD):
                dve.wait_ge(s_tile, i + 1)
                free(V_.tensor_copy(X[:, i, :], G[:, i % 2, 0:T]), i % 2)

            invs, squares, norms, split = [0], [0], [0], [0]

            def inverse(n, func="reciprocal"):
                k = invs[0]
                dve.wait_ge(s_sd, k + 1)
                if k >= 2:
                    dve.wait_ge(s_spread, k - 1)
                if func == "mean":
                    V_.tensor_copy(rs[:, k % 2, 0:n], sd[:, k % 2, 0:n]).then_inc(s_inv, 1)
                elif func == "heads":
                    V_.reciprocal(rs[:, k % 2, 0:n], sd[:, k % 2, 0:n]).then_inc(s_rc, 1)
                    dve.wait_ge(s_rc, heads_done[0] + 1)
                    dve.wait_ge(s_spread, k)
                    V_.tensor_copy(qspread[:, 0:n // 2].rearrange("p t h d -> p (t h) d"),
                                   rs[:, k % 2, 0:n].unsqueeze(2).to_broadcast([128, n, HD])).then_inc(s_inv, 1)
                    heads_done[0] += 1
                else:
                    V_.reciprocal(rs[:, k % 2, 0:n], sd[:, k % 2, 0:n]).then_inc(s_inv, 1)
                invs[0] += 1
            heads_done = [0]

            def add_square(i, r, width):
                if isinstance(i, int) and i == 0:
                    return
                dve.wait_ge(s_sq, squares[0] + i + 1)
                if not (isinstance(i, int) and i == 1):
                    dve.wait_ge(s_ssq, squares[0] // KD * (KD - 1) + i - 1)
                V_.tensor_tensor(SSQ[:, 0:width], SSQ[:, 0:width], SQ[:, r, 0:width], ALU.add).then_inc(s_ssq, 1)

            def norm(scale, shift, segs, width):
                dve.wait_ge(s_spread, invs[0])

                def scaled(i):
                    if i >= 2:
                        dve.wait_ge(s_h, split[0] + i - 1)
                    for a, n, v in segs:
                        ins = stt(HT[:, i % 2, a:a + n], X[:, i, a:a + n], mods[:, l, scale * KD + i, v:v + 1],
                                  M[:, a:a + n], ALU.mult, ALU.mult)
                    ins.then_inc(s_ht, 1)

                def rests(i):
                    dve.wait_ge(s_hh, norms[0] + i + 1)
                    for a, n, v in segs:
                        ins = stt(H[:, 1, i, a:a + n], HT[:, i % 2, a:a + n], mods[:, l, shift * KD + i, v:v + 1],
                                  f(H[:, 0, i, a:a + n]), ALU.add, ALU.subtract)
                    ins.then_inc(s_h, 1)
                scaled(0)
                for i in range(KD):
                    if i + 1 < KD:
                        scaled(i + 1)
                    rests(i)
                norms[0] += KD
                split[0] += KD

            def x_tiles(phase, gate, segs, with_squares):
                t = plan.tile[l, phase]
                phase_read_out(dve, t)

                def turn(i):
                    for r in range(2):
                        dve.wait_ge(s_tile, t + 2 * i + r + 1)
                        for a, n, v in segs:
                            x = X[:, bass.ds(2 * i + r, 1), a:a + n].rearrange("p a n -> p (a n)")
                            m = mods[:, l, bass.ds(2 * i + r + gate * KD, 1), v:v + 1].rearrange("p a n -> p (a n)")
                            ins = stt(x, G[:, r, a:a + n], m, x, ALU.mult, ALU.add)
                        free(ins, r)
                        if with_squares:
                            add_square(2 * i + r, r, WIDTH[l])
                turn(0)
                loop(dve, KD // 2 - 1, lambda i: turn(i + 1))
                if with_squares:
                    squares[0] += KD

            for i in range(KD):
                add_square(i, i % 2, T)
            squares[0] += KD

            for l in range(DEPTH):
                W, segs, Wc = WIDTH[l], SEGS[l], CONV_W[l]
                inverse(T // 128)
                if l == 0:
                    dve.wait_ge(s_adt, ADA_FIRST)
                    dve.wait_ge(s_parc, 4)
                    for v in range(2):
                        src = O[:, 1, 0:2 * ADA_FIRST].rearrange("p (m v) -> p m v", v=2)[:, :, v]
                        V_.tensor_tensor(mods[:, 0, 0:ADA_FIRST, v], src, bada[:, 0, 0:ADA_FIRST], ALU.add)\
                            .then_inc(s_mod, 1)
                    dve.wait_ge(s_mod, 2)
                else:
                    dve.wait_ge(s_mt, DEPTH * MT - ADA_FIRST)
                norm(1, 0, SEGS[0], T)

                dve.wait_ge(s_rope, 32 * (l + 1))
                dve.wait_ge(s_qg, DEPTH)

                def qk_steps(p):
                    n = lagging(p, 4)
                    if n is not None:
                        w = T if n == 0 else W
                        dve.wait_ge(s_qh, 5 * l + n + 1)
                        hi, lo = [K[:, part, 0:w] if n == 0 else Q[:, part, n - 1, 0:w] for part in range(2)]
                        V_.tensor_tensor(lo, qraw[:, n % 4, 0:w], f(hi), ALU.subtract).then_inc(s_q, 1)
                    n = lagging(p, 1)
                    if n is not None:
                        inverse(2 * (T if n == 0 else W) // 128, "heads")
                    n = lagging(p, 2)
                    if n is not None:
                        w = T if n == 0 else W
                        dve.wait_ge(s_spread, invs[0] - (lagging(p, 1) is not None))
                        tq = plan.tile[l, "qkv"] + (n + 1 if n else 0)
                        read_out(dve, tq, tq % 2)
                        stt(qraw[:, n % 4, 0:w], qraw[:, n % 4, 0:w], qg[:, l, (0 if n == 0 else 1):(1 if n == 0 else 2)],
                            M[:, 0:w], ALU.mult, ALU.mult).then_inc(s_qn, 1)
                    n = lagging(p, 3)
                    if n is not None:
                        q, c = qraw[:, n % 4, 0:S], 3 * (5 * l + n)
                        dve.wait_ge(s_rot, 5 * l + n + 1)
                        if c:
                            dve.wait_ge(s_qr, c)
                        V_.tensor_tensor(qrot[:, :], O[:, 1, 0:S], rope[:, 1, :], ALU.mult).then_inc(s_qr, 1)
                        V_.tensor_tensor(q, q, rope[:, 0, :], ALU.mult).then_inc(s_qr, 1)
                        dve.wait_ge(s_qr, c + 2)
                        V_.tensor_tensor(q, q, qrot[:, :], ALU.add).then_inc(s_qr, 1)

                t = plan.tile[l, "qkv"]
                for i in range(6):
                    if i == 1:
                        dve.wait_ge(s_vh, l + 1)
                        free(V_.tensor_tensor(V[:, 1].rearrange("p t n -> p (t n)"), G[:, 1, 0:T],
                                              f(V[:, 0].rearrange("p t n -> p (t n)")), ALU.subtract), 1)
                    qk_steps(i)

                t = plan.tile[l, "conf"]
                dve.wait_ge(s_pad, 7 * l + 3)
                for i in range(2 * KC):
                    if i % 2:
                        dve.wait_ge(s_tile, t + i + 1)
                        read_out(dve, t + i - 1, 0)
                        for a, n, v in segs:
                            ins = V_.tensor_tensor(hpad[:, i // 2, PAD + ctok(a):PAD + ctok(a) + n], G[:, 1, a:a + n],
                                                   GS[:, 0, a:a + n], ALU.mult)
                        free(ins, 1)
                    qk_steps(6 + i)

                st_, s0, t = steps(l), step_base[l], plan.tile[l, "att"]

                bt, b0 = batches(l), batch_base[l]
                ends = [sum(NKV * b[2] // 128 for b in bt[:n + 1]) for n in range(len(bt))]

                def maxima(i):
                    g, tile, q0, k0, nk, c = st_[i]
                    dve.wait_ge(s_tile, t + i + 1)
                    V_.tensor_reduce(nmax[:, i % 4:i % 4 + 1], G[:, i % 2, k0:k0 + nk], AX.X, ALU.max, negate=True)\
                        .then_inc(s_nm, 1)

                def turned(i):
                    g, tile, q0, k0, nk, col = st_[i]
                    j, c = i // 2, 128 * (i % 2)
                    for half, (a, b) in enumerate(((0, 4), (4, T // 128))):
                        if k0 > 128 * a:
                            continue
                        dve.wait_ge(s_ph[half], (s0 if half else S // 128 * NH * l) + i + 1)
                        V_.tensor_tensor(PT[:, j % 2, 1, a:b, c:c + 128],
                                         M[:, 128 * a:128 * b].rearrange("p (k n) -> p k n", n=128),
                                         f(PT[:, j % 2, 0, a:b, c:c + 128]), ALU.subtract).then_inc(s_pl[half], 1)

                def batch_scales(n):
                    c0, w = bt[n][5], NKV * bt[n][2] // 128
                    phase_read_out(dve, t + ends[n])
                    V_.reciprocal(pinv[:, c0:c0 + w], psums[:, c0:c0 + w]).then_inc(s_pr, 1)
                    dve.wait_ge(s_pr, b0 + n + 1)
                    if b0 + n:
                        dve.wait_ge(s_ps, b0 + n)
                    V_.tensor_copy(pspread[:, 0:w], pinv[:, c0:c0 + w].unsqueeze(2).to_broadcast([128, w, HD]))\
                        .then_inc(s_pi, 1)

                def batch_scaled(n):
                    i, q0, nq = bt[n][:3]
                    dve.wait_ge(s_ps, b0 + n + 1)
                    dve.wait_ge(s_oc, (s0 + ends[n]) // 2)
                    V_.tensor_tensor(heads_raw[:, i, q0:q0 + nq], heads_raw[:, i, q0:q0 + nq], M[:, 0:nq], ALU.mult)\
                        .then_inc(s_os, 1)

                def batch_rest(n):
                    i, q0, nq = bt[n][:3]
                    dve.wait_ge(s_oh, b0 + n + 1)
                    V_.tensor_tensor(Q[:, 1, i, q0:q0 + nq], heads_raw[:, i, q0:q0 + nq], f(Q[:, 0, i, q0:q0 + nq]),
                                     ALU.subtract).then_inc(s_ol, 1)
                maxima(0)
                for i in range(len(st_) + 6):
                    if i + 1 < len(st_):
                        maxima(i + 1)
                    for lag, what in ((0, batch_scales), (2, batch_scaled), (5, batch_rest)):
                        if i - lag in ends:
                            what(ends.index(i - lag))
                    if i < len(st_):
                        turned(i)

                def taps(j0, n):
                    def tap(i):
                        for k in range(KC):
                            step = KC * TAPS * l + KC * j0 + k + KC * i
                            dve.wait_ge(s_tap, step - KC + 1)
                            w = cw[:, l, bass.ds(i * KC + KC * j0 + k, 1)]
                            stt(acc[:, k, 0:Wc], hpad[:, k, bass.ds(i + j0, Wc)], w, acc[:, k, 0:Wc],
                                ALU.mult, ALU.add).then_inc(s_tap, 1)
                    loop(dve, n, tap)

                for k in range(KC):
                    V_.tensor_scalar(acc[:, k, 0:Wc], hpad[:, k, 0:Wc], cw[:, l, k:k + 1],
                                     par[:, R_CB + KC * l + k:R_CB + KC * l + k + 1], ALU.mult, ALU.add).then_inc(s_tap, 1)

                def branch(b, i):
                    t = plan.tile[l, ("branch", b)] + 4 * i
                    for n in range(2):
                        dve.wait_ge(s_tile, t + 2 + n + 1)
                        read_out(dve, t + n, n)
                        if b == 0:
                            dst = merged[:, 2 * i + n, 0:W]
                        else:
                            dst = ybuf[:, n, 0:W]
                            done = 16 * l + KD * (b == 1) + 2 * (i - 1) + n + 1
                            if i or b == 1:
                                dve.wait_ge(s_mg, done)
                        free(V_.tensor_tensor(dst, G[:, n, 0:W], GS[:, n, 0:W], ALU.mult), n)
                for i in range(4):
                    taps(1 + 4 * i, 4)
                    branch(0, i)

                t = plan.tile[l, "sc"]
                phase_read_out(dve, t)
                dve.wait_ge(s_pad, 7 * (l + 1))
                Ws = W + 2 if l == 0 else W
                j0 = 17
                for i in range(KC):
                    a, n_taps = 3 * i, 4 - i % 2
                    taps(j0, n_taps)
                    j0 += n_taps
                    dve.wait_ge(s_tile, t + a + 2)
                    read_out(dve, t + a, a % 2)
                    for c, n, v in segs:
                        o_ = 1 + c + 2 * v
                        ins = V_.tensor_tensor(bx[:, o_:o_ + n], G[:, (a + 1) % 2, c:c + n], GS[:, 0, c:c + n], ALU.mult)
                    free(ins, (a + 1) % 2)
                    read_out(dve, t + a + 1, (a + 1) % 2)
                    c0 = 3 * (KC * l + i)
                    for j in range(SC_TAPS):
                        w = par[:, R_SC + (SC_TAPS * l + j) * KC + i:R_SC + (SC_TAPS * l + j) * KC + i + 1]
                        if j == 0:
                            ins = V_.tensor_scalar(sc_sum[:, 0:Ws], bx[:, 0:Ws], w, None, ALU.mult)
                        else:
                            dve.wait_ge(s_sct, c0 + j)
                            ins = stt(sc_sum[:, 0:Ws], bx[:, j:j + Ws], w, sc_sum[:, 0:Ws], ALU.mult, ALU.add)
                        ins.then_inc(s_sct, 1)
                    dve.wait_ge(s_sct, c0 + 3)
                    dve.wait_ge(s_tile, t + a + 3)
                    if i:
                        dve.wait_ge(s_scl, KC * l + i)
                    for c, n, v in segs:
                        ins = V_.tensor_tensor(GS[:, 1, c:c + n], G[:, a % 2, c:c + n], sc_sum[:, c + 2 * v:c + 2 * v + n],
                                               ALU.mult)
                    free(ins, a % 2)
                    dve.wait_ge(s_sch, KC * l + i + 1)
                    V_.tensor_tensor(SCO[:, 1, i, 0:W], GS[:, 1, 0:W], f(SCO[:, 0, i, 0:W]), ALU.subtract).then_inc(s_scl, 1)
                assert j0 == TAPS

                def ln_add(k, out_, in_, src):
                    V_.tensor_tensor(out_, in_, src, ALU.add).then_inc(s_ls, 1)
                dve.wait_ge(s_tap, KC * TAPS * (l + 1))
                for k in range(1, KC):
                    if k > 1:
                        dve.wait_ge(s_ls, 6 * l + k - 1)
                    V_.tensor_tensor(ln_sum[:, 0:Wc], acc[:, 0, 0:Wc] if k == 1 else ln_sum[:, 0:Wc], acc[:, k, 0:Wc],
                                     ALU.add).then_inc(s_ls, 1)
                for i in range(4):
                    branch(2, i)
                    if i == 1:
                        inverse(W // 128, "mean")
                        dve.wait_ge(s_spread, invs[0])
                        for k in range(KC):
                            for a, n, v in segs:
                                c = ctok(a)
                                ins = V_.tensor_tensor(acc[:, k, c:c + n], acc[:, k, c:c + n], M[:, a:a + n], ALU.subtract)
                            ins.then_inc(s_lsm, 1)
                    if i == 2:
                        for k in range(1, KC):
                            dve.wait_ge(s_lsq, KC * l + k + 1)
                            if k > 1:
                                dve.wait_ge(s_ls, 6 * l + 3 + k - 1)
                            V_.tensor_tensor(ln_sum[:, 0:Wc], ln_sum[:, 0:Wc], ln_sq[:, k % 2, 0:Wc], ALU.add)\
                                .then_inc(s_ls, 1)
                inverse(W // 128)
                dve.wait_ge(s_spread, invs[0])
                dve.wait_ge(s_lsm, KC * (2 * l + 1))
                for k in range(KC):
                    for a, n, v in segs:
                        c = ctok(a)
                        ins = stt(acc[:, k, c:c + n], acc[:, k, c:c + n], par[:, R_LG + KC * l + k:R_LG + KC * l + k + 1], M[:, a:a + n],
                                  ALU.mult, ALU.mult)
                    ins.then_inc(s_lsm, 1)
                for k in range(KC):
                    dve.wait_ge(s_lsg, KC * l + k + 1)
                    stt(acc[:, k, 0:Wc], acc[:, k, 0:Wc], par[:, R_LB + KC * l + k:R_LB + KC * l + k + 1], sig[:, k % 2, 0:Wc],
                        ALU.add, ALU.mult).then_inc(s_lv, 1)
                for k in range(KC):
                    dve.wait_ge(s_lh, KC * l + k + 1)
                    for a, n, v in segs:
                        c = ctok(a)
                        ins = V_.tensor_tensor(CF[:, 1, k, a:a + n], acc[:, k, c:c + n], f(CF[:, 0, k, a:a + n]), ALU.subtract)
                    ins.then_inc(s_ll, 1)
                for i in range(4):
                    branch(1, i)

                for i in range(KD):
                    dve.wait_ge(s_mh, KD * l + i + 1)
                    V_.tensor_tensor(H[:, 1, i, 0:W], merged[:, i, 0:W], f(H[:, 0, i, 0:W]), ALU.subtract).then_inc(s_h, 1)
                split[0] += KD
                if l == 0:
                    dve.wait_ge(s_mt, 3 * KD)
                x_tiles("mix", 2, segs, True)
                inverse(W // 128)
                norm(4, 3, segs, W)

                for p, n in enumerate(PARTS):
                    t = plan.tile[l, ("up", p)]

                    def up(i, t=t, p=p):
                        dve.wait_ge(s_tile, t + 2 * i + 2)
                        read_out(dve, t + 2 * i, 0)
                        free(V_.tensor_tensor(GS[:, 0, 0:W], G[:, 1, 0:W], GS[:, 0, 0:W], ALU.mult), 1)
                        dve.wait_ge(s_uh, up_base[l, p] + i + 1)
                        c = bass.ds(i + PARTS[0] * (p % 2), 1)
                        hi, lo = [U[:, c, part, 0:W].rearrange("p a n -> p (a n)") for part in range(2)]
                        V_.tensor_tensor(lo, GS[:, 0, 0:W], f(hi), ALU.subtract).then_inc(s_u, 1)
                    loop(dve, n, up)
                    if l == 0 and p == 0:
                        dve.wait_ge(s_mt, 4 * KD)
                    x_tiles(("down", p), 5, segs, p == len(PARTS) - 1 and l < DEPTH - 1)


_INS = ['x', 'c', 'ctx', 'c_ctx', 'w_ada', 'b_ada', 'w_in', 'q_norm', 'k_norm', 'w_attn_o', 'conf_dw_w', 'conf_dw_b',
        'conf_ln_g', 'conf_ln_b', 'w_conf_out', 'sc_dw_w', 'w_sc_out', 'w_mix_out', 'w_ffn_in', 'w_ffn_out']


def _constants():
    f32 = np.float32
    freqs = (ROPE_THETA ** (-np.arange(0, HD // 2, 2, dtype=f32) / f32(HD // 2))).astype(f32)
    tok = np.arange(S)
    angles = np.concatenate([np.tile((tok // GRID_W).astype(f32)[:, None] * freqs, 2),
                             np.tile((tok % GRID_W).astype(f32)[:, None] * freqs, 2)], axis=1)
    ang = np.tile(angles, 2).T
    swap = np.zeros((128, 128), f32)
    for m in range(128):
        if m % 32 < 16:
            swap[m + 16, m] = -1
        else:
            swap[m - 16, m] = 1
    heads = np.zeros((128, 2), f32)
    heads[:64, 0] = heads[64:, 1] = 1
    return {"ident": np.eye(128, dtype=f32), "swap": swap, "heads": heads,
            "rope": np.ascontiguousarray(np.stack([np.cos(ang), np.sin(ang)]).astype(f32))}


def kernel(**inputs):
    import concourse.bacc as _bacc
    from concourse.bass_utils import run_bass_kernel_spmd as _run

    nc = _bacc.Bacc("TRN2", target_bir_lowering=False, num_devices=1)
    arrays, aps = {}, {}
    for name, a in [(n, np.ascontiguousarray(inputs[n])) for n in _INS] + list(_constants().items()):
        arrays[f"in_{name}"] = a
        aps[name] = nc.dram_tensor(f"in_{name}", a.shape, mybir.dt.from_np(a.dtype), kind="ExternalInput").ap()
    out = nc.dram_tensor("out", (1, S, D), F32, kind="ExternalOutput").ap()
    build(nc, aps, out)
    return _run(nc, [arrays], core_ids=[0]).results[0]["out"]
```

```python
import numpy as np
import concourse.bass as bass
from concourse import mybir

F32, F32R = mybir.dt.float32, mybir.dt.float32r
ALU, ACT, AX = mybir.AluOpType, mybir.ActivationFunctionType, mybir.AxisListType

DEPTH, D, S, LC = 2, 1024, 512, 256
T = S + LC
KD = D // 128
HD, NH, NKV = 64, 8, 2
ATT, KVW = NH * HD, NKV * HD
CW = D // 2
KC = CW // 128
TAPS, SC_TAPS = 31, 3
PAD = TAPS // 2
FFN = 2816
OFF_K, OFF_V, OFF_CONF = ATT, ATT + KVW, ATT + 2 * KVW
OFF_SC = OFF_CONF + 2 * CW
OFF_GATE = OFF_SC + 3 * CW
N_MOD = 6
EPS = 1e-6
ROPE_THETA, GRID_W = 10000.0, 64
MT = N_MOD * KD
PARTS = [6, 6, 6, 4]
SEGS = [[(0, S, 0), (S, LC, 1)], [(0, S, 0)]]
WIDTH = [T, S]
GAP = 2 * PAD
CONV_W = [T + GAP, S]
R_CB = 0
R_LG = R_CB + DEPTH * KC
R_LB = R_LG + DEPTH * KC
R_SC = R_LB + DEPTH * KC
R_QN = R_SC + DEPTH * SC_TAPS * KC
R_KN = R_QN + DEPTH
R_C = R_KN + DEPTH
PAR_ROWS = R_C + 2 * KD
V_AT = 2
CONV_ROWS = TAPS * KC
SPREAD_AT = (3, 4, 5, 7)
LOOPS = True


def ctok(c):
    return c if c < S else c + GAP


def half(width):
    return 512 if width > 512 else width // 2


class Plan:

    def __init__(self):
        self.unit, self.tile, self.last = {}, {}, []
        u = t = 0
        self.tile["load"] = 0
        t += KD
        for l in range(DEPTH):
            phases = [("qkv", [1] * 6), ("conf", [1] * 8), ("att", None)]
            phases += [(("branch", 0), [1, 1, 2] * 4), ("sc", [1] * 12)]
            phases += [(("branch", 2), [1, 1, 2] * 4), (("branch", 1), [1, 1, 2] * 4)]
            phases += [("mix", [1] * KD)]
            for p, n in enumerate(PARTS):
                phases += [(("up", p), [1] * 2 * n), (("down", p), [1] * KD)]
            for name, tiles in phases:
                self.unit[l, name], self.tile[l, name] = u, t
                if name == "att":
                    t += len(steps(l))
                    continue
                for n in tiles:
                    t += n
                    u += 1
                    self.last.append(t)
            assert u % 2 == 0 and t % 2 == 0
        self.tile["store"] = t
        self.width = {(l, name): 128 * PARTS[name[1]] if name[0] == "down" else 1024 for l, name in self.unit}
        self.units = u


def batches(l):
    out = [(i, 0, S, 0, T, 8 * i) for i in range(KC)]
    if l == 0:
        out += [(i, S, LC, S, LC, 32 + 4 * i) for i in range(KC)]
    return out


def steps(l):
    return [(g, i, q0 + 128 * j, k0, nk, c0 + 2 * j + g)
            for i, q0, nq, k0, nk, c0 in batches(l) for g in (1, 0) for j in range(nq // 128)]


def latent_steps(l, i):
    return S // 128 * NH * l + sum(k0 == 0 for g, tile, q0, k0, nk, c in steps(l)[:i])


ADA_FIRST = 2 * KD
ADA_PHASES = [(0, ("branch", 2)), (0, ("branch", 1)), (0, "mix"), (0, ("up", 0)), (0, ("up", 1)), (0, ("up", 2)),
              (1, ("branch", 0)), (1, ("branch", 2)), (1, ("branch", 1))]
ADA_UNITS = [12, 12, KD, 2 * PARTS[0], 2 * PARTS[1], 2 * PARTS[2], 4, 4, 4]
ADA_BASE = {ph: sum(ADA_UNITS[:i]) for i, ph in enumerate(ADA_PHASES)}
ADA_LATER = DEPTH * MT - ADA_FIRST
assert sum(ADA_UNITS) == ADA_LATER and all(b % 2 == 0 for b in ADA_BASE.values())
ADA_STEPS = 2 * KD


def ada_chunk(j):
    return j // 2 + KD // 2 * (j % 2)


def loop(eng, n, body):
    if LOOPS and n > 2:
        with eng.Fori(0, n) as i:
            body(i)
    else:
        for i in range(n):
            body(i)


def build(nc, A, out):
    plan = Plan()

    base = 17 * 1024
    at = {}

    def region(name, size):
        at[name] = base + sum(sizes.values())
        sizes[name] = size
    sizes = {}
    region("X", KD * T * 4)
    region("H", KD * T * 8)
    region("AS", KC * T * 8)
    region("CF", KC * T * 8)
    region("DD", KD * T * 4)
    region("EE", 19200)
    region("RAW", 2 * 4096)
    region("WHL", 2 * 8192)
    region("GS", 2 * T * 4)
    region("CONST", 14560)

    def sb(name, shape, dt, where, off=0):
        return nc.alloc_sbuf_tensor_at(name, shape, dt, offset=at[where] + off)

    X = sb("x_T", [128, KD, T], F32, "X")
    H = sb("h_parts", [128, 2, KD, T], F32R, "H")
    ada = sb("ada_weights", [128, ADA_FIRST // 2, KD, 256], F32, "H")
    Q = sb("q_parts", [128, 2, KC, T], F32R, "AS")
    SCO = sb("shortconv_parts", [128, 2, KC, T], F32R, "AS")
    arow = sb("ada_rows", [2, ADA_FIRST * 128], F32, "CF")
    hpad = sb("conf_padded", [128, KC, T + 2 * GAP], F32, "CF")
    CF = sb("conf_parts", [128, 2, KC, T], F32R, "CF")
    ln_sum = sb("ln_sum", [128, T + GAP], F32, "CF")
    ln_sq = sb("ln_square", [128, 2, T + GAP], F32, "CF", 3200)
    sig = sb("ln_sigmoid", [128, 2, T + GAP], F32, "CF", 9600)
    merged = sb("merged", [128, KD, T], F32, "DD")
    xin = sb("x_rows", [128, T // 128, D], F32, "DD")
    qraw = sb("q_raw", [128, 4, T], F32, "DD")
    qsq = sb("q_square", [128, T], F32, "DD", 16 * T)
    qspread = sb("q_inverse_spread", [128, T // 128, 2, HD], F32, "DD", 20 * T)
    qrot = sb("q_rotated", [128, S], F32, "DD", 24 * T)
    rope = sb("rope_tables", [128, 2, S], F32, "DD", 24 * T + 4 * S)
    heads_raw = sb("heads_unscaled", [128, KC, T], F32, "AS", 4 * KC * T)
    PT = sb("probs_T_parts", [128, 2, 2, T // 128, 256], F32R, "DD")
    U = sb("hidden_parts", [128, 2 * PARTS[0], 2, T], F32R, "AS")
    K_twice = [sb(f"k_high_twice_{g}", [128, T], F32R, *((("EE", 0), ("GS", 4 * T))[g])) for g in range(NKV)]
    K_rest = sb("k_rest", [128, T], F32R, "EE", 4 * T)
    V = sb("v_parts", [128, 2, T // 128, 128], F32R, "EE", 8 * T)
    P = sb("probs", [128, 2, T], F32, "EE", 16 * T)
    vraw = sb("v_raw", [128, T], F32, "EE", 16 * T)
    acc = sb("conv_sum", [128, KC, T + GAP], F32, "EE")
    E2 = 16 * (T + GAP)
    bx = sb("sc_padded", [128, T + 4], F32, "EE", E2)
    sc_sum = sb("sc_sum", [128, T + 2], F32, "EE", E2 + 3104)
    ybuf = sb("gated", [128, 2, T], F32, "EE", E2)
    SQ = sb("x_square", [128, 2, T], F32, "EE")
    SSQ = sb("sum_square", [128, T], F32, "EE", 8 * T)
    HT = sb("h_scaled", [128, 2, T], F32, "EE", 12 * T)
    sgc = sb("sigmoid_c", [128, 2, KD], F32, "EE", 24 * T)
    stage = sb("parameter_rows", [128, 4, 128], F32, "EE")
    xout = sb("out_rows", [128, S // 128, D], F32, "EE")
    raw = sb("w_raw", [128, 2, 1024], F32, "RAW")
    WHL = sb("w_parts", [128, 2, 2, 1024], F32R, "WHL")
    GS = sb("gates", [128, 2, T], F32, "GS")
    pspread = sb("prob_scale_spread", [128, 2, 2 * T // 128, HD], F32, "GS")
    used = [0]

    def const(name, shape):
        t_ = sb(name, shape, F32, "CONST", used[0])
        used[0] += -(-4 * int(np.prod(shape[1:])) // 32) * 32
        return t_

    ident = const("identity", [128, 128])
    swap = const("rope_swap", [128, 128])
    ones = const("ones", [128, 1])
    heads = const("head_columns", [128, 2])
    eps = const("eps", [128, 1])
    bada = const("modulation_bias", [128, DEPTH, MT])
    par = const("parameters", [128, PAR_ROWS])
    cw = const("conv_taps", [128, DEPTH, CONV_ROWS])
    qg = const("head_gains", [128, DEPTH, 2])
    csil = const("silu_c", [128, KD, 2])
    root = const("unused", [128, 1])
    mods = const("modulation", [128, DEPTH, MT, 2])
    adaw = const("ada_tile_weights", [128, 2, KD, 128])
    adp = const("ada_tile_sums", [128, 2, 2, 128])
    sd = const("deviation", [128, 2, 12])
    rs = const("inverse_deviation", [128, 2, 12])
    nmax = const("minus_max", [128, 4])
    psums = const("prob_sums", [128, 48])
    pinv = const("prob_scales", [128, 48])
    assert used[0] <= sizes["CONST"] and at["CONST"] + used[0] <= nc.sbuf_usable_end

    G = nc.alloc_psum_tensor("tiles", [128, 2, 1024], F32)
    M = nc.alloc_psum_tensor("small_wide", [128, 1024], F32)
    O = nc.alloc_psum_tensor("small_pair", [128, 2, 512], F32)

    sem = nc.alloc_semaphore
    s_const, s_in, s_par, s_rope = sem("constants_in"), sem("rows_in"), sem("parameter_rows_in"), sem("rope_in")
    s_ada = [sem(f"ada_in_{i}") for i in range(ADA_FIRST // 2)]
    s_w = [sem(f"raw_in_{i}") for i in range(2)]
    s_out = sem("out_stored")
    s_set = sem("constants_set")
    s_part, s_parc, s_qg = sem("parameters_transposed"), sem("parameters_copied"), sem("gains_scaled")
    s_sgc, s_csil = sem("sigmoid_c_done"), sem("silu_c_done")
    s_adw = [sem(f"ada_tile_in_{i}") for i in range(2)]
    s_adv, s_mt = sem("ada_tile_step"), sem("modulation_tile_done")
    s_ar, s_arow = sem("ada_row_done"), sem("ada_row_copied")
    s_adt, s_mod = sem("ada_tile_done"), sem("modulation_steps")
    s_hi, s_lo = sem("w_high_done"), sem("w_rest_done")
    s_tile = sem("tile_done")
    s_free = [sem(f"tile_read_out_{i}") for i in range(2)]
    s_sq, s_ssq = sem("square_done"), sem("square_summed")
    s_stat, s_sd, s_rc, s_inv, s_spread = (sem("statistic_done"), sem("deviation_done"), sem("reciprocal_done"),
                                           sem("inverse_done"), sem("spread_done"))
    s_ht, s_hh, s_h = sem("h_scaled_done"), sem("h_high_done"), sem("h_parts_done")
    s_qsq, s_qn, s_rot, s_qr = sem("q_square_done"), sem("q_scaled"), sem("q_rotation_done"), sem("q_rope_steps")
    s_qh, s_q = sem("q_high_done"), sem("q_parts_done")
    s_vt, s_vh, s_v = sem("v_transposed"), sem("v_high_done"), sem("v_parts_done")
    s_nm = sem("minus_max_done")
    s_pt = [sem(f"probs_transposed_{i}") for i in range(2)]
    s_ph = [sem(f"probs_T_high_done_{i}") for i in range(2)]
    s_pl = [sem(f"probs_T_parts_done_{i}") for i in range(2)]
    s_o, s_oc = sem("heads_done"), sem("heads_copied")
    s_pr, s_pi, s_ps = sem("prob_reciprocal_done"), sem("prob_scale_done"), sem("prob_scale_spread_done")
    s_os, s_oh, s_ol = sem("heads_scaled"), sem("heads_high_done"), sem("heads_parts_done")
    s_pad = sem("padding_set")
    s_tap, s_ls, s_lsq, s_lsm = sem("conv_step"), sem("ln_sum_step"), sem("ln_square_done"), sem("ln_scale_step")
    s_lsg, s_lv, s_lh, s_ll = sem("ln_sigmoid_done"), sem("ln_silu_done"), sem("conf_high_done"), sem("conf_parts_done")
    s_root = sem("root_table_loaded")
    s_sct, s_sch, s_scl = sem("sc_conv_step"), sem("sc_high_done"), sem("sc_parts_done")
    s_mg, s_mh = sem("merged_added"), sem("merged_high_done")
    s_uh, s_u = sem("hidden_high_done"), sem("hidden_parts_done")

    def f(ap):
        return ap.bitcast(F32)

    def read_out(eng, t, slot):
        eng.wait_ge(s_free[slot], t - slot + 2)

    def ada_tile(n, layer):
        m = n + ADA_FIRST
        return (0, m) if layer == 0 else (1, m - MT)

    def ada_number(l, phase, q):
        if (l, phase) not in ADA_BASE:
            return None
        if l == 0:
            return ADA_BASE[l, phase] + q
        return ADA_BASE[l, phase] + q // 3 if q % 3 == 2 else None

    def ada_layer(l, phase):
        return 0 if ADA_BASE[l, phase] + ADA_FIRST < MT else 1

    def phase_read_out(eng, t):
        for r in range(2):
            eng.wait_ge(s_free[r], t)

    def lagging(p, lag):
        i = p - lag
        return None if i < 0 or i == V_AT or i > 5 else i - (i > V_AT)

    def product_of(n):
        return n + (n >= V_AT)

    step_base = [sum(len(steps(x)) for x in range(l)) for l in range(DEPTH)]
    up_base = {}
    n = 0
    for l in range(DEPTH):
        for p, w in enumerate(PARTS):
            up_base[l, p] = n
            n += w

    with nc.Block() as block:
        @block.sync
        def _(sp):
            dma = sp.dma_start
            dma(ident[:, :], A["ident"]).then_inc(s_const, 16)
            dma(swap[:, :], A["swap"]).then_inc(s_const, 16)
            dma(heads[:, :], A["heads"]).then_inc(s_const, 16)

            def rows(block, r, ap):
                dma(stage[r:r + ap.shape[0], block, 0:ap.shape[1]], ap).then_inc(s_par, 16)
            rows(1, R_C, A["c"][0].rearrange("(r p) -> r p", p=128))
            rows(1, R_C + KD, A["c_ctx"].rearrange("(r p) -> r p", p=128))
            for r, name in ((R_CB, "conf_dw_b"), (R_LG, "conf_ln_g"), (R_LB, "conf_ln_b")):
                rows(1, r, A[name].rearrange("l (r p) -> (l r) p", p=128))
            rows(1, R_SC, A["sc_dw_w"].rearrange("l j (r p) -> (l j r) p", p=128))
            for half in range(2):
                for r, name in ((R_QN, "q_norm"), (R_KN, "k_norm")):
                    dma(stage[r:r + DEPTH, 1, 64 * half:64 * half + 64], A[name]).then_inc(s_par, 16)
            rows(0, 0, A["b_ada"].rearrange("l (r p) -> (l r) p", p=128))
            for l in range(DEPTH):
                rows(2 + l, 0, A["conf_dw_w"][l].rearrange("j (r p) -> (j r) p", p=128))

            def unit(u, slot, halves, turn=None):
                ahead = u - 1 if not (isinstance(u, int) and u < 2) else None
                if ahead is not None:
                    sp.wait_ge(s_lo, ahead * 2)
                for dst, src in halves:
                    dma(dst, src).then_inc(s_w[slot], 16)

            def cols(slot, view, c0):
                nk = view.shape[1]
                r = raw[:, slot, 0:nk * 128].rearrange("p (k n) -> p k n", n=128)
                return [(r[q:q + 64], view[q:q + 64, :, bass.ds(c0, 128)]) for q in (0, 64)]

            for l in range(DEPTH):
                wi = A["w_in"][l].rearrange("(k p) n -> p k n", p=128)
                u = plan.unit[l, "qkv"]
                unit(u, 0, cols(0, wi, OFF_K))
                for i in range(4):
                    j = product_of(i + 1)
                    if j == V_AT + 1:
                        unit(u + V_AT, V_AT % 2, cols(V_AT % 2, wi, OFF_V))
                    if i == 1:
                        sp.wait_ge(s_tile, plan.tile[l, "qkv"])
                        for half in range(2):
                            dma(rope[:, half, :], A["rope"][half]).then_inc(s_rope, 16)
                    rw = raw[:, j % 2, :].rearrange("p (k n) -> p k n", n=128)
                    unit(u + j, j % 2, [(rw[:, :, 64 * g:64 * g + 64],
                                         wi[:, :, 64 * (4 * g + i):64 * (4 * g + i) + 64]) for g in range(2)])

                u = plan.unit[l, "conf"]

                def conf(i):
                    unit(u + 2 * i, 0, cols(0, wi, 128 * i + OFF_CONF + CW))
                    unit(u + 2 * i + 1, 1, cols(1, wi, 128 * i + OFF_CONF))
                loop(sp, KC, conf)

                for b in (0, "sc", 2, 1):
                    if b == "sc":
                        u_sc = plan.unit[l, "sc"]

                        def sc(i):
                            for r in range(2):
                                for n, c in enumerate((1, 2, 0)):
                                    q = 3 * r + n
                                    unit(u_sc + 6 * i + q, q % 2, cols(q % 2, wi, 256 * i + 128 * r + OFF_SC + c * CW))
                        loop(sp, KC // 2, sc)
                        continue
                    u_b = plan.unit[l, ("branch", b)]
                    wo = A[("w_attn_o", "w_conf_out", "w_sc_out")[b]][l]

                    def branch(i, b=b, u_b=u_b, wo=wo):
                        for r in range(2):
                            q = 3 * r
                            for n in range(2):
                                unit(u_b + 6 * i + q + n, (q + n) % 2,
                                     cols((q + n) % 2, wi, 512 * i + 256 * r + 128 * n + OFF_GATE + b * D))
                            slot = (q + 2) % 2
                            rw = raw[:, slot, :].rearrange("p (k n) -> p k n", n=256)
                            v = (wo.rearrange("(g k p) n -> g p k n", g=2, p=64) if b == 0
                                 else wo.rearrange("(k g p) n -> g p k n", g=2, p=64))
                            unit(u_b + 6 * i + q + 2, slot,
                                 [(rw[64 * g:64 * g + 64], v[g, :, :, bass.ds(512 * i + 256 * r, 256)]) for g in range(2)])
                    loop(sp, 2, branch)

                wm = A["w_mix_out"][l].rearrange("(k p) n -> p k n", p=128)
                u_m = plan.unit[l, "mix"]

                def mix(i):
                    for r in range(2):
                        unit(u_m + 2 * i + r, r, cols(r, wm, 256 * i + 128 * r))
                loop(sp, KD // 2, mix)
                wf = A["w_ffn_in"][l].rearrange("(k p) n -> p k n", p=128)
                f0 = 0
                for p, n in enumerate(PARTS):
                    u_u, u_d = plan.unit[l, ("up", p)], plan.unit[l, ("down", p)]

                    def up(i, u_u=u_u, f0=f0):
                        for r in range(2):
                            unit(u_u + 2 * i + r, r, cols(r, wf, 128 * i + 128 * f0 + r * FFN))
                    loop(sp, n, up)
                    wd = A["w_ffn_out"][l][128 * f0:128 * (f0 + n), :].rearrange("(k p) n -> p k n", p=128)

                    def down(i, u_d=u_d, wd=wd):
                        for r in range(2):
                            unit(u_d + 2 * i + r, r, cols(r, wd, 256 * i + 128 * r))
                    loop(sp, KD // 2, down)
                    f0 += n
            for r in range(2):
                sp.wait_ge(s_free[r], plan.tile["store"] + KD)
            dma(out[0].rearrange("(t p) n -> p t n", p=128), xout[:, :, :]).then_inc(s_out, 16)
            sp.wait_ge(s_out, 16)

        @block.tensor
        def _(pe):
            def mm(o_, a, b, start=True, stop=True):
                return nc.tensor.matmul(o_, a, b, start=start, stop=stop)

            def done(ins):
                ins.then_inc(s_tile, 1)

            def take_slot(t, slot):
                if not (isinstance(t, int) and t < 2):
                    pe.wait_ge(s_free[slot], t - slot)

            def three(dst, a, b, first, last):
                mm(dst, a(0), b(0), first, False)
                mm(dst, a(0), b(1), False, False)
                return mm(dst, a(1), b(0), False, last)

            def part(k, slot, u, wslot, ks, rhs, width, cut=0, wn=128):
                segs = [(0, 512)] + ([(512, width)] if width > 512 else [])
                c = k * wn + cut
                h = half(ks * wn)
                if k == 0:
                    pe.wait_ge(s_lo, u * 2 + 1)
                if c + 128 > h and (k == 0 or c - wn + 128 <= h):
                    pe.wait_ge(s_lo, u * 2 + 2)
                for pw, px in ((0, 0), (0, 1), (1, 0)):
                    for a, b in segs:
                        ins = mm(G[:, slot, a:b], WHL[:, wslot, pw, c:c + 128], rhs(px, k, a, b),
                                 k == 0 and (pw, px) == (0, 0), k == ks - 1 and pw == 1)
                return ins

            def product(slot, u, wslot, ks, rhs, width, before_k=None, cut=0, wn=128):
                for k in range(ks):
                    if before_k:
                        before_k(k)
                    ins = part(k, slot, u, wslot, ks, rhs, width, cut, wn)
                return ins

            def two_products(t, u, ks, rhs, widths, before_k):
                for r in range(2):
                    take_slot(t + r, r)
                for k in range(ks):
                    before_k(k)
                    for r in range(2):
                        ins = part(k, r, u + r, r, ks, rhs, widths[r])
                        if k == ks - 1:
                            done(ins)

            def from_h(part, k, a, b):
                return H[:, part, k, a:b]

            pe.wait_ge(s_const, 48)
            pe.wait_ge(s_par, 16 * (11 + DEPTH))
            nc.tensor.transpose(O[:, 0, 0:DEPTH * MT], stage[0:DEPTH * MT, 0, :], ident[0:DEPTH * MT, 0:DEPTH * MT])
            nc.tensor.transpose(O[:, 0, 128:128 + PAR_ROWS], stage[0:PAR_ROWS, 1, :], ident[0:PAR_ROWS, 0:PAR_ROWS])\
                .then_inc(s_part, 1)
            for l in range(DEPTH):
                ins = nc.tensor.transpose(O[:, 1, 128 * l:128 * l + CONV_ROWS],
                                          stage[0:CONV_ROWS, 2 + l, :], ident[0:CONV_ROWS, 0:CONV_ROWS])
            ins.then_inc(s_part, 1)
            pe.wait_ge(s_in, 32)
            def modulation_rows(j):
                pe.wait_ge(s_ada[j], 16)
                if j >= 2:
                    pe.wait_ge(s_arow, j - 1)
                row = M[0:2, 512 * (j % 2):512 * (j % 2) + 256] if j < 4 else G[0:2, j % 2, 0:256]
                for k in range(KD):
                    ins = mm(row, csil[:, k, :], ada[:, j, k, :], k == 0, k == KD - 1)
                ins.then_inc(s_ar, 1)

            def modulation_columns(j):
                pe.wait_ge(s_arow, j + 1)
                if j and j % 2 == 0:
                    pe.wait_ge(s_mod, j)
                for m in (2 * ada_chunk(j), 2 * ada_chunk(j) + 1):
                    ins = nc.tensor.transpose(O[:, 1, 2 * m:2 * m + 2], arow[:, 128 * m:128 * m + 128], ident[0:2, 0:2])
                ins.then_inc(s_adt, 1)

            for i in range(KD):
                take_slot(i, i % 2)
                for t in range(T // 128):
                    ins = nc.tensor.transpose(G[:, i % 2, 128 * t:128 * t + 128],
                                              xin[:, t, 128 * i:128 * i + 128], ident[:, :])
                done(ins)
                if i == 3:
                    pe.wait_ge(s_csil, 1)
                if i % 2 and i >= 3:
                    modulation_rows(i // 2 - 1)
                    if i > 3:
                        modulation_columns(i // 2 - 2)
            modulation_rows(KD // 2 - 1)
            modulation_columns(KD // 2 - 2)

            stats, spreads, squared, normed = [0], [0], [0], [0]

            def statistic(src, width, rhs, n=1, off=lambda c: c):
                k = stats[0]
                if k:
                    pe.wait_ge(s_sd, k)
                for t in range(width // 128):
                    c = off(128 * t)
                    b = 16 * (k % 2) + n * t
                    ins = mm(O[:, 0, b:b + n], src[:, c:c + 128], rhs)
                ins.then_inc(s_stat, 1)
                stats[0] += 1

            def spread(width, n=1):
                k = spreads[0]
                pe.wait_ge(s_inv, k + 1)
                for t in range(width // 128):
                    if n == 1:
                        ins = mm(M[:, 128 * t:128 * t + 128], rs[:, k % 2, t:t + 1].to_broadcast([128, 128]), ident[:, :])
                    else:
                        ins = nc.tensor.transpose(M[:, 128 * t:128 * t + 128],
                                                  qspread[:, t].rearrange("p h d -> p (h d)"), ident[:, :])
                ins.then_inc(s_spread, 1)
                spreads[0] += 1

            def modulation(n, slot):
                pe.wait_ge(s_adv, ADA_STEPS * n + ADA_STEPS)
                pe.wait_ge(*((s_mod, KD) if isinstance(n, int) and n == 0 else (s_mt, n)))
                for v in range(2):
                    ins = mm(O[:, 1, v:v + 1], adp[:, slot, v, :], ones[:, :])
                ins.then_inc(s_adt, 1)

            def modulation_before(n, slot):
                if n is None or isinstance(n, int) and n == 0:
                    return
                modulation(n - 1, 1 - slot)

            def norm(width, between=None):
                squared[0] += KD - 1
                pe.wait_ge(s_ssq, squared[0])
                statistic(SSQ, width, ones[:, :])
                if between:
                    between()
                spread(width)

            def h_ready(k):
                pe.wait_ge(s_h, normed[0] + k + 1)

            pe.wait_ge(s_set, 2)
            for l in range(DEPTH):
                W = WIDTH[l]
                if l == 0:
                    def between():
                        phase_read_out(pe, plan.tile[0, "qkv"])
                        modulation_rows(KD // 2)
                        modulation_columns(KD // 2 - 1)
                    norm(T, between)
                    for j in range(KD // 2 + 1, KD):
                        modulation_rows(j)
                        modulation_columns(j - 1)
                    modulation_columns(KD - 1)
                else:
                    norm(T)

                def qk_steps(p):
                    n = lagging(p, 1)
                    if n is not None:
                        pe.wait_ge(s_qsq, 5 * l + n + 1)
                        statistic(qsq, T if n == 0 else W, heads[:, :], n=2)
                    n = lagging(p, 2)
                    if n is not None:
                        if n == 0:
                            pe.wait_ge(s_h, normed[0])
                        else:
                            pe.wait_ge(s_qn, 5 * l + n)
                        if p == V_AT + 3:
                            pe.wait_ge(s_v, l + 1)
                        spread(T if n == 0 else W, n=2)
                    if p == V_AT + 2:
                        pe.wait_ge(s_qn, 5 * l + V_AT)
                        read_out(pe, plan.tile[l, "qkv"] + V_AT, V_AT % 2)
                        for tt in range(T // 128):
                            ins = nc.tensor.transpose(M[:, 128 * tt:128 * tt + 128], vraw[:, 128 * tt:128 * tt + 128],
                                                      ident[:, :])
                        ins.then_inc(s_vt, 1)
                    n = lagging(p, 3)
                    if n is not None:
                        pe.wait_ge(s_qn, 5 * l + n + 1)
                        if n:
                            pe.wait_ge(s_qr, 3 * (5 * l + n))
                        mm(O[:, 1, 0:S], swap[:, :], qraw[:, n % 4, 0:S]).then_inc(s_rot, 1)

                u, t = plan.unit[l, "qkv"], plan.tile[l, "qkv"]
                two_products(t, u, KD, from_h, (T, W), h_ready)
                normed[0] += KD
                qk_steps(1)
                for i in range(2, 6):
                    take_slot(t + i, i % 2)
                    ins = product(i % 2, u + i, i % 2, KD, from_h, T if i == V_AT else W)
                    done(ins)
                    qk_steps(i)

                u, t = plan.unit[l, "conf"], plan.tile[l, "conf"]
                for i in range(2 * KC):
                    take_slot(t + i, i % 2)
                    done(product(i % 2, u + i, i % 2, KD, from_h, W))
                    qk_steps(6 + i)

                t, st_ = plan.tile[l, "att"], steps(l)
                s0 = step_base[l]

                def scores(i):
                    g, tile, q0, k0, nk, c = st_[i]
                    r = slice(64 * g, 64 * g + 64)
                    take_slot(t + i, i % 2)
                    for a, b in ([(0, 512), (512, 768)] if nk == T else [(512, 768)]):
                        mm(G[:, i % 2, a:b], Q[:, g, tile, q0:q0 + 128], K_twice[g][:, a:b], True, False)
                        ins = mm(G[:, i % 2, a:b], Q[r, g, tile, q0:q0 + 128], K_rest[r, a:b], False, True)
                    done(ins)

                def turn(i):
                    g, tile, q0, k0, nk, c = st_[i]
                    read_out(pe, t + i, i % 2)
                    for half, kts in ((0, range(4)), (1, range(4, T // 128))):
                        if k0 > 128 * kts[0]:
                            continue
                        pe.wait_ge(s_pl[half], s0 + i if half else latent_steps(l, i))
                        for kt in kts:
                            cols_ = slice(128 * kt, 128 * kt + 128)
                            ins = nc.tensor.transpose(M[:, cols_], P[:, i % 2, cols_], ident[:, :])
                        ins.then_inc(s_pt[half], 1)

                def values(j, half):
                    g, tile, q0, k0, nk, c = st_[2 * j]
                    if half == 0:
                        pe.wait_ge(s_pl[1], s0 + 2 * j + 2)
                        if s0 // 2 + j >= 2:
                            pe.wait_ge(s_oc, s0 // 2 + j - 1)
                    kts = range(k0 // 128, (k0 + nk) // 128)
                    n = len(kts) // 2
                    for kt in kts[n * half:n * half + n]:
                        ins = three(O[:, j % 2, 0:256], lambda part: V[:, part, kt, :],
                                    lambda part: PT[:, j % 2, part, kt, :], kt == kts[0], kt == kts[-1])
                    if half:
                        ins.then_inc(s_o, 1)

                def spread_scales(n):
                    pe.wait_ge(s_pi, KC * l + n + 1)
                    if n == 0:
                        for half in range(2):
                            pe.wait_ge(s_pl[half], s0 + len(st_) if half else S // 128 * NH * (l + 1))
                    else:
                        pe.wait_ge(s_os, KC * l + n)
                    for j in range(W // 128):
                        ins = nc.tensor.transpose(M[:, 128 * j:128 * j + 128],
                                                  pspread[:, n % 2, 2 * j:2 * j + 2].rearrange("p h d -> p (h d)"),
                                                  ident[:, :])
                    ins.then_inc(s_ps, 1)

                def attention_end(k):
                    if k == 1:
                        for half in range(2):
                            values(len(st_) // 2 - 1, half)
                    if k in SPREAD_AT:
                        spread_scales(SPREAD_AT.index(k))
                    if k == KD - 1:
                        pe.wait_ge(s_oc, (s0 + len(st_)) // 2)

                pe.wait_ge(s_q, 5 * (l + 1))
                pe.wait_ge(s_v, l + 1)
                scores(0)
                scores(1)
                for i in range(len(st_) + 1):
                    if i + 2 < len(st_):
                        scores(i + 2)
                    if i >= 3:
                        values((i - 3) // 2, (i - 3) % 2)
                    if i < len(st_):
                        turn(i)

                def branch(b, i, among=None):
                    u, t = plan.unit[l, ("branch", b)] + 3 * i, plan.tile[l, ("branch", b)] + 4 * i
                    Y = (Q, CF, SCO)[b]

                    def ada_before(q):
                        n = ada_number(l, ("branch", b), q)
                        if n is not None:
                            modulation_before(n, n % 2)
                    for n in range(2):
                        take_slot(t + n, n)
                        done(product(n, u + n, (i + n) % 2, KD, from_h, W, None if n else among))
                        ada_before(3 * i + n)
                    if i == 0:
                        pe.wait_ge(*((s_ol, KC * (l + 1)), (s_ll, KC * (l + 1)), (s_scl, KC * (l + 1)))[b])
                    for n in range(2):
                        take_slot(t + 2 + n, n)
                        done(product(n, u + 2, i % 2, KC, lambda part, k, a, b_: Y[:, part, k, a:b_], W, cut=128 * n, wn=256))
                    ada_before(3 * i + 2)
                branch(0, 0, attention_end)
                for i in range(1, 4):
                    branch(0, i)

                u, t = plan.unit[l, "sc"], plan.tile[l, "sc"]

                def sc(i, u=u, t=t):
                    for q in range(2):
                        take_slot(t + 2 * i + q, q)
                        done(product(q, u + 2 * i + q, q, KD, from_h, W))
                loop(pe, 6, sc)

                def ln_statistic(n, k):
                    if k == 0:
                        pe.wait_ge(s_ls, 6 * l + 3 + 3 * n)
                        statistic(ln_sum, W, ones[:, :], off=ctok)
                    if k == KD // 2:
                        if n:
                            pe.wait_ge(s_lsm, KC * (2 * l + 1))
                        spread(W)
                branch(2, 0)
                branch(2, 1, lambda k: ln_statistic(0, k))
                branch(2, 2, lambda k: ln_statistic(1, k))
                branch(2, 3)
                for i in range(4):
                    branch(1, i)
                if l == DEPTH - 1:
                    modulation(ADA_LATER - 1, 1)

                def pairs(phase, n, ks, rhs, ready):
                    u, t = plan.unit[l, phase], plan.tile[l, phase]

                    def turn(i, first=False, second=False):
                        for r in range(2):
                            take_slot(t + 2 * i + r, r)
                            done(product(r, u + 2 * i + r, r, ks, rhs, W, ready if first and r == 0 else None))
                            if second and r == 0:
                                modulation_before(ada_number(l, phase, 1), 1)
                            modulation_before(ada_number(l, phase, 2 * i + r), r)
                    if ready and ks == KD:
                        two_products(t, u, ks, rhs, (W, W), ready)
                        modulation_before(ada_number(l, phase, 0), 0)
                        turn(1, second=True)
                        loop(pe, n - 2, lambda i: turn(i + 2))
                    elif ready:
                        turn(0, first=True)
                        loop(pe, n - 1, lambda i: turn(i + 1))
                    else:
                        loop(pe, n, turn)
                pairs("mix", KD // 2, KD, from_h, h_ready)
                normed[0] += KD
                norm(W)
                for p, n in enumerate(PARTS):
                    pairs(("up", p), n, KD, from_h, None if p else h_ready)
                    u0 = PARTS[0] * (p % 2)
                    pairs(("down", p), KD // 2, n, lambda part, k, a, b: U[:, u0 + k, part, a:b],
                          lambda k: pe.wait_ge(s_u, up_base[l, p] + k + 1))
                normed[0] += KD

            t = plan.tile["store"]
            phase_read_out(pe, t)
            for i in range(KD):
                take_slot(t + i, i % 2)
                for tt in range(S // 128):
                    ins = nc.tensor.transpose(G[:, i % 2, 128 * tt:128 * tt + 128], X[:, i, 128 * tt:128 * tt + 128],
                                              ident[:, :])
                done(ins)

        @block.gpsimd
        def _(pool):
            nc.gpsimd.memset(ones[:, :], 1.0).then_inc(s_set, 1)
            nc.gpsimd.memset(eps[:, :], EPS).then_inc(s_set, 1)

            def rest(u, slot, width=1024):
                pool.wait_ge(s_hi, u + 1)
                for c in (slice(0, half(width)), slice(half(width), width)):
                    nc.gpsimd.tensor_tensor(WHL[:, slot, 1, c], raw[:, slot, c], f(WHL[:, slot, 0, c]),
                                            ALU.subtract).then_inc(s_lo, 1)

            def rests(phase, n, next_width=1024):
                u = plan.unit[l, phase] + 2

                def turn(i, width=plan.width[l, phase]):
                    for r in range(2):
                        rest(u + 2 * i + r, r, width)
                loop(pool, n - 1, turn)
                if next_width:
                    turn(n - 1, next_width)

            for r in range(2):
                rest(r, r)
            for l in range(DEPTH):
                W = WIDTH[l]
                pool.wait_ge(s_tile, plan.tile[l, "qkv"] + 1)
                for a, b in ((0, PAD), (PAD + S, PAD + S + GAP), (PAD + S + GAP + LC, T + 2 * GAP)):
                    nc.gpsimd.memset(hpad[:, :, a:b], 0.0).then_inc(s_pad, 1)
                rests("qkv", 3)
                rests("conf", KC)
                for b in (0, "sc", 2, 1):
                    if b == "sc":
                        pool.wait_ge(s_tile, plan.tile[l, "sc"])
                        for a in (0, S + 1, S + 2, T + 3):
                            nc.gpsimd.memset(bx[:, a:a + 1], 0.0).then_inc(s_pad, 1)
                        rests("sc", 6)
                        continue
                    u, t = plan.unit[l, ("branch", b)] + 2, plan.tile[l, ("branch", b)]
                    for i in range(4):
                        for n in range(3):
                            rest(u + 3 * i + n, (i + n) % 2)
                        if b and (b, i) != (1, 3):
                            for n in range(2):
                                read_out(pool, t + 4 * i + 2 + n, n)
                                if b == 1:
                                    pool.wait_ge(s_mg, 16 * l + 2 * i + n + 1)
                                m = merged[:, 2 * i + n, 0:W]
                                nc.gpsimd.tensor_tensor(m, m, ybuf[:, n, 0:W], ALU.add).then_inc(s_mg, 1)
                rests("mix", KD // 2)
                for p, n in enumerate(PARTS):
                    rests(("up", p), n, 128 * n)
                    rests(("down", p), KD // 2, 0 if l == DEPTH - 1 and p == len(PARTS) - 1 else 1024)

        @block.scalar
        def _(act):
            def high(u, slot, width=1024):
                act.wait_ge(s_w[slot], 16 * (u - slot) + 32)
                nc.scalar.activation(WHL[:, slot, 0, 0:width], raw[:, slot, 0:width], ACT.Copy).then_inc(s_hi, 1)

            def tile_and_high(t, u, slot, width=1024):
                act.wait_ge(s_tile, t + 1)
                high(u + 2, slot, width)

            def free(ins, slot):
                ins.then_inc(s_free[slot], 2)

            stats, squares, hh = [0], [0], [0]

            def deviation(n, func, scale):
                k = stats[0]
                act.wait_ge(s_stat, k + 1)
                if k >= 2:
                    act.wait_ge(s_inv, k - 1)
                src = O[:, 0, 16 * (k % 2):16 * (k % 2) + n]
                if func == ACT.Sqrt:
                    ins = nc.scalar.activation(sd[:, k % 2, 0:n], src, func, bias=eps[:, :], scale=scale)
                else:
                    ins = nc.scalar.activation(sd[:, k % 2, 0:n], src, func, scale=scale)
                ins.then_inc(s_sd, 1)
                stats[0] += 1

            def square(i, r, t, width):
                read_out(act, t, r)
                if isinstance(i, int) and i < 3:
                    if i == 0:
                        nc.scalar.activation(SSQ[:, 0:width], X[:, 0, 0:width], ACT.Square).then_inc(s_sq, 1)
                        return
                else:
                    act.wait_ge(s_ssq, squares[0] + i - 2)
                src = X[:, bass.ds(i, 1), 0:width].rearrange("p a n -> p (a n)")
                nc.scalar.activation(SQ[:, r, 0:width], src, ACT.Square).then_inc(s_sq, 1)

            def h_high(shift, segs, rows={}):
                for i in range(KD):
                    if i in rows:
                        row_copy(rows[i])
                    act.wait_ge(s_ht, hh[0] + i + 1)
                    for a, n, v in segs:
                        ins = nc.scalar.activation(H[:, 0, i, a:a + n], HT[:, i % 2, a:a + n], ACT.Identity,
                                                   bias=mods[:, l, shift * KD + i, v:v + 1])
                    ins.then_inc(s_hh, 1)
                hh[0] += KD

            def ada_load(n, slot, layer):
                la, m = ada_tile(n, layer)
                src = A["w_ada"][la].rearrange("(k p) n -> p k n", p=128)[:, :, bass.ds(m * 128, 128)]
                act.dma_start(adaw[:, slot], src).then_inc(s_adw[slot], 16)

            def ada_load_after(n, slot, layer):
                if n is None or isinstance(n, int) and n + 2 >= ADA_LATER:
                    return
                act.wait_ge(s_adv, ADA_STEPS * n + ADA_STEPS)
                ada_load(n + 2, slot, layer)

            def modulation(n, layer):
                act.wait_ge(s_adt, ADA_FIRST // 2 + 1 + n)
                la, m = ada_tile(n, layer)
                dst = mods[:, la, bass.ds(m, 1), :].rearrange("p a v -> p (a v)")
                nc.scalar.activation(dst, O[:, 1, 0:2], ACT.Identity, bias=bada[:, la, bass.ds(m, 1)]).then_inc(s_mt, 1)

            def modulation_before(n, layer):
                if n is None or isinstance(n, int) and n == 0:
                    return
                modulation(n - 1, layer)

            def ada_layers(l, phase, n):
                if n is None:
                    return None, None
                own, fixed = ada_layer(l, phase), isinstance(n, int)
                return (1 if fixed and n + 2 + ADA_FIRST >= MT else own), (0 if fixed and n - 1 + ADA_FIRST < MT else own)

            act.dma_start(xin[:, 0:4, :], A["x"][0].rearrange("(t p) n -> p t n", p=128)).then_inc(s_in, 16)
            act.dma_start(xin[:, 4:6, :], A["ctx"][0].rearrange("(t p) n -> p t n", p=128)).then_inc(s_in, 16)
            w0 = A["w_ada"][0].rearrange("(k p) n -> p k n", p=128)
            act.wait_ge(s_set, 2)
            nc.scalar.activation(root[:, :], eps[:, :], ACT.Sigmoid).then_inc(s_root, 1)
            act.wait_ge(s_par, 16 * (11 + DEPTH))
            for j in range(ADA_FIRST // 2):
                if j == 1:
                    act.wait_ge(s_parc, 1)
                    nc.scalar.activation(sgc[:, :, :], par[:, R_C:R_C + 2 * KD].rearrange("p (v k) -> p v k", v=2),
                                         ACT.Sigmoid).then_inc(s_sgc, 1)
                c = 256 * ada_chunk(j)
                act.dma_start(ada[:, j], w0[:, :, c:c + 256]).then_inc(s_ada[j], 16)
            for n in range(2):
                ada_load(n, n, 0)
            for r in range(2):
                high(r, r)

            def row_copy(j):
                act.wait_ge(s_ar, j + 1)
                c = 256 * ada_chunk(j)
                row = M[0:2, 512 * (j % 2):512 * (j % 2) + 256] if j < 4 else G[0:2, j % 2, 0:256]
                nc.scalar.activation(arow[:, c:c + 256], row, ACT.Copy).then_inc(s_arow, 1)
            act.wait_ge(s_set, 2)
            for i in range(KD):
                square(i, i % 2, i, T)
                if i % 2 and i >= 3:
                    row_copy(i // 2 - 1)
            row_copy(KD // 2 - 1)
            squares[0] += KD - 1
            deviation(T // 128, ACT.Sqrt, 1.0 / D)
            row_copy(KD // 2)
            for l in range(DEPTH):
                W, segs = WIDTH[l], SEGS[l]
                if l:
                    deviation(T // 128, ACT.Sqrt, 1.0 / D)
                    act.wait_ge(s_mt, MT)
                h_high(0, SEGS[0], {} if l else {1: 5, 3: 6, 4: 7})

                def qk_steps(p):
                    n = lagging(p, 1)
                    if n is not None:
                        deviation(2 * (T if n == 0 else W) // 128, ACT.Sqrt, 1.0 / HD)
                    n = lagging(p, 4)
                    if n is not None:
                        w = T if n == 0 else W
                        act.wait_ge(s_qr, 3 * (5 * l + n + 1))
                        for g in range(NKV):
                            own, other = slice(64 * g, 64 * g + 64), slice(64 - 64 * g, 128 - 64 * g)
                            if n == 0:
                                nc.scalar.activation(K_twice[g][other, 0:w], qraw[own, n % 4, 0:w], ACT.Copy)
                            dst = K_twice[g][own, 0:w] if n == 0 else Q[own, g, n - 1, 0:w]
                            ins = nc.scalar.activation(dst, qraw[own, n % 4, 0:w], ACT.Copy)
                        ins.then_inc(s_qh, 1)

                u, t = plan.unit[l, "qkv"], plan.tile[l, "qkv"]
                for i in range(6):
                    tile_and_high(t + i, u + i, i % 2)
                    g = G[:, i % 2]
                    if i == V_AT:
                        free(nc.scalar.activation(vraw[:, :], g[:, 0:T], ACT.Copy), i % 2)
                    else:
                        n = i - (i > V_AT)
                        w = T if n == 0 else W
                        if n == 4:
                            act.wait_ge(s_q, 5 * l + 1)
                        if n:
                            act.wait_ge(s_stat, stats[0] + (n != 2))
                        nc.scalar.activation(qsq[:, 0:w], g[:, 0:w], ACT.Square).then_inc(s_qsq, 1)
                        free(nc.scalar.activation(qraw[:, n % 4, 0:w], g[:, 0:w], ACT.Copy), i % 2)
                    qk_steps(i)
                    if i == V_AT + 2:
                        act.wait_ge(s_vt, l + 1)
                        nc.scalar.activation(V[:, 0].rearrange("p t n -> p (t n)"), M[:, 0:T], ACT.Copy).then_inc(s_vh, 1)

                u, t = plan.unit[l, "conf"], plan.tile[l, "conf"]
                for i in range(2 * KC):
                    tile_and_high(t + i, u + i, i % 2)
                    if i % 2 == 0:
                        if i:
                            read_out(act, t + i - 1, 1)
                        free(nc.scalar.activation(GS[:, 0, 0:W], G[:, 0, 0:W], ACT.Sigmoid), 0)
                    qk_steps(6 + i)

                st_, s0, t = steps(l), step_base[l], plan.tile[l, "att"]

                def probs(i):
                    g, tile, q0, k0, nk, c = st_[i]
                    act.wait_ge(s_nm, s0 + i + 1)
                    if i >= 2:
                        act.wait_ge(s_pt[1], s0 + i - 1)
                    free(nc.scalar.activation(P[:, i % 2, k0:k0 + nk], G[:, i % 2, k0:k0 + nk], ACT.Exp,
                                              bias=nmax[:, i % 4:i % 4 + 1], accum_out=psums[:, c:c + 1]), i % 2)

                def turned(i):
                    g, tile, q0, k0, nk, c = st_[i]
                    j = i // 2
                    if j >= 2:
                        act.wait_ge(s_o, s0 // 2 + j - 1)
                    for half, (a, b) in enumerate(((0, 4), (4, T // 128))):
                        if k0 > 128 * a:
                            continue
                        act.wait_ge(s_pt[half], s0 + i + 1 if half else latent_steps(l, i + 1))
                        nc.scalar.activation(PT[:, j % 2, 0, a:b, 128 * (i % 2):128 * (i % 2) + 128],
                                             M[:, 128 * a:128 * b].rearrange("p (k n) -> p k n", n=128), ACT.Copy)\
                            .then_inc(s_ph[half], 1)

                def outs(j):
                    g, tile, q0, k0, nk, c = st_[2 * j]
                    r = slice(64 * g, 64 * g + 64)
                    act.wait_ge(s_o, s0 // 2 + j + 1)
                    nc.scalar.activation(heads_raw[r, tile, q0:q0 + 256], O[r, j % 2, 0:256], ACT.Copy).then_inc(s_oc, 1)

                probs(0)
                for i in range(len(st_) + 3):
                    if i + 1 < len(st_):
                        probs(i + 1)
                    if i % 2 == 0 and i >= 4:
                        outs((i - 4) // 2)
                    if i < len(st_):
                        turned(i)
                for n in range(KC):
                    act.wait_ge(s_os, KC * l + n + 1)
                    nc.scalar.activation(Q[:, 0, n, 0:W], heads_raw[:, n, 0:W], ACT.Copy).then_inc(s_oh, 1)

                def branch(b, i):
                    u, t = plan.unit[l, ("branch", b)] + 3 * i, plan.tile[l, ("branch", b)] + 4 * i
                    ph = ("branch", b)

                    def ada(q):
                        n = ada_number(l, ph, q)
                        after, before = ada_layers(l, ph, n)
                        if n is not None:
                            ada_load_after(n, n % 2, after)
                        modulation_before(n, before)
                    for n in range(2):
                        tile_and_high(t + n, u + n, (i + n) % 2)
                        if i:
                            read_out(act, t - 2 + n, n)
                        free(nc.scalar.activation(GS[:, n, 0:W], G[:, n, 0:W], ACT.Sigmoid), n)
                        ada(3 * i + n)
                    if (b, i) == (1, 3):
                        merged_high(0, 6)
                    tile_and_high(t + 3, u + 2, i % 2)
                    if (b, i) == (1, 3) and l:
                        ada(3 * i + 2)
                    if (b, i) == (1, 3):
                        merged_high(6, KD)
                    if not ((b, i) == (1, 3) and l):
                        ada(3 * i + 2)

                def merged_high(a, b):
                    for i in range(a, b):
                        act.wait_ge(s_mg, 16 * l + KD + i + 1)
                        nc.scalar.activation(H[:, 0, i, 0:W], merged[:, i, 0:W], ACT.Copy).then_inc(s_mh, 1)
                for i in range(4):
                    branch(0, i)

                u, t = plan.unit[l, "sc"], plan.tile[l, "sc"]
                phase_read_out(act, t)
                for i in range(KC):
                    a = 3 * i
                    tile_and_high(t + a, u + a, a % 2)
                    if i:
                        read_out(act, t + a - 2, a % 2)
                    free(nc.scalar.activation(GS[:, 0, 0:W], G[:, a % 2, 0:W], ACT.Copy), a % 2)
                    tile_and_high(t + a + 1, u + a + 1, (a + 1) % 2)
                    tile_and_high(t + a + 2, u + a + 2, a % 2)
                    read_out(act, t + a + 2, a % 2)
                    nc.scalar.activation(SCO[:, 0, i, 0:W], GS[:, 1, 0:W], ACT.Copy).then_inc(s_sch, 1)
                act.wait_ge(s_scl, KC * (l + 1))

                Wc = CONV_W[l]
                branch(2, 0)
                deviation(W // 128, ACT.Copy, 1.0 / CW)
                for n in range(KC):
                    act.wait_ge(s_lsm, KC * 2 * l + n + 1)
                    if n == 3:
                        act.wait_ge(s_ls, 6 * l + 4)
                    nc.scalar.activation(ln_sum[:, 0:Wc] if n == 0 else ln_sq[:, n % 2, 0:Wc], acc[:, n, 0:Wc],
                                         ACT.Square).then_inc(s_lsq, 1)
                branch(2, 1)
                deviation(W // 128, ACT.Sqrt, 1.0 / CW)
                for n in range(KC):
                    act.wait_ge(s_lsm, KC * (2 * l + 1) + n + 1)
                    if n >= 2:
                        act.wait_ge(s_lv, KC * l + n - 1)
                    nc.scalar.activation(sig[:, n % 2, 0:Wc], acc[:, n, 0:Wc], ACT.Sigmoid,
                                         bias=par[:, R_LB + KC * l + n:R_LB + KC * l + n + 1]).then_inc(s_lsg, 1)
                branch(2, 2)
                act.wait_ge(s_lv, KC * (l + 1))
                for n in range(KC):
                    for a, w, v in segs:
                        ins = nc.scalar.activation(CF[:, 0, n, a:a + w], acc[:, n, ctok(a):ctok(a) + w], ACT.Copy)
                    ins.then_inc(s_lh, 1)
                branch(2, 3)
                for i in range(4):
                    branch(1, i)
                if l == DEPTH - 1:
                    modulation(ADA_LATER - 1, 1)

                def x_tiles(phase, width, with_squares):
                    u, t = plan.unit[l, phase], plan.tile[l, phase]

                    def turn(i, more=True, width_=plan.width[l, phase]):
                        for r in range(2):
                            if more:
                                tile_and_high(t + 2 * i + r, u + 2 * i + r, r, width_)
                            n = ada_number(l, phase, 2 * i + r)
                            after, before = ada_layers(l, phase, n)
                            if with_squares:
                                square(2 * i + r, r, t + 2 * i + r, width)
                            ada_load_after(n, r, after)
                            modulation_before(n, before)
                    turn(0)
                    loop(act, KD // 2 - 2, lambda i: turn(i + 1))
                    turn(KD // 2 - 1, u + KD < plan.units, 1024)
                    if with_squares:
                        squares[0] += KD - 1
                act.wait_ge(s_root, 2 * l + 1)
                nc.scalar.activation(root[:, :], eps[:, :], ACT.Sqrt).then_inc(s_root, 1)
                x_tiles("mix", W, True)
                deviation(W // 128, ACT.Sqrt, 1.0 / D)
                h_high(3, segs)

                for p, n in enumerate(PARTS):
                    u, t = plan.unit[l, ("up", p)], plan.tile[l, ("up", p)]

                    def ada_work(q, slot, p=p):
                        n = ada_number(l, ("up", p), q)
                        after, before = ada_layers(l, ("up", p), n)
                        ada_load_after(n, slot, after)
                        modulation_before(n, before)

                    def up(i, u=u, t=t, p=p, first=False, width=1024):
                        tile_and_high(t + 2 * i, u + 2 * i, 0, width)
                        if not first:
                            act.wait_ge(s_u, up_base[l, p] + i)
                        free(nc.scalar.activation(GS[:, 0, 0:W], G[:, 0, 0:W], ACT.Silu), 0)
                        ada_work(2 * i, 0)
                        tile_and_high(t + 2 * i + 1, u + 2 * i + 1, 1, width)
                        read_out(act, t + 2 * i + 1, 1)
                        dst = U[:, bass.ds(i + PARTS[0] * (p % 2), 1), 0, 0:W].rearrange("p a n -> p (a n)")
                        nc.scalar.activation(dst, GS[:, 0, 0:W], ACT.Copy).then_inc(s_uh, 1)
                        ada_work(2 * i + 1, 1)
                    up(0, first=up_base[l, p] == 0)
                    loop(act, n - 2, lambda i: up(i + 1))
                    up(n - 1, width=plan.width[l, ("down", p)])
                    if p == len(PARTS) - 1 and l < DEPTH - 1:
                        act.wait_ge(s_root, 2 * l + 2)
                        nc.scalar.activation(root[:, :], eps[:, :], ACT.Sqrt).then_inc(s_root, 1)
                    x_tiles(("down", p), W, p == len(PARTS) - 1 and l < DEPTH - 1)

            t = plan.tile["store"]
            for i in range(KD):
                act.wait_ge(s_tile, t + i + 1)
                free(nc.scalar.activation(xout[:, :, 128 * i:128 * i + 128],
                                          G[:, i % 2, 0:S].rearrange("p (t n) -> p t n", n=128), ACT.Copy), i % 2)

        @block.vector
        def _(dve):
            V_ = nc.vector

            def stt(o_, a, s, b, op0, op1):
                return V_.scalar_tensor_tensor(o_, a, s, b, op0, op1)

            def free(ins, slot):
                ins.then_inc(s_free[slot], 2)

            dve.wait_ge(s_part, 1)
            V_.tensor_copy(bada[:, :, :].rearrange("p l m -> p (l m)"), O[:, 0, 0:DEPTH * MT])
            V_.tensor_copy(par[:, :], O[:, 0, 128:128 + PAR_ROWS]).then_inc(s_parc, 1)
            dve.wait_ge(s_part, 2)
            V_.tensor_copy(cw[:, :, :], O[:, 1, 0:128 * DEPTH].rearrange("p (l c) -> p l c", c=128)[:, :, 0:CONV_ROWS])\
                .then_inc(s_parc, 1)
            dve.wait_ge(s_parc, 2)
            for c in (1, 4):
                V_.tensor_scalar(bada[:, :, c * KD:(c + 1) * KD], bada[:, :, c * KD:(c + 1) * KD], 1.0, None, ALU.add)\
                    .then_inc(s_parc, 1)
            for l in range(DEPTH):
                V_.tensor_scalar(qg[:, l, 1:2], par[:, R_QN + l:R_QN + l + 1], HD ** -0.5, None, ALU.mult)
                V_.tensor_copy(qg[:, l, 0:1], par[:, R_KN + l:R_KN + l + 1]).then_inc(s_qg, 1)
            dve.wait_ge(s_sgc, 1)
            V_.tensor_tensor(csil[:, :, :].rearrange("p k v -> p v k"),
                             par[:, R_C:R_C + 2 * KD].rearrange("p (v k) -> p v k", v=2), sgc[:, :, :], ALU.mult)\
                .then_inc(s_csil, 1)

            invs, squares, norms, split = [0], [0], [0], [0]

            def modulation(n, slot):
                if n is None:
                    return
                dve.wait_ge(s_adw[slot], 8 * (n - slot) + 16)
                if not (isinstance(n, int) and n < 2):
                    dve.wait_ge(s_adt, ADA_FIRST // 2 + n - 1)
                for k in range(KD):
                    for v in range(2):
                        o_, c = adp[:, slot, v, :], csil[:, k, v:v + 1]
                        if k == 0:
                            ins = V_.tensor_scalar(o_, adaw[:, slot, k, :], c, None, ALU.mult)
                        else:
                            dve.wait_ge(s_adv, ADA_STEPS * n + 2 * k + v - 1)
                            ins = stt(o_, adaw[:, slot, k, :], c, o_, ALU.mult, ALU.add)
                        ins.then_inc(s_adv, 1)

            def inverse(n, func="reciprocal"):
                k = invs[0]
                dve.wait_ge(s_sd, k + 1)
                if k >= 2:
                    dve.wait_ge(s_spread, k - 1)
                if func == "mean":
                    V_.tensor_copy(rs[:, k % 2, 0:n], sd[:, k % 2, 0:n]).then_inc(s_inv, 1)
                elif func == "heads":
                    V_.reciprocal(rs[:, k % 2, 0:n], sd[:, k % 2, 0:n]).then_inc(s_rc, 1)
                    dve.wait_ge(s_rc, heads_done[0] + 1)
                    dve.wait_ge(s_spread, k)
                    V_.tensor_copy(qspread[:, 0:n // 2].rearrange("p t h d -> p (t h) d"),
                                   rs[:, k % 2, 0:n].unsqueeze(2).to_broadcast([128, n, HD])).then_inc(s_inv, 1)
                    heads_done[0] += 1
                else:
                    V_.reciprocal(rs[:, k % 2, 0:n], sd[:, k % 2, 0:n]).then_inc(s_inv, 1)
                invs[0] += 1
            heads_done = [0]

            def add_square(i, r, width):
                if isinstance(i, int) and i == 0:
                    return
                dve.wait_ge(s_sq, squares[0] + i + 1)
                if not (isinstance(i, int) and i == 1):
                    dve.wait_ge(s_ssq, squares[0] // KD * (KD - 1) + i - 1)
                V_.tensor_tensor(SSQ[:, 0:width], SSQ[:, 0:width], SQ[:, r, 0:width], ALU.add).then_inc(s_ssq, 1)

            def first_modulation(p):
                dve.wait_ge(s_adt, 2 * p + 2)
                dve.wait_ge(s_parc, 4)

                def tiles(ap):
                    return ap.rearrange("p (h m) -> p h m", h=2)[:, :, 2 * p:2 * p + 2]
                for v in range(2):
                    src = O[:, 1, 0:2 * ADA_FIRST].rearrange("p (m v) -> p m v", v=2)[:, :, v]
                    V_.tensor_tensor(tiles(mods[:, 0, 0:ADA_FIRST, v]), tiles(src), tiles(bada[:, 0, 0:ADA_FIRST]), ALU.add)\
                        .then_inc(s_mod, 1)
                dve.wait_ge(s_mod, 2 * p + 2)

            def norm(scale, shift, segs, width, modulated={}):
                dve.wait_ge(s_spread, invs[0])

                def scaled(i):
                    if i in modulated:
                        first_modulation(modulated[i])
                    if i >= 2:
                        dve.wait_ge(s_h, split[0] + i - 1)
                    for a, n, v in segs:
                        ins = stt(HT[:, i % 2, a:a + n], X[:, i, a:a + n], mods[:, l, scale * KD + i, v:v + 1],
                                  M[:, a:a + n], ALU.mult, ALU.mult)
                    ins.then_inc(s_ht, 1)

                def rests(i):
                    dve.wait_ge(s_hh, norms[0] + i + 1)
                    for a, n, v in segs:
                        ins = stt(H[:, 1, i, a:a + n], HT[:, i % 2, a:a + n], mods[:, l, shift * KD + i, v:v + 1],
                                  f(H[:, 0, i, a:a + n]), ALU.add, ALU.subtract)
                    ins.then_inc(s_h, 1)
                scaled(0)
                for i in range(KD):
                    if i + 1 < KD:
                        scaled(i + 1)
                    rests(i)
                norms[0] += KD
                split[0] += KD

            def x_tiles(phase, gate, segs, with_squares):
                t = plan.tile[l, phase]
                phase_read_out(dve, t)

                def turn(i):
                    for r in range(2):
                        modulation(ada_number(l, phase, 2 * i + r), r)
                        dve.wait_ge(s_tile, t + 2 * i + r + 1)
                        for a, n, v in segs:
                            x = X[:, bass.ds(2 * i + r, 1), a:a + n].rearrange("p a n -> p (a n)")
                            m = mods[:, l, bass.ds(2 * i + r + gate * KD, 1), v:v + 1].rearrange("p a n -> p (a n)")
                            ins = stt(x, G[:, r, a:a + n], m, x, ALU.mult, ALU.add)
                        free(ins, r)
                        if with_squares:
                            add_square(2 * i + r, r, WIDTH[l])
                turn(0)
                loop(dve, KD // 2 - 1, lambda i: turn(i + 1))
                if with_squares:
                    squares[0] += KD

            for i in range(KD + 1):
                if i < KD:
                    dve.wait_ge(s_tile, i + 1)
                    free(V_.tensor_copy(X[:, i, :], G[:, i % 2, 0:T]), i % 2)
                if i:
                    add_square(i - 1, (i - 1) % 2, T)
            squares[0] += KD

            for l in range(DEPTH):
                W, segs, Wc = WIDTH[l], SEGS[l], CONV_W[l]
                if l == 0:
                    first_modulation(0)
                    inverse(T // 128)
                    first_modulation(1)
                    norm(1, 0, SEGS[0], T, {4: 2, 6: 3})
                else:
                    inverse(T // 128)
                    dve.wait_ge(s_mt, MT)
                    norm(1, 0, SEGS[0], T)

                dve.wait_ge(s_rope, 32 * (l + 1))
                dve.wait_ge(s_qg, DEPTH)

                def qk_steps(p):
                    n = lagging(p, 4)
                    if n is not None:
                        w = T if n == 0 else W
                        dve.wait_ge(s_qh, 5 * l + n + 1)
                        for g in range(NKV):
                            own, other = slice(64 * g, 64 * g + 64), slice(64 - 64 * g, 128 - 64 * g)
                            hi = K_twice[g][own, 0:w] if n == 0 else Q[own, g, n - 1, 0:w]
                            lo = K_rest[own, 0:w] if n == 0 else Q[other, g, n - 1, 0:w]
                            ins = V_.tensor_tensor(lo, qraw[own, n % 4, 0:w], f(hi), ALU.subtract)
                        ins.then_inc(s_q, 1)
                    n = lagging(p, 1)
                    if n is not None:
                        inverse(2 * (T if n == 0 else W) // 128, "heads")
                    n = lagging(p, 2)
                    if n is not None:
                        w = T if n == 0 else W
                        dve.wait_ge(s_spread, invs[0] - (lagging(p, 1) is not None))
                        tq = plan.tile[l, "qkv"] + product_of(n)
                        read_out(dve, tq, tq % 2)
                        stt(qraw[:, n % 4, 0:w], qraw[:, n % 4, 0:w], qg[:, l, (0 if n == 0 else 1):(1 if n == 0 else 2)],
                            M[:, 0:w], ALU.mult, ALU.mult).then_inc(s_qn, 1)
                    n = lagging(p, 3)
                    if n is not None:
                        q, c = qraw[:, n % 4, 0:S], 3 * (5 * l + n)
                        dve.wait_ge(s_rot, 5 * l + n + 1)
                        if c:
                            dve.wait_ge(s_qr, c)
                        V_.tensor_tensor(qrot[:, :], O[:, 1, 0:S], rope[:, 1, :], ALU.mult).then_inc(s_qr, 1)
                        V_.tensor_tensor(q, q, rope[:, 0, :], ALU.mult).then_inc(s_qr, 1)
                        dve.wait_ge(s_qr, c + 2)
                        V_.tensor_tensor(q, q, qrot[:, :], ALU.add).then_inc(s_qr, 1)

                for i in range(6):
                    qk_steps(i)
                    if i == V_AT + 2:
                        dve.wait_ge(s_vh, l + 1)
                        V_.tensor_tensor(V[:, 1].rearrange("p t n -> p (t n)"), M[:, 0:T],
                                         f(V[:, 0].rearrange("p t n -> p (t n)")), ALU.subtract).then_inc(s_v, 1)

                t = plan.tile[l, "conf"]
                dve.wait_ge(s_pad, 7 * l + 3)
                for i in range(2 * KC):
                    if i % 2:
                        dve.wait_ge(s_tile, t + i + 1)
                        read_out(dve, t + i - 1, 0)
                        for a, n, v in segs:
                            ins = V_.tensor_tensor(hpad[:, i // 2, PAD + ctok(a):PAD + ctok(a) + n], G[:, 1, a:a + n],
                                                   GS[:, 0, a:a + n], ALU.mult)
                        free(ins, 1)
                    qk_steps(6 + i)

                st_, s0, t = steps(l), step_base[l], plan.tile[l, "att"]

                def maxima(i):
                    g, tile, q0, k0, nk, c = st_[i]
                    dve.wait_ge(s_tile, t + i + 1)
                    V_.tensor_reduce(nmax[:, i % 4:i % 4 + 1], G[:, i % 2, k0:k0 + nk], AX.X, ALU.max, negate=True)\
                        .then_inc(s_nm, 1)

                def turned(i):
                    g, tile, q0, k0, nk, col = st_[i]
                    j, c = i // 2, 128 * (i % 2)
                    for half, (a, b) in enumerate(((0, 4), (4, T // 128))):
                        if k0 > 128 * a:
                            continue
                        dve.wait_ge(s_ph[half], s0 + i + 1 if half else latent_steps(l, i + 1))
                        V_.tensor_tensor(PT[:, j % 2, 1, a:b, c:c + 128],
                                         M[:, 128 * a:128 * b].rearrange("p (k n) -> p k n", n=128),
                                         f(PT[:, j % 2, 0, a:b, c:c + 128]), ALU.subtract).then_inc(s_pl[half], 1)

                maxima(0)
                maxima(1)
                for i in range(len(st_)):
                    if i + 2 < len(st_):
                        maxima(i + 2)
                    turned(i)

                nsum = len(st_)
                phase_read_out(dve, t + nsum)
                V_.reciprocal(pinv[:, 0:nsum], psums[:, 0:nsum]).then_inc(s_pr, 1)
                dve.wait_ge(s_pr, l + 1)

                def widen(n):
                    if KC * l + n >= 2:
                        dve.wait_ge(s_ps, KC * l + n - 1)
                    for b in batches(l):
                        if b[0] == n:
                            a, w = NKV * b[1] // 128, NKV * b[2] // 128
                            ins = V_.tensor_copy(pspread[:, n % 2, a:a + w],
                                                 pinv[:, b[5]:b[5] + w].unsqueeze(2).to_broadcast([128, w, HD]))
                    ins.then_inc(s_pi, 1)

                def heads_rest(n):
                    dve.wait_ge(s_oh, KC * l + n + 1)
                    V_.tensor_tensor(Q[:, 1, n, 0:W], heads_raw[:, n, 0:W], f(Q[:, 0, n, 0:W]), ALU.subtract).then_inc(s_ol, 1)
                widen(0)
                widen(1)
                dve.wait_ge(s_oc, (s0 + len(st_)) // 2)
                for n in range(KC):
                    dve.wait_ge(s_ps, KC * l + n + 1)
                    V_.tensor_tensor(heads_raw[:, n, 0:W], heads_raw[:, n, 0:W], M[:, 0:W], ALU.mult).then_inc(s_os, 1)
                    if n + 2 < KC:
                        widen(n + 2)
                    if n:
                        heads_rest(n - 1)
                heads_rest(KC - 1)

                def taps(j0, n):
                    def tap(i):
                        for k in range(KC):
                            step = KC * TAPS * l + KC * j0 + k + KC * i
                            dve.wait_ge(s_tap, step - KC + 1)
                            w = cw[:, l, bass.ds(i * KC + KC * j0 + k, 1)]
                            stt(acc[:, k, 0:Wc], hpad[:, k, bass.ds(i + j0, Wc)], w, acc[:, k, 0:Wc],
                                ALU.mult, ALU.add).then_inc(s_tap, 1)
                    loop(dve, n, tap)

                for k in range(KC):
                    V_.tensor_scalar(acc[:, k, 0:Wc], hpad[:, k, 0:Wc], cw[:, l, k:k + 1],
                                     par[:, R_CB + KC * l + k:R_CB + KC * l + k + 1], ALU.mult, ALU.add).then_inc(s_tap, 1)

                def branch(b, i):
                    t = plan.tile[l, ("branch", b)] + 4 * i

                    def ada(q):
                        n = ada_number(l, ("branch", b), q)
                        if n is not None:
                            modulation(n, n % 2)
                    last = (b, i) == (1, 3)
                    ada(3 * i)
                    ada(3 * i + 1)
                    if l:
                        ada(3 * i + 2)
                    if last:
                        merged_rest(0, 4)
                    for n in range(2):
                        dve.wait_ge(s_tile, t + 2 + n + 1)
                        read_out(dve, t + n, n)
                        if b == 0:
                            dst = merged[:, 2 * i + n, 0:W]
                        else:
                            dst = ybuf[:, n, 0:W]
                            done = 16 * l + KD * (b == 1) + 2 * (i - 1) + n + 1
                            if i or b == 1:
                                dve.wait_ge(s_mg, done)
                        free(V_.tensor_tensor(dst, G[:, n, 0:W], GS[:, n, 0:W], ALU.mult), n)
                        if n == 0 and last:
                            merged_rest(4, 6)
                        if n == 0 and not last and l == 0:
                            ada(3 * i + 2)
                    if last:
                        for n in range(2):
                            read_out(dve, t + 2 + n, n)
                            dve.wait_ge(s_mg, 16 * l + KD + 2 * i + n)
                            m = merged[:, 2 * i + n, 0:W]
                            V_.tensor_tensor(m, m, ybuf[:, n, 0:W], ALU.add).then_inc(s_mg, 1)
                        merged_rest(6, KD)
                        if l == 0:
                            ada(3 * i + 2)

                def merged_rest(a, b):
                    for i in range(a, b):
                        dve.wait_ge(s_mh, KD * l + i + 1)
                        V_.tensor_tensor(H[:, 1, i, 0:W], merged[:, i, 0:W], f(H[:, 0, i, 0:W]), ALU.subtract).then_inc(s_h, 1)
                j0 = 1
                for i, n_taps in enumerate((2, 4, 4, 4)):
                    taps(j0, n_taps)
                    j0 += n_taps
                    branch(0, i)
                taps(j0, 2)

                t = plan.tile[l, "sc"]
                phase_read_out(dve, t)
                dve.wait_ge(s_pad, 7 * (l + 1))
                Ws = W + 2 if l == 0 else W
                j0 = 17
                for i in range(KC):
                    a, n_taps = 3 * i, 4 - i % 2
                    taps(j0, n_taps)
                    j0 += n_taps
                    dve.wait_ge(s_tile, t + a + 2)
                    read_out(dve, t + a, a % 2)
                    for c, n, v in segs:
                        o_ = 1 + c + 2 * v
                        ins = V_.tensor_tensor(bx[:, o_:o_ + n], G[:, (a + 1) % 2, c:c + n], GS[:, 0, c:c + n], ALU.mult)
                    free(ins, (a + 1) % 2)
                    read_out(dve, t + a + 1, (a + 1) % 2)
                    c0 = 3 * (KC * l + i)
                    for j in range(SC_TAPS):
                        w = par[:, R_SC + (SC_TAPS * l + j) * KC + i:R_SC + (SC_TAPS * l + j) * KC + i + 1]
                        if j == 0:
                            ins = V_.tensor_scalar(sc_sum[:, 0:Ws], bx[:, 0:Ws], w, None, ALU.mult)
                        else:
                            dve.wait_ge(s_sct, c0 + j)
                            ins = stt(sc_sum[:, 0:Ws], bx[:, j:j + Ws], w, sc_sum[:, 0:Ws], ALU.mult, ALU.add)
                        ins.then_inc(s_sct, 1)
                    dve.wait_ge(s_sct, c0 + 3)
                    dve.wait_ge(s_tile, t + a + 3)
                    if i:
                        dve.wait_ge(s_scl, KC * l + i)
                    for c, n, v in segs:
                        ins = V_.tensor_tensor(GS[:, 1, c:c + n], G[:, a % 2, c:c + n], sc_sum[:, c + 2 * v:c + 2 * v + n],
                                               ALU.mult)
                    free(ins, a % 2)
                    dve.wait_ge(s_sch, KC * l + i + 1)
                    V_.tensor_tensor(SCO[:, 1, i, 0:W], GS[:, 1, 0:W], f(SCO[:, 0, i, 0:W]), ALU.subtract).then_inc(s_scl, 1)
                assert j0 == TAPS

                def ln_add(out_, a, b):
                    V_.tensor_tensor(out_, a, b, ALU.add).then_inc(s_ls, 1)
                dve.wait_ge(s_tap, KC * TAPS * (l + 1))
                for k in range(1, KC):
                    if k > 1:
                        dve.wait_ge(s_ls, 6 * l + k - 1)
                    ln_add(ln_sum[:, 0:Wc], acc[:, 0, 0:Wc] if k == 1 else ln_sum[:, 0:Wc], acc[:, k, 0:Wc])
                branch(2, 0)
                inverse(W // 128, "mean")
                dve.wait_ge(s_spread, invs[0])
                for k in range(KC):
                    for a, n, v in segs:
                        c = ctok(a)
                        ins = V_.tensor_tensor(acc[:, k, c:c + n], acc[:, k, c:c + n], M[:, a:a + n], ALU.subtract)
                    ins.then_inc(s_lsm, 1)
                for k in range(1, KC):
                    dve.wait_ge(s_lsq, KC * l + k + 1)
                    if k > 1:
                        dve.wait_ge(s_ls, 6 * l + 3 + k - 1)
                    ln_add(ln_sum[:, 0:Wc], ln_sum[:, 0:Wc], ln_sq[:, k % 2, 0:Wc])
                branch(2, 1)
                inverse(W // 128)
                dve.wait_ge(s_spread, invs[0])
                dve.wait_ge(s_lsm, KC * (2 * l + 1))
                for k in range(KC):
                    for a, n, v in segs:
                        c = ctok(a)
                        ins = stt(acc[:, k, c:c + n], acc[:, k, c:c + n], par[:, R_LG + KC * l + k:R_LG + KC * l + k + 1],
                                  M[:, a:a + n], ALU.mult, ALU.mult)
                    ins.then_inc(s_lsm, 1)
                for k in range(KC):
                    dve.wait_ge(s_lsg, KC * l + k + 1)
                    stt(acc[:, k, 0:Wc], acc[:, k, 0:Wc], par[:, R_LB + KC * l + k:R_LB + KC * l + k + 1], sig[:, k % 2, 0:Wc],
                        ALU.add, ALU.mult).then_inc(s_lv, 1)
                branch(2, 2)
                for k in range(KC):
                    dve.wait_ge(s_lh, KC * l + k + 1)
                    for a, n, v in segs:
                        c = ctok(a)
                        ins = V_.tensor_tensor(CF[:, 1, k, a:a + n], acc[:, k, c:c + n], f(CF[:, 0, k, a:a + n]), ALU.subtract)
                    ins.then_inc(s_ll, 1)
                branch(2, 3)
                for i in range(4):
                    branch(1, i)

                split[0] += KD
                dve.wait_ge(s_mt, KD if l == 0 else ADA_LATER)
                x_tiles("mix", 2, segs, True)
                if l == 0:
                    dve.wait_ge(s_mt, 3 * KD)
                inverse(W // 128)
                norm(4, 3, segs, W)

                for p, n in enumerate(PARTS):
                    t = plan.tile[l, ("up", p)]

                    def up(i, t=t, p=p):
                        modulation(ada_number(l, ("up", p), 2 * i), 0)
                        modulation(ada_number(l, ("up", p), 2 * i + 1), 1)
                        dve.wait_ge(s_tile, t + 2 * i + 2)
                        read_out(dve, t + 2 * i, 0)
                        free(V_.tensor_tensor(GS[:, 0, 0:W], G[:, 1, 0:W], GS[:, 0, 0:W], ALU.mult), 1)
                        dve.wait_ge(s_uh, up_base[l, p] + i + 1)
                        c = bass.ds(i + PARTS[0] * (p % 2), 1)
                        hi, lo = [U[:, c, part, 0:W].rearrange("p a n -> p (a n)") for part in range(2)]
                        V_.tensor_tensor(lo, GS[:, 0, 0:W], f(hi), ALU.subtract).then_inc(s_u, 1)
                    loop(dve, n, up)
                    if l == 0 and p == 0:
                        dve.wait_ge(s_mt, 4 * KD)
                    x_tiles(("down", p), 5, segs, p == len(PARTS) - 1 and l < DEPTH - 1)


_INS = ['x', 'c', 'ctx', 'c_ctx', 'w_ada', 'b_ada', 'w_in', 'q_norm', 'k_norm', 'w_attn_o', 'conf_dw_w', 'conf_dw_b',
        'conf_ln_g', 'conf_ln_b', 'w_conf_out', 'sc_dw_w', 'w_sc_out', 'w_mix_out', 'w_ffn_in', 'w_ffn_out']


def _constants():
    f32 = np.float32
    freqs = (ROPE_THETA ** (-np.arange(0, HD // 2, 2, dtype=f32) / f32(HD // 2))).astype(f32)
    tok = np.arange(S)
    angles = np.concatenate([np.tile((tok // GRID_W).astype(f32)[:, None] * freqs, 2),
                             np.tile((tok % GRID_W).astype(f32)[:, None] * freqs, 2)], axis=1)
    ang = np.tile(angles, 2).T
    swap = np.zeros((128, 128), f32)
    for m in range(128):
        if m % 32 < 16:
            swap[m + 16, m] = -1
        else:
            swap[m - 16, m] = 1
    heads = np.zeros((128, 2), f32)
    heads[:64, 0] = heads[64:, 1] = 1
    return {"ident": np.eye(128, dtype=f32), "swap": swap, "heads": heads,
            "rope": np.ascontiguousarray(np.stack([np.cos(ang), np.sin(ang)]).astype(f32))}


def kernel(**inputs):
    import concourse.bacc as _bacc
    from concourse.bass_utils import run_bass_kernel_spmd as _run

    nc = _bacc.Bacc("TRN2", target_bir_lowering=False, num_devices=1)
    arrays, aps = {}, {}
    for name, a in [(n, np.ascontiguousarray(inputs[n])) for n in _INS] + list(_constants().items()):
        arrays[f"in_{name}"] = a
        aps[name] = nc.dram_tensor(f"in_{name}", a.shape, mybir.dt.from_np(a.dtype), kind="ExternalInput").ap()
    out = nc.dram_tensor("out", (1, S, D), F32, kind="ExternalOutput").ap()
    build(nc, aps, out)
    return _run(nc, [arrays], core_ids=[0]).results[0]["out"]
```
